# Optimizing a Trainium2 kernel written in Bass

```python
import jax, jax.numpy as jnp
from jax import lax
import numpy as np
import jax
import jax.numpy as jnp

D_MODEL = 1024
BATCH = 1
SEQ = 256
DEPTH = 2

GRID_W = 64
CTX_LEN = 256
NORM_EPS = 1e-6
ROPE_BASE = 10000.0
Q_BLOCK = 128

MLA_HEADS = 6
MLA_Q_RANK = 256
MLA_KV_RANK = 128
MLA_NOPE = 64
MLA_ROPE = 32
MLA_V = 64
MLA_WIDTH = MLA_HEADS * MLA_V
MLA_SCALE = (MLA_NOPE + MLA_ROPE) ** -0.5

SWA_HEADS = 6
SWA_KV_HEADS = 2
SWA_REP = SWA_HEADS // SWA_KV_HEADS
SWA_HEAD_DIM = 64
SWA_WINDOW = 128
SWA_WIDTH = SWA_HEADS * SWA_HEAD_DIM
SWA_SCALE = SWA_HEAD_DIM ** -0.5

CONV_CH = 256
CONV_K = 3

MIX_WIDTH = MLA_WIDTH + SWA_WIDTH + CONV_CH
IN_SPLITS = (MLA_Q_RANK, MLA_KV_RANK, MLA_ROPE, SWA_WIDTH, SWA_KV_HEADS * SWA_HEAD_DIM, SWA_KV_HEADS * SWA_HEAD_DIM, CONV_CH, CONV_CH, CONV_CH)
IN_WIDTH = sum(IN_SPLITS)

N_EXPERTS = 16
EXPERT_FF = 512
EC_CAPACITY_FACTOR = 2
N_MOD = 6


def rmsnorm(x, g):
    xf = x.astype(jnp.float32)
    y = xf * lax.rsqrt(jnp.mean(xf * xf, axis=-1, keepdims=True) + NORM_EPS)
    return (y * g.astype(jnp.float32)).astype(x.dtype)

def axial_rope(n_tokens, rot_dim, dtype):
    rows = n_tokens // GRID_W
    row = jnp.repeat(jnp.arange(rows, dtype=jnp.float32), GRID_W)
    col = jnp.tile(jnp.arange(GRID_W, dtype=jnp.float32), rows)
    n_freq = rot_dim // 4
    inv = ROPE_BASE ** (-jnp.arange(n_freq, dtype=jnp.float32) / n_freq)
    ang = jnp.concatenate([row[:, None] * inv, col[:, None] * inv], axis=-1)
    return jnp.cos(ang).astype(dtype), jnp.sin(ang).astype(dtype)

def apply_rope(x, cos, sin):
    shape = (cos.shape[0],) + (1,) * (x.ndim - 3) + (cos.shape[1],)
    cos = cos.reshape(shape)
    sin = sin.reshape(shape)
    x1, x2 = jnp.split(x, 2, axis=-1)
    return jnp.concatenate([x1 * cos - x2 * sin, x2 * cos + x1 * sin], axis=-1)

def split_columns(p):
    offs = [int(o) for o in np.cumsum(IN_SPLITS)[:-1]]
    return jnp.split(p, offs, axis=-1)

def to_blocks(t):
    b, n = t.shape[0], t.shape[1]
    return jnp.moveaxis(t.reshape((b, n // Q_BLOCK, Q_BLOCK) + t.shape[2:]), 1, 0)

def from_blocks(o):
    nb, b, qb = o.shape[0], o.shape[1], o.shape[2]
    return jnp.moveaxis(o, 0, 1).reshape(b, nb * qb, -1)

def mla_q(p_q, q_norm_g, w_uq):
    b, t = p_q.shape[0], p_q.shape[1]
    q = (rmsnorm(p_q, q_norm_g) @ w_uq).reshape(b, t, MLA_HEADS, MLA_NOPE + MLA_ROPE)
    return q[..., :MLA_NOPE], q[..., MLA_NOPE:]

def mla_kv(p_kv, kv_norm_g, w_ukv):
    b, t = p_kv.shape[0], p_kv.shape[1]
    kv = (rmsnorm(p_kv, kv_norm_g) @ w_ukv).reshape(b, t, MLA_HEADS, MLA_NOPE + MLA_V)
    return kv[..., :MLA_NOPE], kv[..., MLA_NOPE:]

def mla_block(qn, qr, kn, kr, v):
    s = (jnp.einsum('bqhd,bkhd->bhqk', qn, kn) + jnp.einsum('bqhr,bkr->bhqk', qr, kr)).astype(jnp.float32) * MLA_SCALE
    p = jax.nn.softmax(s, axis=-1).astype(v.dtype)
    return jnp.einsum('bhqk,bkhd->bqhd', p, v)

def mla_latent(qn, qr, kn, kr, v):
    out = lax.map(lambda a: mla_block(a[0], a[1], kn, kr, v), (to_blocks(qn), to_blocks(qr)))
    return from_blocks(out)

def sink_softmax(scores, sink):
    s_sink = jnp.broadcast_to(sink.astype(jnp.float32)[None, :, :, None, None], scores.shape[:-1] + (1,))
    p = jax.nn.softmax(jnp.concatenate([scores, s_sink], axis=-1), axis=-1)
    return p[..., :-1]

def swa_latent(q, k, v, k_ctx, v_ctx, sink):
    s_len = q.shape[1]
    n_ctx = k_ctx.shape[1]
    nb = s_len // Q_BLOCK
    band = Q_BLOCK + 2 * SWA_WINDOW
    pad = ((0, 0), (SWA_WINDOW, SWA_WINDOW), (0, 0), (0, 0))
    kp = jnp.pad(k, pad)
    vp = jnp.pad(v, pad)
    q_off = jnp.arange(Q_BLOCK)
    k_off = jnp.arange(band)

    def block(args):
        i, q_b = args
        start = i * Q_BLOCK
        k_b = lax.dynamic_slice_in_dim(kp, start, band, axis=1)
        v_b = lax.dynamic_slice_in_dim(vp, start, band, axis=1)
        q_pos = start + q_off
        k_pos = start - SWA_WINDOW + k_off
        valid = (jnp.abs(q_pos[:, None] - k_pos[None, :]) <= SWA_WINDOW) & ((k_pos >= 0) & (k_pos < s_len))[None, :]
        s_loc = jnp.einsum('bqgrd,bkgd->bgrqk', q_b, k_b).astype(jnp.float32) * SWA_SCALE
        s_loc = jnp.where(valid, s_loc, -jnp.inf)
        s_ctx = jnp.einsum('bqgrd,bcgd->bgrqc', q_b, k_ctx).astype(jnp.float32) * SWA_SCALE
        p = sink_softmax(jnp.concatenate([s_ctx, s_loc], axis=-1), sink).astype(v.dtype)
        return (jnp.einsum('bgrqc,bcgd->bqgrd', p[..., :n_ctx], v_ctx)
                + jnp.einsum('bgrqk,bkgd->bqgrd', p[..., n_ctx:], v_b))

    out = lax.map(block, (jnp.arange(nb), to_blocks(q)))
    return from_blocks(out)

def swa_context(q, k, v, sink):
    s = jnp.einsum('bqgrd,bcgd->bgrqc', q, k).astype(jnp.float32) * SWA_SCALE
    p = sink_softmax(s, sink).astype(v.dtype)
    o = jnp.einsum('bgrqc,bcgd->bqgrd', p, v)
    return o.reshape(o.shape[0], o.shape[1], SWA_WIDTH)

def short_conv(b_gate, c_gate, u, w):
    z = c_gate * u
    y = lax.conv_general_dilated(z, w[:, None, :].astype(z.dtype), window_strides=(1,),
                                 padding=((CONV_K // 2, CONV_K // 2),),
                                 dimension_numbers=('NWC', 'WIO', 'NWC'),
                                 feature_group_count=CONV_CH)
    return b_gate * y

def ec_ffn(h, router_w, w_gate, w_up, w_down):
    n_tok, d = h.shape[1], h.shape[2]
    cap = EC_CAPACITY_FACTOR * n_tok // N_EXPERTS
    aff = jax.nn.softmax((h @ router_w).astype(jnp.float32), axis=-1)
    top_aff, idx = lax.top_k(jnp.swapaxes(aff, 1, 2), cap)
    xg = jax.vmap(lambda hb, ib: hb[ib])(h, idx)
    hid = jax.nn.silu(jnp.einsum('becd,edf->becf', xg, w_gate)) * jnp.einsum('becd,edf->becf', xg, w_up)
    y = jnp.einsum('becf,efd->becd', hid, w_down) * top_aff[..., None].astype(h.dtype)
    return jax.vmap(lambda yb, ib: jnp.zeros((n_tok, d), yb.dtype).at[ib.reshape(-1)].add(yb.reshape(-1, d)))(y, idx)

def hybrid_layer(xl, xc, c, c_ctx, ada_w, ada_b, norm1_g, w_in, q_norm_g, w_uq, kv_norm_g, w_ukv,
                 sink, conv_w, w_o, norm2_g, router_w, w_gate, w_up, w_down, rope_mla, rope_swa, update_ctx):
    b, s_len = xl.shape[0], xl.shape[1]
    n_ctx = xc.shape[1]
    sh1, sc1, g1, sh2, sc2, g2 = jnp.split((jax.nn.silu(c) @ ada_w + ada_b)[:, None, :], N_MOD, axis=-1)
    csh1, csc1, cg1, csh2, csc2, cg2 = jnp.split(jax.nn.silu(c_ctx) @ ada_w + ada_b, N_MOD, axis=-1)

    hl = rmsnorm(xl, norm1_g) * (1 + sc1) + sh1
    hc = rmsnorm(xc, norm1_g) * (1 + csc1) + csh1
    l_cq, l_ckv, l_kr, l_q, l_k, l_v, l_b, l_c, l_u = split_columns(hl @ w_in)
    c_cq, c_ckv, c_kr, c_q, c_k, c_v, c_b, c_c, c_u = split_columns(hc @ w_in)

    qn_l, qr_l = mla_q(l_cq, q_norm_g, w_uq)
    qr_l = apply_rope(qr_l, *rope_mla)
    kn_l, va_l = mla_kv(l_ckv, kv_norm_g, w_ukv)
    kr_l = apply_rope(l_kr, *rope_mla)
    kn_c, va_c = mla_kv(c_ckv, kv_norm_g, w_ukv)
    a_l = mla_latent(qn_l, qr_l, jnp.concatenate([kn_c, kn_l], axis=1),
                     jnp.concatenate([c_kr, kr_l], axis=1), jnp.concatenate([va_c, va_l], axis=1))

    sink_gr = sink.reshape(SWA_KV_HEADS, SWA_REP)
    q_l = apply_rope(l_q.reshape(b, s_len, SWA_KV_HEADS, SWA_REP, SWA_HEAD_DIM), *rope_swa)
    k_l = apply_rope(l_k.reshape(b, s_len, SWA_KV_HEADS, SWA_HEAD_DIM), *rope_swa)
    v_l = l_v.reshape(b, s_len, SWA_KV_HEADS, SWA_HEAD_DIM)
    k_c = c_k.reshape(b, n_ctx, SWA_KV_HEADS, SWA_HEAD_DIM)
    v_c = c_v.reshape(b, n_ctx, SWA_KV_HEADS, SWA_HEAD_DIM)
    b_l = swa_latent(q_l, k_l, v_l, k_c, v_c, sink_gr)

    cv_l = short_conv(l_b, l_c, l_u, conv_w)

    xl = xl + g1 * (jnp.concatenate([a_l, b_l, cv_l], axis=-1) @ w_o)
    xl = xl + g2 * ec_ffn(rmsnorm(xl, norm2_g) * (1 + sc2) + sh2, router_w, w_gate, w_up, w_down)

    if update_ctx:
        qn_c, qr_c = mla_q(c_cq, q_norm_g, w_uq)
        a_c = mla_block(qn_c, qr_c, kn_c, c_kr, va_c).reshape(b, n_ctx, MLA_WIDTH)
        b_c = swa_context(c_q.reshape(b, n_ctx, SWA_KV_HEADS, SWA_REP, SWA_HEAD_DIM), k_c, v_c, sink_gr)
        cv_c = short_conv(c_b, c_c, c_u, conv_w)
        xc = xc + cg1 * (jnp.concatenate([a_c, b_c, cv_c], axis=-1) @ w_o)
        xc = xc + cg2 * ec_ffn(rmsnorm(xc, norm2_g) * (1 + csc2) + csh2, router_w, w_gate, w_up, w_down)
    return xl, xc

def first_inputs(seed: int = 0) -> dict:
    key = jax.random.key(seed)
    ks = jax.random.split(key, 21)
    f32 = jnp.float32
    D = D_MODEL

    def nrm(k, shape, scale):
        return jax.random.normal(k, shape, f32) * scale

    def gain(k, shape):
        return 1.0 + 0.02 * jax.random.normal(k, shape, f32)

    return {
        'x': nrm(ks[0], (BATCH, SEQ, D), 1.0),
        'c': nrm(ks[1], (BATCH, D), 1.0),
        'ctx': nrm(ks[2], (BATCH, CTX_LEN, D), 1.0),
        'c_ctx': nrm(ks[3], (D,), 1.0),
        'ada_w': nrm(ks[4], (DEPTH, D, N_MOD * D), 0.5 * D ** -0.5),
        'ada_b': nrm(ks[5], (DEPTH, N_MOD * D), 0.02),
        'norm1_g': gain(ks[6], (DEPTH, D)),
        'w_in': nrm(ks[7], (DEPTH, D, IN_WIDTH), D ** -0.5),
        'mla_q_norm_g': gain(ks[8], (DEPTH, MLA_Q_RANK)),
        'mla_w_uq': nrm(ks[9], (DEPTH, MLA_Q_RANK, MLA_HEADS * (MLA_NOPE + MLA_ROPE)), MLA_Q_RANK ** -0.5),
        'mla_kv_norm_g': gain(ks[10], (DEPTH, MLA_KV_RANK)),
        'mla_w_ukv': nrm(ks[11], (DEPTH, MLA_KV_RANK, MLA_HEADS * (MLA_NOPE + MLA_V)), MLA_KV_RANK ** -0.5),
        'swa_sink': nrm(ks[12], (DEPTH, SWA_HEADS), 0.5),
        'conv_w': nrm(ks[13], (DEPTH, CONV_K, CONV_CH), CONV_K ** -0.5),
        'w_o': nrm(ks[14], (DEPTH, MIX_WIDTH, D), MIX_WIDTH ** -0.5),
        'norm2_g': gain(ks[15], (DEPTH, D)),
        'router_w': nrm(ks[16], (DEPTH, D, N_EXPERTS), D ** -0.5),
        'exp_w_gate': nrm(ks[17], (DEPTH, N_EXPERTS, D, EXPERT_FF), D ** -0.5),
        'exp_w_up': nrm(ks[18], (DEPTH, N_EXPERTS, D, EXPERT_FF), D ** -0.5),
        'exp_w_down': nrm(ks[19], (DEPTH, N_EXPERTS, EXPERT_FF, D), EXPERT_FF ** -0.5),
        'final_norm_g': gain(ks[20], (D,)),
    }

def first_block(x, c, ctx, c_ctx, ada_w, ada_b, norm1_g, w_in, mla_q_norm_g, mla_w_uq, mla_kv_norm_g,
              mla_w_ukv, swa_sink, conv_w, w_o, norm2_g, router_w, exp_w_gate, exp_w_up, exp_w_down,
              final_norm_g):
    n_lat = x.shape[1]
    rope_mla = axial_rope(n_lat, MLA_ROPE, x.dtype)
    rope_swa = axial_rope(n_lat, SWA_HEAD_DIM, x.dtype)
    xl, xc = x, ctx
    for li in range(DEPTH):
        xl, xc = hybrid_layer(xl, xc, c, c_ctx, ada_w[li], ada_b[li], norm1_g[li], w_in[li],
                              mla_q_norm_g[li], mla_w_uq[li], mla_kv_norm_g[li], mla_w_ukv[li],
                              swa_sink[li], conv_w[li], w_o[li], norm2_g[li], router_w[li],
                              exp_w_gate[li], exp_w_up[li], exp_w_down[li], rope_mla, rope_swa,
                              li < DEPTH - 1)
    return rmsnorm(xl, final_norm_g)


HEAD_DIM = 64
N_HEADS = 4
MIX_WIDTH_2 = N_HEADS * HEAD_DIM
N_BRANCH = 4
MASK_VALUE = -1e30

SB_QBLOCK = 128

RWKV_DECAY_LORA = 64
RWKV_AAA_LORA = 64
RWKV_MV_LORA = 32
RWKV_GATE_LORA = 128
RWKV_GN_EPS = 64e-5

MOBA_BLOCK = 256
MOBA_TOPK = 3
MOBA_QCHUNK = 32
ROPE_THETA = 500000.0
ROPE_DIM = HEAD_DIM // 4

HGRN_CHUNK = 16

D_FF = -(-(8 * D_MODEL) // (3 * 256)) * 256

SB_COLS = 3 * MIX_WIDTH_2
RWKV_COLS = 3 * MIX_WIDTH_2 + RWKV_DECAY_LORA + RWKV_AAA_LORA + RWKV_GATE_LORA
MOBA_COLS = 3 * MIX_WIDTH_2
HGRN_COLS = 4 * MIX_WIDTH_2
SB_OFF = 0
RWKV_OFF = SB_OFF + SB_COLS
MOBA_OFF = RWKV_OFF + RWKV_COLS
HGRN_OFF = MOBA_OFF + MOBA_COLS
GATE_OFF = HGRN_OFF + HGRN_COLS
IN_COLS = GATE_OFF + N_BRANCH * D_MODEL


def rms_norm(x, g):
    xf = x.astype(jnp.float32)
    y = xf * lax.rsqrt(jnp.mean(xf * xf, axis=-1, keepdims=True) + NORM_EPS)
    return (y * g.astype(jnp.float32)).astype(x.dtype)

def split_heads(t):
    b, s, _ = t.shape
    return t.reshape(b, s, N_HEADS, HEAD_DIM).transpose(0, 2, 1, 3)

def merge_heads(t):
    b, h, s, d = t.shape
    return t.transpose(0, 2, 1, 3).reshape(b, s, h * d)

def stick_breaking_attention(q, k, v):
    seq = q.shape[2]
    scale = HEAD_DIM ** -0.5
    qf = q.astype(jnp.float32)
    kf = k.astype(jnp.float32)
    vf = v.astype(jnp.float32)
    outs = []
    for blk in range(seq // SB_QBLOCK):
        t0 = blk * SB_QBLOCK
        kv_len = t0 + SB_QBLOCK
        z = jnp.einsum('bhtd,bhsd->bhts', qf[:, :, t0:kv_len], kf[:, :, :kv_len]) * scale
        t_pos = t0 + jnp.arange(SB_QBLOCK)[:, None]
        s_pos = jnp.arange(kv_len)[None, :]
        past = s_pos < t_pos
        log_keep = jnp.where(past, jax.nn.log_sigmoid(-z), 0.0)
        log_between = lax.cumsum(log_keep, axis=3, reverse=True) - log_keep
        att = jnp.where(past, jnp.exp(jax.nn.log_sigmoid(z) + log_between), 0.0)
        outs.append(jnp.einsum('bhts,bhsd->bhtd', att, vf[:, :, :kv_len]))
    return jnp.concatenate(outs, axis=2).astype(v.dtype)

def token_shift(p, mu):
    prev = jnp.pad(p, ((0, 0), (1, 0), (0, 0)))[:, :-1]
    return p + (prev - p) * mu

def rwkv7_recurrence(r, w, k, v, a, b):
    bsz, _, nh, nd = r.shape

    def step(state, inp):
        r_t, w_t, k_t, v_t, a_t, b_t = inp
        sa = jnp.einsum('bhvk,bhk->bhv', state, a_t)
        state = (state * w_t[:, :, None, :] + sa[..., None] * b_t[:, :, None, :]
                 + v_t[..., None] * k_t[:, :, None, :])
        return state, jnp.einsum('bhvk,bhk->bhv', state, r_t)

    xs = (jnp.moveaxis(r, 1, 0), jnp.moveaxis(w, 1, 0), jnp.moveaxis(k, 1, 0),
          jnp.moveaxis(v, 1, 0), jnp.moveaxis(a, 1, 0), jnp.moveaxis(b, 1, 0))
    init = jnp.zeros((bsz, nh, nd, nd), jnp.float32)
    _, y = lax.scan(step, init, xs)
    return jnp.moveaxis(y, 0, 1)

def rwkv7_time_mix(p, mu, w0, w2, a0, a2, g2, k_k, k_a, r_k, gn_w, gn_b, v_first, v0, v1, v2):
    bsz, seq, _ = p.shape
    p = token_shift(p, mu).astype(jnp.float32)
    c = MIX_WIDTH_2
    r = p[..., :c]
    k = p[..., c:2 * c]
    v = p[..., 2 * c:3 * c]
    o = 3 * c
    wl = p[..., o:o + RWKV_DECAY_LORA]
    o += RWKV_DECAY_LORA
    al = p[..., o:o + RWKV_AAA_LORA]
    o += RWKV_AAA_LORA
    gl = p[..., o:o + RWKV_GATE_LORA]
    w_log = -jax.nn.softplus(-(w0 + jnp.tanh(wl) @ w2)) - 0.5
    decay = jnp.exp(-jnp.exp(w_log))
    if v_first is None:
        v_first = v
    else:
        v = v + (v_first - v) * jax.nn.sigmoid(v0 + (v @ v1) @ v2)
    a = jax.nn.sigmoid(a0 + al @ a2)
    g = jax.nn.sigmoid(gl) @ g2

    def hs(t):
        return t.reshape(bsz, seq, N_HEADS, HEAD_DIM)

    kk = hs(k * k_k)
    kk = kk / jnp.maximum(jnp.sqrt(jnp.sum(kk * kk, axis=-1, keepdims=True)), 1e-12)
    k = k * (1.0 + (a - 1.0) * k_a)
    rh, kh, vh, ah = hs(r), hs(k), hs(v), hs(a)
    y = rwkv7_recurrence(rh, hs(decay), kh, vh, -kk, kk * ah)
    mean = jnp.mean(y, axis=-1, keepdims=True)
    var = jnp.mean(jnp.square(y - mean), axis=-1, keepdims=True)
    y = ((y - mean) * lax.rsqrt(var + RWKV_GN_EPS)).reshape(bsz, seq, c) * gn_w + gn_b
    bonus = jnp.sum(rh * kh * r_k, axis=-1, keepdims=True) * vh
    y = (y + bonus.reshape(bsz, seq, c)) * g
    return y, v_first

def rotary_tables(seq):
    inv_freq = ROPE_THETA ** (-jnp.arange(0, ROPE_DIM, 2, dtype=jnp.float32) / ROPE_DIM)
    ang = jnp.arange(seq, dtype=jnp.float32)[:, None] * inv_freq[None, :]
    return jnp.cos(ang), jnp.sin(ang)

def partial_rotary(t, cos, sin):
    half = ROPE_DIM // 2
    x1 = t[..., :half]
    x2 = t[..., half:ROPE_DIM]
    return jnp.concatenate([x1 * cos - x2 * sin, x2 * cos + x1 * sin, t[..., ROPE_DIM:]], axis=-1)

def moba_attention(q, k, v):
    bsz, nh, seq, hd = q.shape
    dt = v.dtype
    seq_pad = -(-seq // MOBA_BLOCK) * MOBA_BLOCK
    pad = ((0, 0), (0, 0), (0, seq_pad - seq), (0, 0))
    q = jnp.pad(q.astype(jnp.float32), pad)
    k = jnp.pad(k.astype(jnp.float32), pad)
    v = jnp.pad(v.astype(jnp.float32), pad)
    n_blk = seq_pad // MOBA_BLOCK
    k_blocks = k.reshape(bsz, nh, n_blk, MOBA_BLOCK, hd)
    v_blocks = v.reshape(bsz, nh, n_blk, MOBA_BLOCK, hd)
    k_mean = jnp.mean(k_blocks, axis=3)
    gate = jnp.einsum('bhtd,bhnd->bhtn', q, k_mean)
    q_blk = jnp.arange(seq_pad) // MOBA_BLOCK
    fully_past = jnp.arange(n_blk)[None, :] < q_blk[:, None]
    gate = jnp.where(fully_past, gate, MASK_VALUE)
    n_sel = min(MOBA_TOPK, n_blk)
    _, sel_idx = lax.top_k(gate, n_sel)
    sel_valid = sel_idx < q_blk[None, None, :, None]
    bi = jnp.arange(bsz)[:, None, None, None]
    hi = jnp.arange(nh)[None, :, None, None]
    scale = hd ** -0.5
    n_gathered = n_sel * MOBA_BLOCK

    def attend_chunk(t0):
        qc = lax.dynamic_slice_in_dim(q, t0, MOBA_QCHUNK, axis=2)
        idx = lax.dynamic_slice_in_dim(sel_idx, t0, MOBA_QCHUNK, axis=2)
        valid = lax.dynamic_slice_in_dim(sel_valid, t0, MOBA_QCHUNK, axis=2)
        k_sel = k_blocks[bi, hi, idx]
        v_sel = v_blocks[bi, hi, idx]
        s_sel = jnp.einsum('bhqd,bhqnkd->bhqnk', qc, k_sel) * scale
        s_sel = jnp.where(valid[..., None], s_sel, MASK_VALUE)
        own = t0 // MOBA_BLOCK
        k_own = lax.dynamic_index_in_dim(k_blocks, own, axis=2, keepdims=False)
        v_own = lax.dynamic_index_in_dim(v_blocks, own, axis=2, keepdims=False)
        s_own = jnp.einsum('bhqd,bhkd->bhqk', qc, k_own) * scale
        q_pos = t0 + jnp.arange(MOBA_QCHUNK)
        k_pos = own * MOBA_BLOCK + jnp.arange(MOBA_BLOCK)
        s_own = jnp.where(k_pos[None, :] <= q_pos[:, None], s_own, MASK_VALUE)
        scores = jnp.concatenate([s_sel.reshape(bsz, nh, MOBA_QCHUNK, n_gathered), s_own], axis=-1)
        probs = jax.nn.softmax(scores, axis=-1)
        p_sel = probs[..., :n_gathered].reshape(bsz, nh, MOBA_QCHUNK, n_sel, MOBA_BLOCK)
        p_own = probs[..., n_gathered:]
        return (jnp.einsum('bhqnk,bhqnkd->bhqd', p_sel, v_sel)
                + jnp.einsum('bhqk,bhkd->bhqd', p_own, v_own))

    starts = jnp.arange(seq_pad // MOBA_QCHUNK) * MOBA_QCHUNK
    out = lax.map(attend_chunk, starts)
    out = out.transpose(1, 2, 0, 3, 4).reshape(bsz, nh, seq_pad, hd)[:, :, :seq]
    return out.astype(dt)

def hgrn2_mixer(q, f_logit, i, g, lb, gn_g):
    bsz, seq, _ = q.shape
    n_chunk = seq // HGRN_CHUNK
    q = q.astype(jnp.float32)
    i = i.astype(jnp.float32)
    f_logit = f_logit.astype(jnp.float32)
    lb = lb.astype(jnp.float32)
    sig = jax.nn.sigmoid(f_logit)
    log_f = jnp.log(lb + (1.0 - lb) * sig)
    key = (1.0 - lb) * (1.0 - sig)

    def chunks(t):
        return t.reshape(bsz, n_chunk, HGRN_CHUNK, N_HEADS, HEAD_DIM).transpose(0, 3, 1, 2, 4)

    qc, kc, vc, lc = chunks(q), chunks(key), chunks(i), chunks(log_f)
    b = jnp.cumsum(lc, axis=3)
    b_end = b[:, :, :, -1:, :]
    causal = jnp.tril(jnp.ones((HGRN_CHUNK, HGRN_CHUNK), dtype=bool))
    diff = b[:, :, :, :, None, :] - b[:, :, :, None, :, :]
    pair_decay = jnp.exp(jnp.where(causal[:, :, None], diff, 0.0))
    scores = jnp.einsum('bhnck,bhnsk,bhncsk->bhncs', qc, kc, pair_decay)
    scores = jnp.where(causal, scores, 0.0)
    o = jnp.einsum('bhncs,bhnsv->bhncv', scores, vc)
    q_dec = qc * jnp.exp(b)
    k_end = kc * jnp.exp(b_end - b)
    chunk_kv = jnp.einsum('bhnsk,bhnsv->bhnkv', k_end, vc)
    chunk_decay = jnp.exp(b_end[:, :, :, 0, :])

    def step(state, inp):
        dec, kv = inp
        return dec[..., None] * state + kv, state

    init = jnp.zeros((bsz, N_HEADS, HEAD_DIM, HEAD_DIM), jnp.float32)
    _, prev = lax.scan(step, init, (jnp.moveaxis(chunk_decay, 2, 0), jnp.moveaxis(chunk_kv, 2, 0)))
    prev = jnp.moveaxis(prev, 0, 2)
    o = o + jnp.einsum('bhnck,bhnkv->bhncv', q_dec, prev)
    o = o.transpose(0, 2, 3, 1, 4).reshape(bsz, seq, N_HEADS, HEAD_DIM)
    o = o * lax.rsqrt(jnp.mean(o * o, axis=-1, keepdims=True) + NORM_EPS)
    return o.reshape(bsz, seq, MIX_WIDTH_2) * gn_g * jax.nn.silu(g.astype(jnp.float32))

def second_inputs(seed: int = 0) -> dict:
    key = jax.random.key(seed)
    ks = jax.random.split(key, 32)
    L, D, W = DEPTH, D_MODEL, MIX_WIDTH_2
    LV = max(DEPTH - 1, 0)

    def nrm(k, shape, scale):
        return jax.random.normal(k, shape, jnp.float32) * scale

    return {
        'x': nrm(ks[0], (BATCH, SEQ, D), 1.0),
        'norm1_g': 1.0 + nrm(ks[1], (L, D), 0.02),
        'w_in': nrm(ks[2], (L, D, IN_COLS), D ** -0.5),
        'rwkv_mu': jax.random.uniform(ks[3], (L, RWKV_COLS), jnp.float32),
        'rwkv_w0': nrm(ks[4], (L, W), 0.5),
        'rwkv_w2': nrm(ks[5], (L, RWKV_DECAY_LORA, W), 0.1),
        'rwkv_a0': nrm(ks[6], (L, W), 0.1),
        'rwkv_a2': nrm(ks[7], (L, RWKV_AAA_LORA, W), 0.1),
        'rwkv_g2': nrm(ks[8], (L, RWKV_GATE_LORA, W), RWKV_GATE_LORA ** -0.5),
        'rwkv_k_k': 1.0 + nrm(ks[9], (L, W), 0.1),
        'rwkv_k_a': 1.0 + nrm(ks[10], (L, W), 0.1),
        'rwkv_r_k': nrm(ks[11], (L, N_HEADS, HEAD_DIM), 0.1),
        'rwkv_gn_w': 1.0 + nrm(ks[12], (L, W), 0.02),
        'rwkv_gn_b': nrm(ks[13], (L, W), 0.02),
        'rwkv_v0': nrm(ks[14], (LV, W), 0.1),
        'rwkv_v1': nrm(ks[15], (LV, W, RWKV_MV_LORA), W ** -0.5),
        'rwkv_v2': nrm(ks[16], (LV, RWKV_MV_LORA, W), 0.1),
        'hgrn_lb_logits': nrm(ks[17], (L, W), 1.0),
        'hgrn_gn_g': 1.0 + nrm(ks[18], (L, W), 0.02),
        'w_branch': nrm(ks[19], (L, N_BRANCH, W, D), W ** -0.5),
        'w_out': nrm(ks[20], (L, D, D), D ** -0.5),
        'norm2_g': 1.0 + nrm(ks[21], (L, D), 0.02),
        'w_ffn_gate': nrm(ks[22], (L, D, D_FF), D ** -0.5),
        'w_ffn_up': nrm(ks[23], (L, D, D_FF), D ** -0.5),
        'w_ffn_down': nrm(ks[24], (L, D_FF, D), D_FF ** -0.5),
        'final_g': 1.0 + nrm(ks[25], (D,), 0.02),
    }

def second_block(x, norm1_g, w_in, rwkv_mu, rwkv_w0, rwkv_w2, rwkv_a0, rwkv_a2, rwkv_g2,
              rwkv_k_k, rwkv_k_a, rwkv_r_k, rwkv_gn_w, rwkv_gn_b, rwkv_v0, rwkv_v1, rwkv_v2,
              hgrn_lb_logits, hgrn_gn_g, w_branch, w_out, norm2_g, w_ffn_gate, w_ffn_up,
              w_ffn_down, final_g):
    seq = x.shape[1]
    W = MIX_WIDTH_2
    cos, sin = rotary_tables(seq)
    lb_w = jax.nn.softmax(hgrn_lb_logits.astype(jnp.float32), axis=0)
    lower_bounds = jnp.cumsum(lb_w, axis=0) - lb_w[0]
    v_first = None
    for layer in range(DEPTH):
        h = rms_norm(x, norm1_g[layer])
        w_l = w_in[layer]

        def cols(lo, width):
            return h @ w_l[:, lo:lo + width]

        sb = cols(SB_OFF, SB_COLS)
        y_sb = merge_heads(stick_breaking_attention(
            split_heads(sb[..., :W]), split_heads(sb[..., W:2 * W]), split_heads(sb[..., 2 * W:])))
        if layer == 0:
            v0 = v1 = v2 = None
        else:
            v0, v1, v2 = rwkv_v0[layer - 1], rwkv_v1[layer - 1], rwkv_v2[layer - 1]
        y_rwkv, v_first = rwkv7_time_mix(
            cols(RWKV_OFF, RWKV_COLS), rwkv_mu[layer], rwkv_w0[layer], rwkv_w2[layer],
            rwkv_a0[layer], rwkv_a2[layer], rwkv_g2[layer], rwkv_k_k[layer], rwkv_k_a[layer],
            rwkv_r_k[layer], rwkv_gn_w[layer], rwkv_gn_b[layer], v_first, v0, v1, v2)
        mc = cols(MOBA_OFF, MOBA_COLS)
        q_m = partial_rotary(split_heads(mc[..., :W]), cos, sin)
        k_m = partial_rotary(split_heads(mc[..., W:2 * W]), cos, sin)
        y_moba = merge_heads(moba_attention(q_m, k_m, split_heads(mc[..., 2 * W:])))
        hc = cols(HGRN_OFF, HGRN_COLS)
        y_hgrn = hgrn2_mixer(hc[..., :W], hc[..., W:2 * W], hc[..., 2 * W:3 * W], hc[..., 3 * W:],
                             lower_bounds[layer], hgrn_gn_g[layer])
        merged = None
        for n, y_n in enumerate((y_sb, y_rwkv, y_moba, y_hgrn)):
            gate = jax.nn.sigmoid(cols(GATE_OFF + n * D_MODEL, D_MODEL))
            term = gate * (y_n.astype(x.dtype) @ w_branch[layer, n])
            merged = term if merged is None else merged + term
        x = x + merged @ w_out[layer]
        h2 = rms_norm(x, norm2_g[layer])
        x = x + (jax.nn.silu(h2 @ w_ffn_gate[layer]) * (h2 @ w_ffn_up[layer])) @ w_ffn_down[layer]
    return rms_norm(x, final_g)


def setup_inputs(seed=0):
    out = dict(first_inputs(seed))
    for name, value in second_inputs(seed + 1).items():
        if name != "x":
            out[name + "_2"] = value
    return out


def reference(
    x, c, ctx, c_ctx, ada_w, ada_b, norm1_g, w_in, mla_q_norm_g, mla_w_uq, mla_kv_norm_g,
    mla_w_ukv, swa_sink, conv_w, w_o, norm2_g, router_w, exp_w_gate, exp_w_up, exp_w_down,
    final_norm_g, norm1_g_2, w_in_2, rwkv_mu_2, rwkv_w0_2, rwkv_w2_2, rwkv_a0_2, rwkv_a2_2,
    rwkv_g2_2, rwkv_k_k_2, rwkv_k_a_2, rwkv_r_k_2, rwkv_gn_w_2, rwkv_gn_b_2, rwkv_v0_2,
    rwkv_v1_2, rwkv_v2_2, hgrn_lb_logits_2, hgrn_gn_g_2, w_branch_2, w_out_2, norm2_g_2,
    w_ffn_gate_2, w_ffn_up_2, w_ffn_down_2, final_g_2,
):
    x = first_block(
        x, c, ctx, c_ctx, ada_w, ada_b, norm1_g, w_in, mla_q_norm_g, mla_w_uq, mla_kv_norm_g,
        mla_w_ukv, swa_sink, conv_w, w_o, norm2_g, router_w, exp_w_gate, exp_w_up, exp_w_down,
        final_norm_g,
    )
    return second_block(
        x, norm1_g_2, w_in_2, rwkv_mu_2, rwkv_w0_2, rwkv_w2_2, rwkv_a0_2, rwkv_a2_2, rwkv_g2_2,
        rwkv_k_k_2, rwkv_k_a_2, rwkv_r_k_2, rwkv_gn_w_2, rwkv_gn_b_2, rwkv_v0_2, rwkv_v1_2,
        rwkv_v2_2, hgrn_lb_logits_2, hgrn_gn_g_2, w_branch_2, w_out_2, norm2_g_2, w_ffn_gate_2,
        w_ffn_up_2, w_ffn_down_2, final_g_2,
    )


_drawn_inputs = setup_inputs


def setup_inputs(seed=0):
    import zlib

    import numpy as np

    out = dict(_drawn_inputs(seed))
    spreads = {}
    factors = {'norm1_g': 2.764,
     'mla_q_norm_g': 8.0,
     'mla_kv_norm_g': 8.0,
     'swa_sink': 64.0,
     'norm2_g': 3.036,
     'rwkv_k_k_2': 6.447,
     'rwkv_gn_w_2': 6.118,
     'rwkv_gn_b_2': 6.445,
     'rwkv_v0_2': 5.288,
     'hgrn_gn_g_2': 6.519,
     'norm2_g_2': 2.851,
     'final_g_2': 8.002}
    for name, (base, spread) in spreads.items():
        noise = np.random.default_rng([zlib.crc32(name.encode()), seed]).standard_normal(out[name].shape)
        drawn = base * np.exp(spread * noise) if base else spread * noise
        out[name] = jnp.asarray(drawn.astype(out[name].dtype))
    for name, factor in factors.items():
        out[name] = (out[name] * factor).astype(out[name].dtype)
    return out
```

```python
import numpy as np
import concourse.bass as bass
from concourse import mybir
from contextlib import ExitStack

F32 = mybir.dt.float32
U32 = mybir.dt.uint32
ALU = mybir.AluOpType
ACT = mybir.ActivationFunctionType
AX = mybir.AxisListType.X

P = 128
D = 1024
KD = D // P
S = 256
T2 = 2 * S
EPS = 1e-6
NEG = -1e30
L = 2
H1 = 6
NE, CAP, FF = 16, 32, 512
DFF = 2816
NF = DFF // P
MLA_SCALE = 96 ** -0.5
HEAD_SCALE = 64 ** -0.5
GN_EPS = 64e-5
SLOT = 4096
RING = 3
LEVELS = 7


def constants():
    cols, at, width = ([], []), {}, [0, 0]

    def put(name, a, first=False):
        a = np.asarray(a, np.float32)
        full = np.zeros((P, a.shape[1]), np.float32)
        full[:a.shape[0]] = a
        cols[first].append(full)
        at[name] = (first, width[first], a.shape[1])
        width[first] += a.shape[1]

    i = np.arange(P)
    t = np.arange(S)
    put("ident", np.eye(P))
    put("ones", np.ones((P, P)))
    put("heads", (i[:, None] // 64 == i[None, :] // 64))
    put("suffix", (i[:, None] >= i[None, :]))
    lev = []
    for l in range(LEVELS):
        n = 2 ** l
        a, b = i[:, None] // n, i[None, :] // n
        lev.append((a // 2 == b // 2) & (a % 2 == 0) & (b % 2 == 1))
    put("levels", np.concatenate(lev, 1))
    put("before", i[:, None] < i[None, :])
    put("upto", i[:, None] <= i[None, :])
    put("seg", np.tile((i > 0)[None, :], (P, 4)))
    put("no_sink", np.full((P, 1), NEG))
    q = np.arange(2)[None, :, None] * P + i[:, None, None]
    put("window", np.where(np.abs(q - t[None, None, :]) <= 128, 0, NEG).reshape(P, -1), True)
    put("causal", np.where(t[None, None, :] <= q, 0, NEG).reshape(P, -1))
    put("stick", np.where(q < t[None, None, :], -1.0, 0).reshape(P, -1))
    put("stick_add", np.where(q < t[None, None, :], 0, NEG).reshape(P, -1))

    def axial(rot):
        n = rot // 4
        inv = np.float32(10000.0) ** (-np.arange(n, dtype=np.float32) / np.float32(n))
        row, col = (t // 64).astype(np.float32), (t % 64).astype(np.float32)
        ang = np.concatenate([row[:, None] * inv, col[:, None] * inv], 1).astype(np.float32)
        return np.cos(ang).T, np.sin(ang).T

    def rot(n, base, half):
        r = np.zeros((n, n), np.float32)
        for b in base:
            for k in range(half):
                r[b + half + k, b + k] = -1.0
                r[b + k, b + half + k] = 1.0
        return r

    c, s = axial(64)
    put("cos_swa", np.tile(c, (4, 1)), True)
    put("sin_swa", np.tile(s, (4, 1)), True)
    rs = rot(P, (0, 64), 32)
    put("rot_swa", rs, True)
    for g in range(2):
        dup = np.zeros((P, P), np.float32)
        dup[64 * g + i % 64, i] = 1.0
        put(f"dup{g}", dup, True)
        put(f"duprot{g}", rs @ dup, True)
    c, s = axial(32)
    put("cos_mla", np.concatenate([np.ones((64, S)), c, c]), True)
    put("sin_mla", np.concatenate([np.zeros((64, S)), s, s]), True)
    put("rot_mla", rot(96, (64,), 16), True)
    inv = np.float32(500000.0) ** (-np.arange(0, 16, 2, dtype=np.float32) / np.float32(16))
    ang = (t.astype(np.float32)[:, None] * inv[None, :]).astype(np.float32)
    c, s = np.cos(ang).T, np.sin(ang).T
    one = np.concatenate([c, c, np.ones((48, S))])
    zero = np.concatenate([s, s, np.zeros((48, S))])
    put("cos_moba", np.concatenate([one, one]))
    put("sin_moba", np.concatenate([zero, zero]))
    put("rot_moba", rot(P, (0, 64), 8))
    e = np.zeros((32, 8, P), np.float32)
    for sg in range(8):
        for p in range(P):
            e[(sg // 4) * 16 + (sg % 4) * 4 + p // CAP, sg, p] = 1.0
    put("spread", e.reshape(32, -1), True)
    put("slot", (i % CAP + 1)[:, None], True)
    put("slots", np.tile(np.arange(1, CAP + 1)[None, :], (P, 1)), True)
    return np.concatenate(cols[0] + cols[1], 1), at, width


CONST, CONST_AT, (N_BOTH, N_FIRST) = constants()

VECS = [
    ("ada_b", 96), ("norm1_g", 16), ("norm2_g", 16),
    ("mla_q_norm_g", 4), ("mla_kv_norm_g", 2), ("conv_w", 12), ("norm1_g_2", 16), ("norm2_g_2", 16),
    ("rwkv_mu_2", 16), ("final_g_2", 8), ("rwkv_w0_2", 4), ("rwkv_a0_2", 4), ("rwkv_k_k_2", 4),
    ("rwkv_k_a_2", 4), ("rwkv_r_k_2", 4), ("rwkv_gn_w_2", 4), ("rwkv_gn_b_2", 4), ("rwkv_v0_2", 2),
    ("hgrn_lb_logits_2", 4), ("hgrn_gn_g_2", 4), ("final_norm_g", 8),
]


class Book:

    def __init__(self):
        self.old, self.new = {}, {}

    def turn(self):
        self.old, self.new = self.new, {}


class Signals:

    def __init__(self, engine, nc, ctx, book):
        self.engine, self.nc, self.ctx, self.book, self.sems, self.n = engine, nc, ctx, book, {}, {}
        self.last = None

    def sem(self, kind):
        kind = kind.split("_")[0]
        if kind not in self.sems:
            self.sems[kind] = self.ctx.enter_context(self.nc.semaphore(f"{self.engine}_{kind}"))
            self.n[kind] = 0
        return self.sems[kind]

    def mark(self, *key):
        s, kind = self.sem(key[0]), key[0].split("_")[0]
        self.n[kind] += 1
        self.book.new[(self.engine,) + key] = self.n[kind]
        self.last = (kind, self.n[kind])
        return s, 1

    def at(self, *key):
        return self.sem(key[0]), self.book.old.get((self.engine,) + key, 1)

    def now(self, kind):
        return self.sem(kind), self.n[kind.split("_")[0]]

    def close(self, tag):
        self.book.new[("join", self.engine, tag)] = self.last

    def closed(self, tag):
        kind, n = self.book.old.get(("join", self.engine, tag)) or ("chain", 0)
        return (self.sem(kind), n) if n else None


def program(nc, A, out, book):
    ctx = ExitStack()
    with ctx:
        def sb(name, n):
            return ctx.enter_context(nc.sbuf_tensor(name, [P, n], F32))

        def sem(name):
            return ctx.enter_context(nc.semaphore(name))

        tensor, scalar, vector = (Signals(n, nc, ctx, book) for n in ("tensor", "scalar", "vector"))
        loaded = [sem(f"slot_loaded_{i}") for i in range(RING)]
        const_loaded, small_loaded, stored = (sem(n) for n in ("const_loaded", "small_loaded", "stored"))
        V, SC, PE = nc.vector, nc.scalar, nc.tensor

        ring = sb("ring", RING * SLOT)
        x = sb("x", KD * T2)[:, :].rearrange("p (k t) -> p k t", k=KD)
        h = sb("h", KD * T2)[:, :].rearrange("p (k t) -> p k t", k=KD)
        cst = sb("cst", N_BOTH)
        vec = sb("vec", 256)
        mods = sb("mods", 2 * 96)[:, :].rearrange("p (l m s) -> p l m s", l=L, s=2)
        stat = sb("stat", 160)
        rstd = sb("rstd", T2)
        wa2 = sb("wa2", L * 256)[:, :].rearrange("p (l n) -> p l n", l=L)
        g2w = sb("g2w", L * 256)[:, :].rearrange("p (l n) -> p l n", l=L)
        v1w = sb("v1w", 64)[:, :].rearrange("p (k n) -> p k n", k=2)
        v2w = sb("v2w", 256)
        v_first = sb("v_first", 512)[:, :].rearrange("p (c t) -> p c t", c=2)
        AR1 = 16384
        n_first = N_FIRST + L * (2 * 576 + 768 + KD * NE + 12)
        AR = max(AR1 + n_first, 25096)
        arena = sb("arena", AR)
        o = AR1
        cst1 = arena[:, o:o + N_FIRST]
        o += N_FIRST
        uq = arena[:, o:o + L * 1152].rearrange("p (l k n) -> p l k n", l=L, k=2)
        o += L * 1152
        ukv = arena[:, o:o + L * 768].rearrange("p (l n) -> p l n", l=L)
        o += L * 768
        rtr = arena[:, o:o + L * 128].rearrange("p (l k e) -> p l k e", l=L, k=KD)
        o += L * 128
        sinkb = arena[:, o:o + L * 12].rearrange("p (l n) -> p l n", l=L)
        banks = [ctx.enter_context(nc.psum_tensor(f"bank{i}", [P, 512], F32)) for i in range(8)]

        def C(name):
            first, a, n = CONST_AT[name]
            return (cst1 if first else cst)[:, a:a + n]

        ident, ones = C("ident"), C("ones")
        vcol, row = {}, 0
        for name, n in VECS:
            vcol[name] = row
            row += n
        rows = row

        def vc(name, i, n=1):
            return vec[:, vcol[name] + i:vcol[name] + i + n]

        def tiles(off, n, w):
            return arena[:, off:off + n * w].rearrange("p (n w) -> p n w", n=n)

        def flat(a):
            return a.rearrange("p c t -> p (c t)")

        def mm(o, lhsT, rhs, k, n):
            return PE.matmul(o, lhsT, rhs, start=(k == 0), stop=(k == n - 1))

        turn, rotating = [0], [8]
        holder = [None] * 8

        def got(*key):
            return (scalar if ("scalar",) + key in book.old else vector).at(*key)

        def take(pe, *key):
            if key[0] == "hgrn_scores":
                b = 6 + key[-1]
            else:
                b = turn[0] % rotating[0]
                turn[0] += 1
            if holder[b]:
                pe.wait_ge(*got(*holder[b]))
            holder[b] = key
            book.new[("bank",) + key] = b
            return banks[b]

        def bank(*key):
            return banks[book.old.get(("bank",) + key, 0)]

        def join(me, eng, tag):
            me.close(tag)
            for s in (tensor, scalar, vector):
                value = s.closed(tag)
                if value:
                    eng.wait_ge(*value)

        stream, used = [], {}

        def w_chunk(src, k, n):
            stream.append((src.rearrange("(k p) n -> p k n", p=P), k, n))

        IN1 = [(1312, 1824), (928, 1312), (0, 416), (416, 928)]
        IN2 = [(0, 512), (512, 768), (1792, 2304), (2304, 2560), (768, 1280), (1280, 1792), (2560, 3072), (3072, 3584)]
        ADA_LATE = 12

        def ada_chunk(l, i):
            w_chunk(A["ada_w"][l, :, i * 512:(i + 1) * 512], KD, 512)

        expert_chunk = {}
        for i in range(12):
            ada_chunk(0, i)
        for l in range(L):
            for a, b in IN1:
                w_chunk(A["w_in"][l, :, a:b], KD, b - a)
            if l == 0:
                for i in range(ADA_LATE):
                    ada_chunk(1, i)
            for i in range(2):
                w_chunk(A["w_o"][l, :, i * 512:(i + 1) * 512], KD, 512)
            expert_chunk[l] = len(stream)
            for e in range(NE):
                w_chunk(A["exp_w_gate"][l, e], KD, FF)
                w_chunk(A["exp_w_up"][l, e], KD, FF)
                w_chunk(A["exp_w_down"][l, e], FF // P, D)
        for l in range(L):
            for a, b in IN2:
                w_chunk(A["w_in_2"][l, :, a:b], KD, b - a)
            for i in range(2):
                for br in range(4):
                    a = 3584 + br * D + i * 512
                    w_chunk(A["w_in_2"][l, :, a:a + 512], KD, 512)
                w_chunk(A["w_branch_2"][l].rearrange("b k n -> (b k) n")[:, i * 512:(i + 1) * 512], 8, 512)
            for i in range(2):
                w_chunk(A["w_out_2"][l, :, i * 512:(i + 1) * 512], KD, 512)
            for i in range(6):
                n = min(512, DFF - i * 512)
                w_chunk(A["w_ffn_gate_2"][l, :, i * 512:i * 512 + n], KD, n)
                w_chunk(A["w_ffn_up_2"][l, :, i * 512:i * 512 + n], KD, n)
            for i in range(KD):
                w_chunk(A["w_ffn_down_2"][l, :, i * P:(i + 1) * P], NF, P)

        def slot(n):
            src, k, w = stream[n]
            return ring[:, n % RING * SLOT:n % RING * SLOT + k * w].rearrange("p (k n) -> p k n", k=k)

        at = [0]

        def next_weights(pe):
            n = at[0]
            at[0] += 1
            pe.wait_ge(loaded[n % RING], 16 * (n // RING + 1))
            return slot(n)

        def chunk_read():
            book.new[("used", at[0] - 1)] = tensor.last


        stage = arena[:, 0:384].rearrange("p (s c) -> p s c", c=P)
        xtok = arena[:, 512:512 + 4096].rearrange("p (s j d) -> p s j d", s=2, j=2)
        sink_row = stat[0:1, 128:152]
        cond = stat[:, 80:96].rearrange("p (s k) -> p s k", s=2)
        TURNS = ((0, P), (1, rows - P), (2, 16))

        def start_tensor(pe):
            for s, n in TURNS:
                b = take(pe, "turned", s)
                PE.transpose(b[:, 0:n], stage[0:n, s, :], ident[0:n, 0:n]).then_inc(*tensor.mark("turned", s))
            b = take(pe, "sinks")
            mm(b[:, 0:12], ones[0:1, :], sink_row[:, 0:12], 0, 1).then_inc(*tensor.mark("sinks"))
            for s in range(2):
                for k in range(KD):
                    b = take(pe, "streams", s, k)
                    for j in range(2):
                        last = PE.transpose(b[:, j * P:(j + 1) * P], xtok[:, s, j, k * P:(k + 1) * P], ident)
                    last.then_inc(*tensor.mark("streams", s, k))

        def start_vector(dve):
            for s, n in TURNS:
                dve.wait_ge(*tensor.at("turned", s))
                dst = vec[:, s * P:s * P + n] if s < 2 else stat[:, 64:80]
                V.tensor_copy(dst, bank("turned", s)[:, 0:n]).then_inc(*vector.mark("turned", s))
            V.memset(sinkb, NEG).then_inc(*vector.mark("chain"))
            dve.wait_ge(*vector.now("chain"))
            dve.wait_ge(*tensor.at("sinks"))
            V.tensor_copy(sinkb[:, :, 6:12], bank("sinks")[:, 0:12].rearrange("p (l n) -> p l n", l=L))\
             .then_inc(*vector.mark("sinks"))
            for k in range(KD):
                dve.wait_ge(*tensor.at("streams", 0, k))
                V.tensor_copy(x[:, k, 0:S], bank("streams", 0, k)[:, 0:S]).then_inc(*vector.mark("streams", 0, k))

        def start_scalar(act):
            act.wait_ge(*vector.at("turned", 2))
            SC.activation(stat[:, 80:96], stat[:, 64:80], ACT.Silu).then_inc(*scalar.mark("cond"))
            for k in range(KD):
                act.wait_ge(*tensor.at("streams", 1, k))
                SC.activation(x[:, k, S:T2], bank("streams", 1, k)[:, 0:S], ACT.Copy).then_inc(*scalar.mark("streams", 1, k))

        def ada_tensor(pe, l, i):
            w = next_weights(pe)
            b = take(pe, "mods", l, i)
            for m in range(4):
                for k in range(KD):
                    last = mm(b[:, 2 * m:2 * m + 2], w[:, k, m * P:(m + 1) * P], cond[:, :, k], k, KD)
            last.then_inc(*tensor.mark("mods", l, i))
            chunk_read()

        def ada_vector(dve, l, i):
            dve.wait_ge(*tensor.at("mods", l, i))
            V.tensor_tensor(mods[:, l, 4 * i:4 * i + 4, :], bank("mods", l, i)[:, 0:8].rearrange("p (m s) -> p m s", s=2),
                            vec[:, l * 48 + 4 * i:l * 48 + 4 * i + 4].unsqueeze(2).broadcast_to((P, 4, 2)), ALU.add)\
             .then_inc(*vector.mark("mods", l, i))

        def link(dve, ins):
            ins.then_inc(*vector.mark("chain"))
            dve.wait_ge(*vector.now("chain"))

        def link_s(act, ins):
            ins.then_inc(*scalar.mark("chain"))
            act.wait_ge(*scalar.now("chain"))

        def norm_scalar(act, T, tag):
            SC.activation(h[:, :, 0:T], x[:, :, 0:T], ACT.Square).then_inc(*scalar.mark("squares", tag))
            act.wait_ge(*vector.at("mean", tag))
            SC.activation(rstd[:, 0:T], rstd[:, 0:T], ACT.Sqrt).then_inc(*scalar.mark("root", tag))

        def norm_tensor(pe, T, tag):
            pe.wait_ge(*scalar.at("squares", tag))
            b = take(pe, "mean", tag)
            for k in range(KD):
                last = mm(b[:, 0:T], ones, h[:, k, 0:T], k, KD)
            last.then_inc(*tensor.mark("mean", tag))

        def norm_vector(dve, T, tag, gain, shift=None):
            dve.wait_ge(*tensor.at("mean", tag))
            link(dve, V.tensor_scalar(rstd[:, 0:T], bank("mean", tag)[:, 0:T], 1.0 / D, EPS, ALU.mult, ALU.add))
            V.reciprocal(rstd[:, 0:T], rstd[:, 0:T]).then_inc(*vector.mark("mean", tag))
            dve.wait_ge(*scalar.at("root", tag))
            for k in range(KD):
                V.tensor_tensor(h[:, k, 0:T], x[:, k, 0:T], rstd[:, 0:T], ALU.mult).then_inc(*vector.mark("chain"))
                dve.wait_ge(*vector.now("chain"))
                for s in range(T // S):
                    a = h[:, k, s * S:(s + 1) * S]
                    if shift is None:
                        V.tensor_scalar(a, a, gain(s, k), None, ALU.mult).then_inc(*vector.mark("normed", tag, k))
                    else:
                        V.tensor_scalar(a, a, gain(s, k), shift(s, k), ALU.mult, ALU.add).then_inc(*vector.mark("normed", tag, k))

        gcol = stat[:, 0:16].rearrange("p (k s) -> p k s", s=2)

        def modulation_vector(dve, l, gname, sh, sc):
            link(dve, V.scalar_tensor_tensor(gcol, mods[:, l, sc:sc + 8, :], 1.0,
                                             vc(gname, 8 * l, 8).unsqueeze(2).broadcast_to((P, 8, 2)), ALU.add, ALU.mult))
            return (lambda s, k: gcol[:, k, s:s + 1]), (lambda s, k: mods[:, l, sh + k, s:s + 1])

        def project_tensor(pe, w, c0, n, T, key, parts=None):
            b = take(pe, *key)
            ps = b[parts if parts else slice(0, n), 0:T]
            for k in range(KD):
                last = mm(ps, w[:, k, c0:c0 + n], h[:, k, 0:T], k, KD)
            last.then_inc(*tensor.mark(*key))

        def out_vector(dve, dst, src, *key):
            dve.wait_ge(*tensor.at(*key))
            V.tensor_copy(dst, src).then_inc(*vector.mark(*key))

        def out_scalar(act, dst, src, *key, func=ACT.Copy, **kw):
            act.wait_ge(*tensor.at(*key))
            SC.activation(dst, src, func, **kw).then_inc(*scalar.mark(*key))

        def rotate_tensor(pe, q, rot, K, key):
            b = take(pe, *key)
            mm(b[K, 0:S], rot, q, 0, 1).then_inc(*tensor.mark(*key))

        def rotate_vector(dve, q, cos, sin, K, key):
            dve.wait_ge(*tensor.at(*key))
            ps = bank(*key)[K, 0:S]
            V.tensor_tensor(ps, ps, sin, ALU.mult).then_inc(*vector.mark("chain"))
            link(dve, V.tensor_tensor(q, q, cos, ALU.mult))
            V.tensor_tensor(q, q, ps, ALU.add).then_inc(*vector.mark(*key))

        def attend_tensor(pe, heads, prob, probT, tag, between=None):
            def scores(i):
                q, keys, nk = heads[i][0:3]
                for j in range(2):
                    b = take(pe, "scores", tag, i, j)
                    mm(b[:, 0:nk], q(j), keys, 0, 1).then_inc(*tensor.mark("scores", tag, i, j))

            def values(i):
                nk, vals, parts = heads[i][2:5]
                n = nk // P
                for j in range(2):
                    pe.wait_ge(*vector.at("probs", tag, i, j))
                    b = take(pe, "turned_probs", tag, i, j)
                    for k in range(n):
                        last = PE.transpose(b[:, k * P:(k + 1) * P], prob[i % 2][:, j, k * P:(k + 1) * P], ident)
                    last.then_inc(*tensor.mark("turned_probs", tag, i, j))
                b = take(pe, "attended", tag, i)
                for j in range(2):
                    pe.wait_ge(*got("turned_probs", tag, i, j))
                for k in range(n):
                    last = mm(b[parts, 0:S], vals(k), probT[i % 2][:, k, :], k, n)
                last.then_inc(*tensor.mark("attended", tag, i))

            for i in range(len(heads) + 1):
                if i < len(heads):
                    scores(i)
                if between:
                    between(i)
                if i:
                    values(i - 1)

        def attend_vector(dve, heads, prob, probT, tag, between=None):
            def stats(i):
                nk, mask, sink, scale = heads[i][2], heads[i][6], heads[i][7], heads[i][8]
                mx, nm, es = (stat[:, 32 + 8 * (i % 2) + 2 * n:34 + 8 * (i % 2) + 2 * n] for n in range(3))
                for j in range(2):
                    dve.wait_ge(*tensor.at("scores", tag, i, j))
                    b = bank("scores", tag, i, j)
                    if mask is not None:
                        link(dve, V.tensor_tensor(b[:, 0:S], b[:, 0:S], mask[:, j, :], ALU.add))
                    V.reduce_max(mx[:, j:j + 1], b[:, 0:nk], AX).then_inc(*vector.mark("chain"))
                dve.wait_ge(*vector.now("chain"))
                sk = sink.broadcast_to((P, 2))
                link(dve, V.scalar_tensor_tensor(mx, mx, scale, sk, ALU.mult, ALU.max))
                V.tensor_scalar(nm, mx, -1.0, None, ALU.mult).then_inc(*vector.mark("chain"))
                V.tensor_tensor(es, sk, mx, ALU.subtract).then_inc(*vector.mark("maxima", tag, i))

            def normalise(i):
                nk = heads[i][2]
                es, sm = (stat[:, 32 + 8 * (i % 2) + 2 * n:34 + 8 * (i % 2) + 2 * n] for n in (2, 3))
                dve.wait_ge(*scalar.at("sink", tag, i))
                link(dve, V.tensor_tensor(sm, sm, es, ALU.add))
                link(dve, V.reciprocal(sm, sm))
                for j in range(2):
                    pr = prob[i % 2][:, j, 0:nk]
                    V.tensor_scalar(pr, pr, sm[:, j:j + 1], None, ALU.mult).then_inc(*vector.mark("probs", tag, i, j))
                out_turned(i, 1)

            def out_turned(i, j):
                n = heads[i][2] // P
                out_vector(dve, probT[i % 2][:, 0:n, j * P:(j + 1) * P],
                           bank("turned_probs", tag, i, j)[:, 0:n * P].rearrange("p (k q) -> p k q", k=n),
                           "turned_probs", tag, i, j)

            for i in range(len(heads) + 1):
                if i < len(heads):
                    stats(i)
                if between:
                    between(i)
                if i:
                    normalise(i - 1)

        def attend_scalar(act, heads, prob, probT, tag, between=None):
            def exps(i):
                nk, scale = heads[i][2], heads[i][8]
                nm, es, sm = (stat[:, 32 + 8 * (i % 2) + 2 * n:34 + 8 * (i % 2) + 2 * n] for n in (1, 2, 3))
                act.wait_ge(*vector.at("maxima", tag, i))
                if i >= 2:
                    act.wait_ge(*tensor.at("turned_probs", tag, i - 2, 1))
                for j in range(2):
                    SC.activation(prob[i % 2][:, j, 0:nk], bank("scores", tag, i, j)[:, 0:nk], ACT.Exp,
                                  bias=nm[:, j:j + 1], scale=scale, accum_out=sm[:, j:j + 1])\
                      .then_inc(*scalar.mark("scores", tag, i, j))
                SC.activation(es, es, ACT.Exp).then_inc(*scalar.mark("sink", tag, i))

            def outs(i):
                nk, parts, dst = heads[i][2], heads[i][4], heads[i][5]
                n = nk // P
                out_scalar(act, probT[i % 2][:, 0:n, 0:P],
                           bank("turned_probs", tag, i, 0)[:, 0:n * P].rearrange("p (k q) -> p k q", k=n),
                           "turned_probs", tag, i, 0)
                out_scalar(act, dst, bank("attended", tag, i)[parts, 0:S], "attended", tag, i)

            for i in range(len(heads) + 1):
                if i < len(heads):
                    exps(i)
                if between:
                    between(i)
                if i:
                    outs(i - 1)

        bcu, k96, cv = tiles(0, 6, 512), tiles(0, 6, 512), tiles(3072, 2, 512)
        swaq, kd, q96, vall = tiles(4096, 3, 512), tiles(5632, 2, 512), tiles(6656, 6, 512), tiles(9728, 4, 512)
        prob1 = [tiles(11776, 2, 512), tiles(12800, 2, 512)]
        probT1 = [tiles(13824, 4, 256), tiles(14848, 4, 256)]
        cq, ckv, swak, swav = tiles(11776, 2, 512), tiles(12800, 1, 512), tiles(13312, 1, 512), tiles(13824, 1, 512)
        sq, krb = tiles(14336, 3, 512), tiles(15872, 1, 512)
        LO, HI = slice(0, 64), slice(64, 96)
        mix = h
        z = q96[:, 0:3, :].rearrange("p a b -> p (a b)")[:, 0:2 * 2 * (S + 2)].rearrange("p (c s t) -> p c s t", c=2, s=2)

        def in_list(l):
            TQ = T2 if l < L - 1 else S
            return [
                [(i * P, P, TQ, bcu[:, 2 + i, 0:TQ], None) for i in range(4)],
                [(0, P, T2, swav[:, 0, :], None)] + [(P + i * P, P, TQ, bcu[:, i, 0:TQ], None) for i in range(2)],
                [(i * P, P, TQ, cq[:, i, 0:TQ], None) for i in range(2)] + [(256, P, T2, ckv[:, 0, :], None),
                                                                            (384, 32, T2, krb[HI, 0, :], HI)],
                [(i * P, P, TQ, swaq[:, i, 0:TQ], None) for i in range(3)] + [(384, P, T2, swak[:, 0, :], None)],
            ]

        def head_list(l, s):
            k0, nk = (0, T2) if s == 0 else (S, S)
            window = C("window").rearrange("p (a t) -> p a t", a=2)
            heads = []
            for hd in range(12):
                o = 64 * (hd % 2)
                parts = slice(o, o + 64)
                if hd < 6:
                    q = lambda j, hd=hd: q96[0:96, hd, s * S + j * P:s * S + j * P + P]
                    keys = k96[0:96, hd, k0:k0 + nk]
                    vals = lambda k, hd=hd: vall[:, k + 2 * s, 64 * hd:64 * hd + 64]
                else:
                    q = lambda j, hd=hd, parts=parts: swaq[parts, hd // 2 - 3, s * S + j * P:s * S + j * P + P]
                    keys = kd[parts, (hd - 6) // 3, k0:k0 + nk]
                    vals = lambda k, hd=hd: vall[:, k + 2 * s, 384 + 64 * ((hd - 6) // 3):448 + 64 * ((hd - 6) // 3)]
                heads.append((q, keys, nk, vals, parts, mix[parts, hd // 2, s * S:(s + 1) * S],
                              window if hd >= 6 and s == 0 else None, sinkb[:, l, hd:hd + 1],
                              MLA_SCALE if hd < 6 else HEAD_SCALE))
            return heads

        ROT_MLA = (C("rot_mla")[0:96, 0:96], C("cos_mla")[0:96, :], C("sin_mla")[0:96, :])

        def hybrid_tensor(pe, l):
            TQ = T2 if l < L - 1 else S
            norm_tensor(pe, T2, ("n1", l))
            pe.wait_ge(*vector.at("normed", ("n1", l), KD - 1))
            for c, chunk in enumerate(in_list(l)):
                w = next_weights(pe)
                for i, (c0, n, T, dst, parts) in enumerate(chunk):
                    project_tensor(pe, w, c0, n, T, ("projected", l, c, i), parts)
                chunk_read()
            join(tensor, pe, ("in", l))
            b = take(pe, "values", l)
            for j in range(4):
                last = PE.transpose(b[:, j * P:(j + 1) * P], swav[:, 0, j * P:(j + 1) * P], ident)
            last.then_inc(*tensor.mark("values", l))
            for g in range(2):
                b = take(pe, "keys", l, g)
                mm(b[:, :], C(f"dup{g}"), swak[:, 0, :], 0, 1).then_inc(*tensor.mark("keys", l, g))
                b = take(pe, "keys_rot", l, g)
                mm(b[:, 0:S], C(f"duprot{g}"), swak[:, 0, 0:S], 0, 1).then_inc(*tensor.mark("keys_rot", l, g))
            for i in range(3):
                rotate_tensor(pe, swaq[:, i, 0:S], C("rot_swa"), slice(0, P), ("rot", l, "swa", i))
            rotate_tensor(pe, krb[HI, 0, 0:S], C("rot_mla")[HI, 64:96], HI, ("rot", l, "kr"))
            for name, n, T, o in (("q", 2, TQ, 0), ("kv", 1, T2, 2)):
                pe.wait_ge(*scalar.at("squares", l, name))
                b = take(pe, "mean", l, name)
                for k in range(n):
                    last = mm(b[:, 0:T], ones, sq[:, o + k, 0:T], k, n)
                last.then_inc(*tensor.mark("mean", l, name))
            pe.wait_ge(*vector.at("latent", l, "q"))
            for i in range(H1):
                b = take(pe, "q96", l, i)
                for k in range(2):
                    last = mm(b[0:96, 0:TQ], uq[:, l, k, 96 * i:96 * i + 96], cq[:, k, 0:TQ], k, 2)
                last.then_inc(*tensor.mark("q96", l, i))
            pe.wait_ge(*vector.at("latent", l, "kv"))
            for i in range(H1):
                b = take(pe, "k96", l, i)
                mm(b[LO, :], ukv[:, l, 128 * i:128 * i + 64], ckv[:, 0, :], 0, 1).then_inc(*tensor.mark("k96", l, i))
            wv = ukv[:, l, :].rearrange("p (h a) -> p h a", a=P)[:, :, 64:128]
            for j in range(4):
                b = take(pe, "v_mla", l, j)
                mm(b[:, 0:384], ckv[:, 0, j * P:(j + 1) * P], wv, 0, 1).then_inc(*tensor.mark("v_mla", l, j))
            for i in range(H1):
                pe.wait_ge(*got("q96", l, i))
                rotate_tensor(pe, q96[0:96, i, 0:S], ROT_MLA[0], slice(0, 96), ("rot", l, "q", i))
            join(tensor, pe, ("heads", l))
            attend_tensor(pe, head_list(l, 0), prob1, probT1, ("lat", l),
                          lambda i: ada_tensor(pe, 1, i) if l == 0 and i < ADA_LATE else None)
            join(tensor, pe, ("lat_done", l))
            if l < L - 1:
                attend_tensor(pe, head_list(l, 1), prob1, probT1, ("ctx", l))
                join(tensor, pe, ("ctx_done", l))
            for i in range(2):
                w = next_weights(pe)
                for m in range(4):
                    b = take(pe, "out", l, 4 * i + m)
                    for k in range(KD):
                        last = mm(b[:, 0:TQ], w[:, k, m * P:(m + 1) * P], mix[:, k, 0:TQ], k, KD)
                    last.then_inc(*tensor.mark("out", l, 4 * i + m))
                chunk_read()
            join(tensor, pe, ("mixed", l))

        def hybrid_vector(dve, l):
            TQ = T2 if l < L - 1 else S
            NS = TQ // S
            g, sh = modulation_vector(dve, l, "norm1_g", 0, 8)
            norm_vector(dve, T2, ("n1", l), g, sh)
            lists = in_list(l)

            def outs(c):
                for i, (c0, n, T, dst, parts) in enumerate(lists[c]):
                    if i % 2:
                        src = bank("projected", l, c, i)[parts if parts else slice(0, n), 0:T]
                        out_vector(dve, dst, src, "projected", l, c, i)

            outs(0)
            outs(1)
            dve.wait_ge(*vector.now("projected"))
            dve.wait_ge(*scalar.at("projected", l, 1, 2))
            link(dve, V.memset(z, 0.0))
            for c in range(2):
                halves = [bcu[:, i + c, 0:TQ].rearrange("p (s t) -> p s t", s=NS) for i in (2, 4)]
                link(dve, V.tensor_tensor(z[:, c, 0:NS, 1:S + 1], halves[0], halves[1], ALU.mult))
                y = cv[:, c, 0:TQ].rearrange("p (s t) -> p s t", s=NS)
                link(dve, V.tensor_scalar(y, z[:, c, 0:NS, 0:S], vc("conv_w", 6 * l + c), None, ALU.mult))
                for tap in (1, 2):
                    link(dve, V.scalar_tensor_tensor(y, z[:, c, 0:NS, tap:tap + S], vc("conv_w", 6 * l + 2 * tap + c), y,
                                                     ALU.mult, ALU.add))
                link(dve, V.tensor_tensor(cv[:, c, 0:TQ], cv[:, c, 0:TQ], bcu[:, c, 0:TQ], ALU.mult))
            outs(2)
            outs(3)
            join(vector, dve, ("in", l))
            out_vector(dve, vall[:, :, 384:512], bank("values", l)[:, :].rearrange("p (j c) -> p j c", j=4), "values", l)
            for g in range(2):
                a, r = bank("keys", l, g), bank("keys_rot", l, g)
                dve.wait_ge(*tensor.at("keys", l, g))
                link(dve, V.tensor_tensor(kd[:, g, 0:S], a[:, 0:S], C("cos_swa"), ALU.mult))
                V.tensor_copy(kd[:, g, S:T2], a[:, S:T2]).then_inc(*vector.mark("keys", l, g))
                dve.wait_ge(*tensor.at("keys_rot", l, g))
                link(dve, V.tensor_tensor(r[:, 0:S], r[:, 0:S], C("sin_swa"), ALU.mult))
                V.tensor_tensor(kd[:, g, 0:S], kd[:, g, 0:S], r[:, 0:S], ALU.add).then_inc(*vector.mark("keys_rot", l, g))
            for i in range(3):
                rotate_vector(dve, swaq[:, i, 0:S], C("cos_swa"), C("sin_swa"), slice(0, P), ("rot", l, "swa", i))
            rotate_vector(dve, krb[HI, 0, 0:S], C("cos_mla")[HI, :], C("sin_mla")[HI, :], HI, ("rot", l, "kr"))
            for name, src, n, T, gname in (("q", cq, 2, TQ, "mla_q_norm_g"), ("kv", ckv, 1, T2, "mla_kv_norm_g")):
                dve.wait_ge(*tensor.at("mean", l, name))
                link(dve, V.tensor_scalar(rstd[:, 0:T], bank("mean", l, name)[:, 0:T], 1.0 / (n * P), EPS, ALU.mult, ALU.add))
                V.reciprocal(rstd[:, 0:T], rstd[:, 0:T]).then_inc(*vector.mark("mean", l, name))
                dve.wait_ge(*scalar.at("root", l, name))
                for i in range(n):
                    V.scalar_tensor_tensor(src[:, i, 0:T], src[:, i, 0:T], vc(gname, n * l + i), rstd[:, 0:T],
                                           ALU.mult, ALU.mult).then_inc(*vector.mark("latent", l, name))
                dve.wait_ge(*vector.now("latent"))
            for i in range(0, H1, 2):
                out_vector(dve, q96[0:96, i, 0:TQ], bank("q96", l, i)[0:96, 0:TQ], "q96", l, i)
            for i in range(0, H1, 2):
                out_vector(dve, k96[LO, i, :], bank("k96", l, i)[LO, :], "k96", l, i)
            for j in range(0, 4, 2):
                out_vector(dve, vall[:, j, 0:384], bank("v_mla", l, j)[:, 0:384], "v_mla", l, j)
            for i in range(H1):
                dve.wait_ge(*got("q96", l, i))
                rotate_vector(dve, q96[0:96, i, 0:S], ROT_MLA[1], ROT_MLA[2], slice(0, 96), ("rot", l, "q", i))
            join(vector, dve, ("heads", l))
            attend_vector(dve, head_list(l, 0), prob1, probT1, ("lat", l),
                          lambda i: ada_vector(dve, 1, i) if l == 0 and i < ADA_LATE else None)
            join(vector, dve, ("lat_done", l))
            if l < L - 1:
                attend_vector(dve, head_list(l, 1), prob1, probT1, ("ctx", l))
                join(vector, dve, ("ctx_done", l))
            for d in range(KD):
                dve.wait_ge(*tensor.at("out", l, d))
                for s in range(NS):
                    xs = x[:, d, s * S:(s + 1) * S]
                    V.scalar_tensor_tensor(xs, bank("out", l, d)[:, s * S:(s + 1) * S], mods[:, l, 16 + d, s:s + 1], xs,
                                           ALU.mult, ALU.add).then_inc(*vector.mark("out", l, d))
            join(vector, dve, ("mixed", l))

        def hybrid_scalar(act, l):
            TQ = T2 if l < L - 1 else S
            norm_scalar(act, T2, ("n1", l))
            for c, chunk in enumerate(in_list(l)):
                for i, (c0, n, T, dst, parts) in enumerate(chunk):
                    if i % 2 == 0:
                        src = bank("projected", l, c, i)[parts if parts else slice(0, n), 0:T]
                        out_scalar(act, dst, src, "projected", l, c, i)
            join(scalar, act, ("in", l))
            for name, src, n, T, o in (("q", cq, 2, TQ, 0), ("kv", ckv, 1, T2, 2)):
                SC.activation(sq[:, o:o + n, 0:T], src[:, :, 0:T], ACT.Square).then_inc(*scalar.mark("squares", l, name))
            for name, T in (("q", TQ), ("kv", T2)):
                act.wait_ge(*vector.at("mean", l, name))
                SC.activation(rstd[:, 0:T], rstd[:, 0:T], ACT.Sqrt).then_inc(*scalar.mark("root", l, name))
            for i in range(1, H1, 2):
                out_scalar(act, q96[0:96, i, 0:TQ], bank("q96", l, i)[0:96, 0:TQ], "q96", l, i)
            for i in range(1, H1, 2):
                out_scalar(act, k96[LO, i, :], bank("k96", l, i)[LO, :], "k96", l, i)
            for j in range(1, 4, 2):
                out_scalar(act, vall[:, j, 0:384], bank("v_mla", l, j)[:, 0:384], "v_mla", l, j)
            act.wait_ge(*vector.at("rot", l, "kr"))
            for i in range(H1):
                SC.activation(k96[HI, i, :], krb[HI, 0, :], ACT.Copy).then_inc(*scalar.mark("chain"))
            join(scalar, act, ("heads", l))
            attend_scalar(act, head_list(l, 0), prob1, probT1, ("lat", l))
            SC.activation(mix[:, 6:8, 0:TQ], cv[:, :, 0:TQ], ACT.Copy).then_inc(*scalar.mark("chain"))
            join(scalar, act, ("lat_done", l))
            if l < L - 1:
                attend_scalar(act, head_list(l, 1), prob1, probT1, ("ctx", l))
                join(scalar, act, ("ctx_done", l))
            join(scalar, act, ("mixed", l))

        xg = arena[:, 0:8192].rearrange("p (k e c) -> p k e c", k=KD, e=NE)
        htok = arena[:, 8192:12288].rearrange("p (j d) -> p j d", j=4)
        sel = arena[:, 12288:14336].rearrange("p (s j e c) -> p s j e c", s=2, j=2, e=NE)
        aff = arena[:, 14336:14400].rearrange("p (j s e) -> p j s e", j=2, s=2)
        posT = arena[:, 14400:14464].rearrange("p (j s e) -> p j s e", j=2, s=2)
        affT, work, pos = (arena[0:32, 14464 + 256 * i:14720 + 256 * i] for i in range(3))
        m8 = arena[0:32, 15232:15240]
        scat = h[:, 0:4, :].rearrange("p a b -> p (a b)").rearrange("p (s g t) -> p s g t", s=2, g=4)
        yst = arena[:, 8192:16384].rearrange("p (s g d) -> p s g d", s=2, g=4)
        hid1 = h[:, 4:5, :].rearrange("p a b -> p (a b)").rearrange("p (i f c) -> p i f c", i=2, f=4)
        GB, UB, YB = (0, 4), (1, 5), ((2, 3), (6, 7))
        gate_made, up_made, half_made = sem("gate_made"), sem("up_made"), sem("half_made")
        silu_done, hid_done = sem("silu_done"), sem("hid_done")
        half_out = sem("half_out_scalar"), sem("half_out_vector")

        def moe_tensor(pe, l):
            NS = 2 if l < L - 1 else 1
            T, CS = NS * S, NS * CAP
            norm_tensor(pe, T, ("n2", l))
            pe.wait_ge(*vector.at("normed", ("n2", l), KD - 1))
            b = take(pe, "router", l)
            for s in range(NS):
                for j in range(2):
                    o = 32 * j + 16 * s
                    for k in range(KD):
                        last = mm(b[:, o:o + 16], h[:, k, s * S + j * P:s * S + j * P + P], rtr[:, l, k, :], k, KD)
            last.then_inc(*tensor.mark("router", l))
            for j in range(2 * NS):
                for half in range(2):
                    b = take(pe, "htok", l, j, half)
                    for k in range(4):
                        last = PE.transpose(b[:, k * P:(k + 1) * P], h[:, 4 * half + k, j * P:(j + 1) * P], ident)
                    last.then_inc(*tensor.mark("htok", l, j, half))
            pe.wait_ge(*vector.at("aff", l))
            b = take(pe, "affT", l)
            for j in range(2):
                last = PE.transpose(b[0:32, j * P:(j + 1) * P], aff[:, j].rearrange("p s e -> p (s e)"), ident)
            last.then_inc(*tensor.mark("affT", l))
            pe.wait_ge(*vector.at("pos", l))
            b = take(pe, "posT", l)
            for j in range(2):
                last = PE.transpose(b[:, j * 32:(j + 1) * 32], pos[:, j * P:(j + 1) * P], ident[0:32, 0:32])
            last.then_inc(*tensor.mark("posT", l))
            pe.wait_ge(*scalar.at("htok", l, 2 * NS - 1, 1))
            for s in range(NS):
                pe.wait_ge(*vector.at("sel", l, s, 1))
                for k in range(KD):
                    b = take(pe, "xg", l, s, k)
                    for j in range(2):
                        last = mm(b[:, :], htok[:, 2 * s + j, k * P:(k + 1) * P], sel[:, s, j].rearrange("p e c -> p (e c)"), j, 2)
                    last.then_inc(*tensor.mark("xg", l, s, k))
            for s in range(NS):
                for g in range(4):
                    sp = C("spread")[0:32, (4 * s + g) * P:(4 * s + g + 1) * P]
                    b = take(pe, "slot_of", l, s, g)
                    mm(b[:, 0:S], sp, pos, 0, 1).then_inc(*tensor.mark("slot_of", l, s, g))
                    b = take(pe, "weight_of", l, s, g)
                    mm(b[:, 0:S], sp, affT, 0, 1).then_inc(*tensor.mark("weight_of", l, s, g))
            join(tensor, pe, ("gathered", l))
            n0 = expert_chunk[l]
            assert at[0] == n0
            with pe.Fori(0, NE // 4) as g:
                for q in range(4):
                    e = NE * l + q
                    for c, (B, made) in enumerate(((GB, gate_made), (UB, up_made))):
                        n = n0 + 3 * q + c
                        pe.wait_ge(loaded[n % RING], 16 * (n // RING + 1) + (16 * 12 // RING) * g)
                        if c == 0:
                            pe.wait_ge(hid_done, max(e - 1, 0) + 4 * g)
                        for f in range(4):
                            for k in range(KD):
                                last = mm(banks[B[q % 2]][:, 64 * f:64 * f + CS], slot(n)[:, k, f * P:(f + 1) * P],
                                          xg[:, k, bass.ds(4 * g + q, 1), 0:CS].rearrange("p e c -> p (e c)"), k, KD)
                        last.then_inc(made, 1)
                    n = n0 + 3 * q + 2
                    pe.wait_ge(loaded[n % RING], 16 * (n // RING + 1) + (16 * 12 // RING) * g)
                    pe.wait_ge(hid_done, e + 1 + 4 * g)
                    for half in range(2):
                        pe.wait_ge(half_out[half], max(e - 1, 0) + 4 * g)
                        for f in range(4):
                            last = mm(banks[YB[q % 2][half]][0:CS, :], hid1[:, q % 2, f, 0:CS], slot(n)[:, f, half * 512:(half + 1) * 512], f, 4)
                        last.then_inc(half_made, 1)
            at[0] += 3 * NE
            for i in range(2):
                pe.wait_ge(half_out[i], NE * (l + 1))
            for b in range(8):
                holder[b] = None
            for s in range(NS):
                for d in range(KD):
                    b = take(pe, "scattered", l, s, d)
                    for g in range(4):
                        last = mm(b[:, 0:S], yst[:, s, g, d * P:(d + 1) * P], scat[:, s, g, :], g, 4)
                    last.then_inc(*tensor.mark("scattered", l, s, d))
            join(tensor, pe, ("moe", l))

        def moe_vector(dve, l):
            NS = 2 if l < L - 1 else 1
            CS = NS * CAP
            g, sh = modulation_vector(dve, l, "norm2_g", 24, 32)
            norm_vector(dve, NS * S, ("n2", l), g, sh)
            if NS == 1:
                link(dve, V.memset(aff, 0.0))
            dve.wait_ge(*tensor.at("router", l))
            lg = bank("router", l)[:, 0:64].rearrange("p (j s e) -> p j s e", j=2, s=2)
            mx = stat[:, 32:36].rearrange("p (j s) -> p j s", j=2)
            for s in range(NS):
                a = aff[:, :, s, :]
                link(dve, V.tensor_reduce(mx[:, :, s:s + 1], lg[:, :, s, :], AX, ALU.max))
                V.tensor_tensor(a, lg[:, :, s, :], mx[:, :, s:s + 1].broadcast_to((P, 2, NE)), ALU.subtract)\
                 .then_inc(*vector.mark("router", l))
                book.new[("vector", "shifted", l, s)] = vector.n["router"]
            for s in range(NS):
                a = aff[:, :, s, :]
                dve.wait_ge(*scalar.at("aff_exp", l, s))
                link(dve, V.tensor_reduce(mx[:, :, s:s + 1], a, AX, ALU.add))
                link(dve, V.reciprocal(mx[:, :, s:s + 1], mx[:, :, s:s + 1]))
                V.tensor_tensor(a, a, mx[:, :, s:s + 1].broadcast_to((P, 2, NE)), ALU.mult).then_inc(*vector.mark("aff", l))
            dve.wait_ge(*tensor.at("affT", l))
            V.tensor_copy(affT, bank("affT", l)[0:32, 0:S]).then_inc(*vector.mark("chain"))
            V.tensor_copy(work, bank("affT", l)[0:32, 0:S]).then_inc(*vector.mark("affT", l))
            dve.wait_ge(*vector.now("affT"))
            for r in range(CAP // 8):
                link(dve, V.max(m8, work))
                link(dve, V.match_replace(work, m8, work, -1.0))
            link(dve, V.tensor_scalar(work, work, 0.0, None, ALU.is_lt))
            link(dve, V.tensor_tensor_scan(pos, ones[0:32, 0:1].broadcast_to((32, S)), work, 0.0, ALU.mult, ALU.add))
            V.tensor_tensor(pos, pos, work, ALU.mult).then_inc(*vector.mark("pos", l))
            out_vector(dve, posT.rearrange("p j s e -> p (j s e)"), bank("posT", l)[:, 0:64], "posT", l)
            dve.wait_ge(*vector.now("posT"))
            for s in range(NS):
                for j in range(2):
                    V.tensor_tensor(sel[:, s, j], posT[:, j, s, :].unsqueeze(2).broadcast_to((P, NE, CAP)),
                                    C("slots").unsqueeze(1).broadcast_to((P, NE, CAP)), ALU.is_equal)\
                     .then_inc(*vector.mark("sel", l, s, j))
            for s in range(NS):
                for k in range(0, KD, 2):
                    out_vector(dve, xg[:, k, :, s * CAP:(s + 1) * CAP],
                               bank("xg", l, s, k)[:, :].rearrange("p (e c) -> p e c", e=NE), "xg", l, s, k)
            dve.wait_ge(*tensor.at("xg", l, NS - 1, KD - 1))
            for s in range(NS):
                for gr in range(4):
                    o = scat[:, s, gr, :]
                    dve.wait_ge(*tensor.at("slot_of", l, s, gr))
                    V.tensor_scalar(o, bank("slot_of", l, s, gr)[:, 0:S], C("slot"), None, ALU.is_equal)\
                     .then_inc(*vector.mark("slot_of", l, s, gr))
                    dve.wait_ge(*vector.now("slot_of"))
                    dve.wait_ge(*tensor.at("weight_of", l, s, gr))
                    V.tensor_tensor(o, o, bank("weight_of", l, s, gr)[:, 0:S], ALU.mult).then_inc(*vector.mark("weight_of", l, s, gr))
            join(vector, dve, ("gathered", l))
            with dve.Fori(0, NE // 4) as g:
                for q in range(4):
                    e = NE * l + q
                    hd = hid1[:, q % 2, :, 0:CS]
                    uv = banks[UB[q % 2]][:, 0:256].rearrange("p (f c) -> p f c", f=4)[:, :, 0:CS]
                    dve.wait_ge(silu_done, e + 1 + 4 * g)
                    dve.wait_ge(up_made, e + 1 + 4 * g)
                    V.tensor_tensor(hd, hd, uv, ALU.mult).then_inc(hid_done, 1)
                    dve.wait_ge(half_made, 2 * e + 2 + 8 * g)
                    for s in range(NS):
                        ins = V.tensor_copy(yst[32 * q:32 * q + 32, s, bass.ds(g, 1), 512:1024].rearrange("p g d -> p (g d)"),
                                            banks[YB[q % 2][1]][s * CAP:(s + 1) * CAP, :])
                    ins.then_inc(half_out[1], 1)
            for s in range(NS):
                for d in range(KD):
                    dve.wait_ge(*tensor.at("scattered", l, s, d))
                    xs = x[:, d, s * S:(s + 1) * S]
                    V.scalar_tensor_tensor(xs, bank("scattered", l, s, d)[:, 0:S], mods[:, l, 40 + d, s:s + 1], xs,
                                           ALU.mult, ALU.add).then_inc(*vector.mark("scattered", l, s, d))
            join(vector, dve, ("moe", l))

        def moe_scalar(act, l):
            NS = 2 if l < L - 1 else 1
            CS = NS * CAP
            norm_scalar(act, NS * S, ("n2", l))
            for s in range(NS):
                a = aff[:, :, s, :]
                act.wait_ge(vector.sem("router"), book.old.get(("vector", "shifted", l, s), 1))
                SC.activation(a, a, ACT.Exp).then_inc(*scalar.mark("aff_exp", l, s))
            for j in range(2 * NS):
                for half in range(2):
                    out_scalar(act, htok[:, j, half * 512:(half + 1) * 512], bank("htok", l, j, half)[:, :], "htok", l, j, half)
            for s in range(NS):
                for k in range(1, KD, 2):
                    out_scalar(act, xg[:, k, :, s * CAP:(s + 1) * CAP],
                               bank("xg", l, s, k)[:, :].rearrange("p (e c) -> p e c", e=NE), "xg", l, s, k)
            join(scalar, act, ("gathered", l))
            with act.Fori(0, NE // 4) as g:
                for q in range(4):
                    e = NE * l + q
                    act.wait_ge(gate_made, e + 1 + 4 * g)
                    act.wait_ge(half_made, max(2 * e - 2, 0) + 8 * g)
                    gv = banks[GB[q % 2]][:, 0:256].rearrange("p (f c) -> p f c", f=4)[:, :, 0:CS]
                    SC.activation(hid1[:, q % 2, :, 0:CS], gv, ACT.Silu).then_inc(silu_done, 1)
                    act.wait_ge(half_made, 2 * e + 1 + 8 * g)
                    for s in range(NS):
                        ins = SC.activation(yst[32 * q:32 * q + 32, s, bass.ds(g, 1), 0:512].rearrange("p g d -> p (g d)"),
                                            banks[YB[q % 2][0]][s * CAP:(s + 1) * CAP, :], ACT.Copy)
                    ins.then_inc(half_out[0], 1)
            join(scalar, act, ("moe", l))

        o = 0

        def place(n):
            nonlocal o
            a = arena[:, o:o + n]
            o += n
            return a

        def chan():
            return place(512).rearrange("p (c t) -> p c t", c=2)

        gates = place(4096).rearrange("p (n t) -> p n t", n=16)
        ys = [chan() for _ in range(4)]
        raw_r = place(2056).rearrange("p (n t) -> p n t", n=8)
        raw_h = place(2048).rearrange("p (n t) -> p n t", n=8)
        pool0 = o
        raw_s = place(1536).rearrange("p (n t) -> p n t", n=6)
        raw_m = place(1536).rearrange("p (n t) -> p n t", n=6)
        vt_s, vt_m = chan(), chan()
        Zs, Es = place(2048), place(2048)
        prob_m = [place(512).rearrange("p (j n) -> p j n", j=2) for _ in range(2)]
        probT_m = [place(512).rearrange("p (k q) -> p k q", k=2) for _ in range(2)]
        assert o <= AR, (o, AR)
        o = pool0
        NT, AkT, RbT, RkT, Tm, TT, Xm = (place(1024) for _ in range(7))
        sc_d, sc_x = place(1024), place(512)
        assert o <= AR, (o, AR)
        x_hi = [x[:, k, S:T2] for k in range(KD)]

        def wide(t, k):
            return t[:, k:k + 2, S:T2]

        def sl_of(hd):
            return slice(64 * (hd % 2), 64 * (hd % 2) + 64)

        def turn_tensor(pe, src, *key):
            b = take(pe, *key)
            for j in range(2):
                for c in range(2):
                    last = PE.transpose(b[:, j * S + c * P:j * S + (c + 1) * P], src[:, c, j * P:(j + 1) * P], ident)
            last.then_inc(*tensor.mark(*key))

        def halves(b):
            return b[:, :].rearrange("p (j c) -> p j c", j=2)

        def head_sum_tensor(pe, src, *key):
            b = take(pe, *key)
            mm(b[:, :], C("heads"), src, 0, 1).then_inc(*tensor.mark(*key))

        sq_, sk_, sv_ = raw_s[:, 0:2, :], raw_s[:, 2:4, :], raw_s[:, 4:6, :]
        Z4, E4 = (t.rearrange("p (h s t) -> p h s t", h=4, s=2) for t in (Zs, Es))
        Z2, E2 = (t.rearrange("p (h x) -> p h x", h=4) for t in (Zs, Es))

        def stick_tensor(pe, l):
            for hd in range(4):
                b = take(pe, "stick_z", l, hd)
                for st in range(2):
                    last = mm(b[:, st * S:(st + 1) * S], sk_[sl_of(hd), hd // 2, st * P:(st + 1) * P], sq_[sl_of(hd), hd // 2, :], 0, 1)
                last.then_inc(*tensor.mark("stick_z", l, hd))
            turn_tensor(pe, sv_, "stick_v", l)
            yield
            pe.wait_ge(*vector.at("stick_keep", l))
            for hd in range(4):
                b = take(pe, "stick_sum", l, hd)
                mm(b[:, 0:S], C("suffix"), E4[:, hd, 0, :], 0, 2)
                mm(b[:, 0:S], ones, E4[:, hd, 1, :], 1, 2)
                mm(b[:, S:T2], C("suffix"), E4[:, hd, 1, :], 0, 1).then_inc(*tensor.mark("stick_sum", l, hd))
            yield
            pe.wait_ge(*scalar.at("stick_att", l))
            pe.wait_ge(*got("stick_v", l))
            b = take(pe, "stick_y", l)
            for hd in range(4):
                for st in range(2):
                    last = mm(b[sl_of(hd), (hd // 2) * S:(hd // 2 + 1) * S], vt_s[:, st, 64 * hd:64 * hd + 64], Z4[:, hd, st, :], st, 2)
            last.then_inc(*tensor.mark("stick_y", l))
            yield

        def stick_vector(dve, l):
            out_vector(dve, vt_s, halves(bank("stick_v", l)), "stick_v", l)
            dve.wait_ge(*scalar.at("stick_z", l, 3))
            V.scalar_tensor_tensor(Es, Zs, -1.0, Zs, ALU.mult, ALU.max).then_inc(*vector.mark("stick_abs", l))
            yield
            dve.wait_ge(*scalar.at("stick_log", l))
            link(dve, V.scalar_tensor_tensor(Es, Zs, 0.0, Es, ALU.max, ALU.add))
            V.tensor_tensor(E2, E2, C("stick").unsqueeze(1).broadcast_to((P, 4, 512)), ALU.mult).then_inc(*vector.mark("stick_keep", l))
            link(dve, V.tensor_tensor(Z2, Z2, C("stick_add").unsqueeze(1).broadcast_to((P, 4, 512)), ALU.add))
            for hd in range(4):
                dve.wait_ge(*tensor.at("stick_sum", l, hd))
                V.tensor_tensor(Z2[:, hd], Z2[:, hd], bank("stick_sum", l, hd)[:, :], ALU.add).then_inc(*vector.mark("stick_sum", l, hd))
            yield
            out_vector(dve, flat(ys[0]), bank("stick_y", l)[:, :], "stick_y", l)
            yield

        def stick_scalar(act, l):
            for hd in range(4):
                out_scalar(act, Zs[:, hd * 512:(hd + 1) * 512], bank("stick_z", l, hd)[:, :], "stick_z", l, hd, scale=HEAD_SCALE)
            act.wait_ge(*vector.at("stick_abs", l))
            link_s(act, SC.activation(Es, Es, ACT.Exp, scale=-1.0))
            SC.activation(Es, Es, ACT.Ln, bias=1.0).then_inc(*scalar.mark("stick_log", l))
            yield
            act.wait_ge(*vector.at("stick_sum", l, 3))
            SC.activation(Zs, Zs, ACT.Exp).then_inc(*scalar.mark("stick_att", l))
            yield
            yield

        def moba_heads():
            causal = C("causal").rearrange("p (a t) -> p a t", a=2)
            heads = []
            for hd in range(4):
                parts, c = sl_of(hd), hd // 2
                heads.append((lambda j, parts=parts, c=c: raw_m[parts, c, j * P:(j + 1) * P], raw_m[parts, 2 + c, :], S,
                              lambda k, hd=hd: vt_m[:, k, 64 * hd:64 * hd + 64], parts, ys[2][parts, c, :],
                              causal, C("no_sink"), HEAD_SCALE))
            return heads

        def moba_tensor(pe, l, fill):
            turn_tensor(pe, raw_m[:, 4:6, :], "moba_v", l)
            for i in range(4):
                rotate_tensor(pe, raw_m[:, i, :], C("rot_moba"), slice(0, P), ("moba_rot", l, i))
            yield
            pe.wait_ge(*vector.at("moba_rot", l, 3))
            pe.wait_ge(*got("moba_v", l))
            attend_tensor(pe, moba_heads(), prob_m, probT_m, ("moba", l), lambda i: next(fill, None))
            yield
            yield

        def moba_vector(dve, l):
            for i in range(4):
                rotate_vector(dve, raw_m[:, i, :], C("cos_moba"), C("sin_moba"), slice(0, P), ("moba_rot", l, i))
            yield
            attend_vector(dve, moba_heads(), prob_m, probT_m, ("moba", l))
            yield
            yield

        def moba_scalar(act, l, fill):
            out_scalar(act, vt_m, halves(bank("moba_v", l)), "moba_v", l)
            yield
            attend_scalar(act, moba_heads(), prob_m, probT_m, ("moba", l), lambda i: next(fill, None))
            yield
            yield

        hq, hf, hi_, hg = (raw_h[:, 2 * n:2 * n + 2, :] for n in range(4))
        key_h, B_h, D_h, qd, kdc, vt_h = (wide(h, 0), wide(h, 2), wide(h, 4), wide(h, 6), wide(x, 0), wide(x, 2))
        one_m, lb = stat[:, 20:22], stat[:, 22:24]

        def blocks(t, n):
            return t.rearrange("p c (a n) -> p c a n", n=n)

        def hgrn_scores_tensor(pe, l, lev, a, bq):
            for par in range(2):
                sl = slice(64 * par, 64 * par + 64)
                b = take(pe, "hgrn_scores", l, lev, par)
                for c in range(2):
                    for j in range(2):
                        o_ = (2 * c + j) * P
                        last = mm(b[:, o_:o_ + P], a[sl, c, j * P:(j + 1) * P], bq[sl, c, j * P:(j + 1) * P], 0, 1)
                last.then_inc(*tensor.mark("hgrn_scores", l, lev, par))

        def hgrn_scores_vector(dve, l, lev, mask):
            for par in range(2):
                dve.wait_ge(*tensor.at("hgrn_scores", l, lev, par))
                dst = sc_d[:, par * 512:(par + 1) * 512].rearrange("p (u t) -> p u t", u=4)
                src = bank("hgrn_scores", l, lev, par)[:, :].rearrange("p (u t) -> p u t", u=4)
                m = mask.unsqueeze(1).broadcast_to((P, 4, P))
                if lev < 0:
                    V.tensor_tensor(dst, src, m, ALU.mult).then_inc(*vector.mark("hgrn_scores", l, lev, par))
                else:
                    V.copy_predicated(dst, m.bitcast(U32), src).then_inc(*vector.mark("hgrn_scores", l, lev, par))
            dve.wait_ge(*vector.now("hgrn_scores"))

        def hgrn_tensor(pe, l):
            turn_tensor(pe, hi_, "hgrn_v", l)
            pe.wait_ge(*vector.at("hgrn_key", l))
            hgrn_scores_tensor(pe, l, -1, key_h, hq)
            yield
            for lev in range(LEVELS + 1):
                pe.wait_ge(*vector.at("hgrn_decayed", l, lev))
                if lev < LEVELS:
                    hgrn_scores_tensor(pe, l, lev, kdc, qd)
                else:
                    for par in range(2):
                        sl = slice(64 * par, 64 * par + 64)
                        b = take(pe, "hgrn_cross", l, par)
                        for c in range(2):
                            last = mm(b[:, c * P:(c + 1) * P], kdc[sl, c, 0:P], qd[sl, c, P:S], 0, 1)
                        last.then_inc(*tensor.mark("hgrn_cross", l, par))
                yield
            pe.wait_ge(*scalar.at("hgrn_cross", l, 1))
            pe.wait_ge(*vector.at("hgrn_scores", l, LEVELS - 1, 1))
            pe.wait_ge(*got("hgrn_v", l))
            b = take(pe, "hgrn_y", l)
            for hd in range(4):
                par, c = hd % 2, hd // 2
                o_, d0 = c * S, par * 512 + 2 * c * P
                hs = slice(64 * hd, 64 * hd + 64)
                mm(b[sl_of(hd), o_:o_ + P], vt_h[:, 0, hs], sc_d[:, d0:d0 + P], 0, 1)
                mm(b[sl_of(hd), o_ + P:o_ + S], vt_h[:, 0, hs], sc_x[:, par * S + c * P:par * S + (c + 1) * P], 0, 2)
                last = mm(b[sl_of(hd), o_ + P:o_ + S], vt_h[:, 1, hs], sc_d[:, d0 + P:d0 + 2 * P], 1, 2)
            last.then_inc(*tensor.mark("hgrn_y", l))
            yield
            pe.wait_ge(*scalar.at("hgrn_sq", l))
            head_sum_tensor(pe, kdc, "hgrn_sum", l)
            yield

        def hgrn_vector(dve, l):
            if l == 0:
                V.memset(lb, 0.0).then_inc(*vector.mark("chain"))
                link(dve, V.memset(one_m, 1.0))
            else:
                e0, e1, top = stat[:, 24:26], stat[:, 26:28], stat[:, 28:30]
                l0, l1 = vc("hgrn_lb_logits_2", 0, 2), vc("hgrn_lb_logits_2", 2, 2)
                link(dve, V.tensor_tensor(top, l0, l1, ALU.max))
                V.tensor_tensor(e0, l0, top, ALU.subtract).then_inc(*vector.mark("chain"))
                V.tensor_tensor(e1, l1, top, ALU.subtract).then_inc(*vector.mark("hgrn_lb", l))
                dve.wait_ge(*scalar.at("hgrn_lb", l))
                link(dve, V.tensor_tensor(top, e0, e1, ALU.add))
                link(dve, V.reciprocal(top, top))
                link(dve, V.tensor_tensor(lb, e1, top, ALU.mult))
                link(dve, V.tensor_scalar(one_m, lb, -1.0, 1.0, ALU.mult, ALU.add))
            out_vector(dve, vt_h, halves(bank("hgrn_v", l)), "hgrn_v", l)
            dve.wait_ge(*scalar.at("hgrn_sig", l))
            for c in range(2):
                V.tensor_scalar(key_h[:, c, :], key_h[:, c, :], one_m[:, c:c + 1], None, ALU.mult).then_inc(*vector.mark("hgrn_key", l))
            for c in range(2):
                V.tensor_scalar(B_h[:, c, :], B_h[:, c, :], one_m[:, c:c + 1], lb[:, c:c + 1], ALU.mult, ALU.add)\
                 .then_inc(*vector.mark("hgrn_forget", l))
            hgrn_scores_vector(dve, l, -1, ident)
            dve.wait_ge(*scalar.at("hgrn_log", l))
            for c in range(2):
                V.tensor_tensor_scan(B_h[:, c, :], ones[:, 0:1].broadcast_to((P, S)), D_h[:, c, :], 0.0, ALU.mult, ALU.add).then_inc(*vector.mark("chain"))
            dve.wait_ge(*vector.now("chain"))
            yield
            for lev in range(LEVELS + 1):
                n = 2 ** (lev + 1)
                half = n // 2
                if lev:
                    dve.wait_ge(*vector.at("hgrn_decayed", l, lev - 1))
                for c in range(2):
                    Bp, Dp = B_h[:, c, :].rearrange("p (a n) -> p a n", n=n), D_h[:, c, :].rearrange("p (a n) -> p a n", n=n)
                    V.tensor_tensor(Dp, Bp, Bp[:, :, half - 1:half].broadcast_to((P, S // n, n)), ALU.subtract)\
                     .then_inc(*vector.mark("chain"))
                dve.wait_ge(*vector.now("chain"))
                V.scalar_tensor_tensor(D_h, D_h, -1.0, D_h, ALU.mult, ALU.min).then_inc(*vector.mark("hgrn_decay", l, lev))
                if lev:
                    hgrn_scores_vector(dve, l, lev - 1, C("levels")[:, (lev - 1) * P:lev * P])
                dve.wait_ge(*scalar.at("hgrn_decay", l, lev))
                V.tensor_tensor(qd, hq, D_h, ALU.mult).then_inc(*vector.mark("chain"))
                V.tensor_tensor(kdc, key_h, D_h, ALU.mult).then_inc(*vector.mark("hgrn_decayed", l, lev))
                yield
            yield
            dve.wait_ge(*tensor.at("hgrn_sum", l))
            link(dve, V.tensor_scalar(D_h, halves(bank("hgrn_sum", l)), 1.0 / 64, EPS, ALU.mult, ALU.add))
            V.reciprocal(D_h, D_h).then_inc(*vector.mark("hgrn_sum", l))
            dve.wait_ge(*scalar.at("hgrn_silu", l))
            link(dve, V.tensor_tensor(qd, qd, D_h, ALU.mult))
            for c in range(2):
                V.scalar_tensor_tensor(ys[3][:, c, :], qd[:, c, :], vc("hgrn_gn_g_2", 2 * l + c), key_h[:, c, :], ALU.mult, ALU.mult)\
                 .then_inc(*vector.mark("chain"))
            yield

        def hgrn_scalar(act, l):
            SC.activation(key_h, hf, ACT.Sigmoid, scale=-1.0).then_inc(*scalar.mark("chain"))
            SC.activation(B_h, hf, ACT.Sigmoid).then_inc(*scalar.mark("hgrn_sig", l))
            if l:
                act.wait_ge(*vector.at("hgrn_lb", l))
                SC.activation(stat[:, 24:28], stat[:, 24:28], ACT.Exp).then_inc(*scalar.mark("hgrn_lb", l))
            act.wait_ge(*vector.at("hgrn_forget", l))
            SC.activation(D_h, B_h, ACT.Ln).then_inc(*scalar.mark("hgrn_log", l))
            yield
            for lev in range(LEVELS + 1):
                act.wait_ge(*vector.at("hgrn_decay", l, lev))
                SC.activation(D_h, D_h, ACT.Exp).then_inc(*scalar.mark("hgrn_decay", l, lev))
                if lev == LEVELS:
                    for par in range(2):
                        out_scalar(act, sc_x[:, par * S:(par + 1) * S], bank("hgrn_cross", l, par)[:, 0:S], "hgrn_cross", l, par)
                yield
            out_scalar(act, qd, halves(bank("hgrn_y", l)), "hgrn_y", l)
            act.wait_ge(*scalar.now("hgrn_y"))
            SC.activation(kdc, qd, ACT.Square).then_inc(*scalar.mark("hgrn_sq", l))
            yield
            act.wait_ge(*vector.at("hgrn_sum", l))
            SC.activation(D_h, D_h, ACT.Sqrt).then_inc(*scalar.mark("chain"))
            SC.activation(key_h, hg, ACT.Silu).then_inc(*scalar.mark("hgrn_silu", l))
            yield

        pr_ = raw_r[:, :, 1:S + 1]
        r_, k_, v_ = pr_[:, 0:2, :], pr_[:, 2:4, :], pr_[:, 4:6, :]

        def rwkv_buffers():
            names = ("ld", "av", "gv", "kk", "B", "rt", "at", "bt", "kt")
            return dict(zip(names, BUF9))

        LORA = (("ld", "wa2", 6, slice(0, 64), "rwkv_w0_2"), ("av", "wa2", 6, slice(64, 128), "rwkv_a0_2"), ("gv", "g2w", 7, slice(0, 128), None))

        def pairs(Bf):
            return (("NT", NT, "bt", "at", "before"), ("AkT", AkT, "kt", "at", "before"), ("RbT", RbT, "bt", "rt", "upto"), ("RkT", RkT, "kt", "rt", "upto"))

        def rwkv_tensor(pe, l):
            W = rwkv_buffers()
            yield
            pe.wait_ge(*scalar.at("lora_in", l))
            pe.wait_ge(*vector.at("shifted_r", l, 7))
            for dst, w_, src, sl, bias in LORA:
                wt = wa2 if w_ == "wa2" else g2w
                b = take(pe, "lora", l, dst)
                for c in range(2):
                    last = mm(b[:, c * S:(c + 1) * S], wt[sl, l, c * P:(c + 1) * P], pr_[sl, src, :], 0, 1)
                last.then_inc(*tensor.mark("lora", l, dst))
            if l:
                b = take(pe, "vmix1", l)
                for c in range(2):
                    last = mm(b[0:32, 0:S], v1w[:, c, :], v_[:, c, :], c, 2)
                last.then_inc(*tensor.mark("vmix1", l))
                pe.wait_ge(*scalar.at("vmix1", l))
                b = take(pe, "vmix2", l)
                for c in range(2):
                    last = mm(b[:, c * S:(c + 1) * S], v2w[0:32, c * P:(c + 1) * P], W["kt"][0:32, 0, :], 0, 1)
                last.then_inc(*tensor.mark("vmix2", l))
            yield
            pe.wait_ge(*scalar.at("kk_sq", l))
            head_sum_tensor(pe, W["rt"], "kk_sum", l)
            yield
            pe.wait_ge(*vector.at("rk", l))
            head_sum_tensor(pe, W["av"], "bonus", l)
            yield
            pe.wait_ge(*vector.at("rwkv_v", l))
            turn_tensor(pe, v_, "rwkv_vt", l)
            pe.wait_ge(*vector.at("decayed", l))
            for name, dst, a, bq, m in pairs(W):
                for par in range(2):
                    sl = slice(64 * par, 64 * par + 64)
                    b = take(pe, "pairs", l, name, par)
                    for c in range(2):
                        for j in range(2):
                            o_ = (2 * c + j) * P
                            last = mm(b[:, o_:o_ + P], W[a][sl, c, j * P:(j + 1) * P], W[bq][sl, c, j * P:(j + 1) * P], 0, 1)
                    last.then_inc(*tensor.mark("pairs", l, name, par))
            yield
            pe.wait_ge(*vector.at("moved", l))
            bx, kx = W["kk"][:, :, 0:P], W["kk"][:, :, P:S]
            for n, (a, bq) in enumerate(((bx, "at"), (kx, "at"), (bx, "rt"), (kx, "rt"))):
                for par in range(2):
                    sl = slice(64 * par, 64 * par + 64)
                    b = take(pe, "cross", l, n, par)
                    for c in range(2):
                        last = mm(b[:, c * P:(c + 1) * P], a[sl, c, :], W[bq][sl, c, P:S], 0, 1)
                    last.then_inc(*tensor.mark("cross", l, n, par))
            yield
            for lev in range(LEVELS):
                pe.wait_ge(*vector.at("level", l, lev))
                for par in range(2):
                    b = take(pe, "NT_T", l, lev, par)
                    for u in range(4):
                        o_ = par * 512 + u * P
                        last = mm(b[:, u * P:(u + 1) * P], NL[par][:, u * P:(u + 1) * P], Tm[:, o_:o_ + P], 0, 1)
                    last.then_inc(*tensor.mark("NT_T", l, lev, par))
                yield
                for par in range(2):
                    pe.wait_ge(*got("NT_T", l, lev, par))
                    b = take(pe, "dT", l, lev, par)
                    for u in range(4):
                        o_ = par * 512 + u * P
                        last = mm(b[:, u * P:(u + 1) * P], TT[:, o_:o_ + P], Xm[:, o_:o_ + P], 0, 1)
                    last.then_inc(*tensor.mark("dT", l, lev, par))
                    b = take(pe, "dTT", l, lev, par)
                    for u in range(4):
                        o_ = par * 512 + u * P
                        last = mm(b[:, u * P:(u + 1) * P], Xm[:, o_:o_ + P], TT[:, o_:o_ + P], 0, 1)
                    last.then_inc(*tensor.mark("dTT", l, lev, par))
                yield
            pe.wait_ge(*vector.at("dTT", l, LEVELS - 1, 1))
            pe.wait_ge(*scalar.at("rwkv_vt", l))
            pe.wait_ge(*scalar.at("cross", l, 3, 1))
            vt = W["B"]
            for j in range(2):
                b = take(pe, "W", l, j)
                for hd in range(4):
                    hs = slice(64 * hd, 64 * hd + 64)
                    n = 1 + 2 * j
                    last = mm(b[:, hs], unit(AkT, hd, j), vt[:, j, hs], 0, n)
                    if j == 1:
                        mm(b[:, hs], cross_of(1, hd), vt[:, 0, hs], 1, n)
                        last = mm(b[:, hs], cross_of(0, hd), SA[:, 0, hs], 2, n)
                last.then_inc(*tensor.mark("W", l, j))
                pe.wait_ge(*scalar.at("W", l, j))
                b = take(pe, "SA", l, j)
                for hd in range(4):
                    hs = slice(64 * hd, 64 * hd + 64)
                    last = mm(b[:, hs], unit(TT, hd, j), Wm[:, j, hs], 0, 1)
                last.then_inc(*tensor.mark("SA", l, j))
                pe.wait_ge(*scalar.at("SA", l, j))
                yield
            b = take(pe, "rwkv_y", l)
            for hd in range(4):
                hs = slice(64 * hd, 64 * hd + 64)
                o_ = (hd // 2) * S
                ps = b[sl_of(hd), o_:o_ + P]
                mm(ps, SA[:, 0, hs], unit(RbT, hd, 0), 0, 2)
                mm(ps, vt[:, 0, hs], unit(RkT, hd, 0), 1, 2)
                ps = b[sl_of(hd), o_ + P:o_ + S]
                mm(ps, SA[:, 0, hs], cross_of(2, hd), 0, 4)
                mm(ps, vt[:, 0, hs], cross_of(3, hd), 1, 4)
                mm(ps, SA[:, 1, hs], unit(RbT, hd, 1), 2, 4)
                last = mm(ps, vt[:, 1, hs], unit(RkT, hd, 1), 3, 4)
            last.then_inc(*tensor.mark("rwkv_y", l))
            pe.wait_ge(*scalar.at("rwkv_y", l))
            head_sum_tensor(pe, W["rt"], "gn_mean", l)
            yield
            pe.wait_ge(*scalar.at("gn_sq", l))
            head_sum_tensor(pe, W["kt"], "gn_var", l)
            yield

        def unit(M, hd, j):
            o_ = (hd % 2) * 512 + (2 * (hd // 2) + j) * P
            return M[:, o_:o_ + P]

        def rwkv_vector(dve, l):
            W = rwkv_buffers()
            ld, av, gv, kk, Bc, rt, at_, bt, kt = (W[n] for n in ("ld", "av", "gv", "kk", "B", "rt", "at", "bt", "kt"))
            d = arena[:, pool0:pool0 + 2048].rearrange("p (n t) -> p n t", n=8)
            link(dve, V.tensor_tensor(d, raw_r[:, :, 0:S], pr_, ALU.subtract))
            for i in (6, 7, 0, 1, 2, 3, 4, 5):
                V.scalar_tensor_tensor(pr_[:, i, :], d[:, i, :], vc("rwkv_mu_2", 8 * l + i), pr_[:, i, :], ALU.mult, ALU.add)\
                 .then_inc(*vector.mark("shifted_r", l, i))
            book.new[("vector", "shifted_r", l, 7)] = vector.n["shifted"]
            book.new[("vector", "shifted_67", l)] = vector.n["shifted"] - 6
            dve.wait_ge(*vector.now("shifted_r"))
            yield
            for c in range(2):
                V.tensor_scalar(kk[:, c, :], k_[:, c, :], vc("rwkv_k_k_2", 2 * l + c), None, ALU.mult).then_inc(*vector.mark("kk", l))
            dve.wait_ge(*vector.now("kk"))
            dve.wait_ge(*scalar.at("lora", l, "gv"))
            link(dve, V.tensor_scalar(ld, ld, -float(np.exp(-0.5)), None, ALU.mult))
            link(dve, V.tensor_tensor_scan(flat(Bc), C("seg"), flat(ld), 0.0, ALU.mult, ALU.add))
            if l:
                dve.wait_ge(*scalar.at("vmix2", l))
                link(dve, V.tensor_tensor(kt, v_first, v_, ALU.subtract))
                link(dve, V.tensor_tensor(kt, kt, bt, ALU.mult))
                V.tensor_tensor(v_, v_, kt, ALU.add).then_inc(*vector.mark("rwkv_v", l))
            else:
                V.tensor_copy(v_first, v_).then_inc(*vector.mark("rwkv_v", l))
            dve.wait_ge(*vector.now("rwkv_v"))
            yield
            dve.wait_ge(*tensor.at("kk_sum", l))
            link(dve, V.tensor_scalar(rt, halves(bank("kk_sum", l)), 1e-24, None, ALU.max))
            V.reciprocal(rt, rt).then_inc(*vector.mark("kk_sum", l))
            dve.wait_ge(*scalar.at("kk_root", l))
            link(dve, V.tensor_tensor(kk, kk, rt, ALU.mult))
            link(dve, V.tensor_tensor(bt, kk, av, ALU.mult))
            for c in range(2):
                link(dve, V.tensor_scalar(av[:, c, :], av[:, c, :], -1.0, vc("rwkv_k_a_2", 2 * l + c), ALU.add, ALU.mult))
            link(dve, V.scalar_tensor_tensor(k_, av, 1.0, k_, ALU.add, ALU.mult))
            for c in range(2):
                V.scalar_tensor_tensor(av[:, c, :], r_[:, c, :], vc("rwkv_r_k_2", 2 * l + c), k_[:, c, :], ALU.mult, ALU.mult)\
                 .then_inc(*vector.mark("rk", l))
            B4, D4 = (flat(t).rearrange("p (u t) -> p u t", u=4) for t in (Bc, rt))
            mid, endx = stat[:, 48:52], stat[:, 52:54]
            link(dve, V.tensor_copy(mid.unsqueeze(2), B4[:, :, 63:64]))
            m2 = mid.rearrange("p (c j) -> p c j", c=2)
            link(dve, V.tensor_tensor(endx.unsqueeze(2), m2[:, :, 1:2], m2[:, :, 0:1], ALU.subtract))
            link(dve, V.tensor_tensor(endx, endx, Bc[:, :, P - 1], ALU.add))
            link(dve, V.tensor_tensor(D4, B4, mid.unsqueeze(2).broadcast_to((P, 4, P)), ALU.subtract))
            V.tensor_tensor(ld, rt, ld, ALU.subtract).then_inc(*vector.mark("exponents", l))
            yield
            dve.wait_ge(*tensor.at("bonus", l))
            V.tensor_tensor(av, halves(bank("bonus", l)), v_, ALU.mult).then_inc(*vector.mark("bonus", l))
            dve.wait_ge(*scalar.at("exponentials", l))
            V.scalar_tensor_tensor(at_, kk, -1.0, ld, ALU.mult, ALU.mult).then_inc(*vector.mark("chain"))
            V.tensor_tensor(bt, bt, kt, ALU.mult).then_inc(*vector.mark("chain"))
            V.tensor_tensor(rt, rt, r_, ALU.mult).then_inc(*vector.mark("chain"))
            V.tensor_tensor(kt, kt, k_, ALU.mult).then_inc(*vector.mark("decayed", l))
            dve.wait_ge(*vector.now("decayed"))
            bx, kx = kk[:, :, 0:P], kk[:, :, P:S]
            for c in range(2):
                V.tensor_scalar(bx[:, c, :], bt[:, c, 0:P], endx[:, c:c + 1], None, ALU.mult).then_inc(*vector.mark("chain"))
                V.tensor_scalar(kx[:, c, :], kt[:, c, 0:P], endx[:, c:c + 1], None, ALU.mult).then_inc(*vector.mark("moved", l))
            idb = ident.unsqueeze(1).broadcast_to((P, 8, P))
            V.tensor_copy(Tm.rearrange("p (u t) -> p u t", u=8), idb).then_inc(*vector.mark("chain"))
            link(dve, V.tensor_copy(TT.rearrange("p (u t) -> p u t", u=8), idb))
            yield
            for name, dst, a, bq, m in pairs(W):
                for par in range(2):
                    dve.wait_ge(*tensor.at("pairs", l, name, par))
                    V.tensor_tensor(dst[:, par * 512:(par + 1) * 512].rearrange("p (u t) -> p u t", u=4),
                                    bank("pairs", l, name, par)[:, :].rearrange("p (u t) -> p u t", u=4),
                                    C(m).unsqueeze(1).broadcast_to((P, 4, P)), ALU.mult).then_inc(*vector.mark("pairs", l, name, par))
            dve.wait_ge(*vector.now("pairs"))
            yield
            yield
            for lev in range(LEVELS):
                if lev:
                    dve.wait_ge(*tensor.at("NT_T", l, lev - 1, 1))
                for par in range(2):
                    V.tensor_tensor(NL[par].rearrange("p (u t) -> p u t", u=4),
                                    NT[:, par * 512:(par + 1) * 512].rearrange("p (u t) -> p u t", u=4),
                                    C("levels")[:, lev * P:(lev + 1) * P].unsqueeze(1).broadcast_to((P, 4, P)), ALU.mult)\
                     .then_inc(*vector.mark("level", l, lev))
                out_vector(dve, Xm[:, 512:1024], bank("NT_T", l, lev, 1)[:, :], "NT_T", l, lev, 1)
                yield
                for par in range(2):
                    hs = slice(par * 512, par * 512 + 512)
                    dve.wait_ge(*tensor.at("dTT", l, lev, par))
                    V.tensor_tensor(Tm[:, hs], Tm[:, hs], bank("dT", l, lev, par)[:, :], ALU.add).then_inc(*vector.mark("dT", l, lev, par))
                    V.tensor_tensor(TT[:, hs], TT[:, hs], bank("dTT", l, lev, par)[:, :], ALU.add).then_inc(*vector.mark("dTT", l, lev, par))
                dve.wait_ge(*vector.now("dTT"))
                yield
            yield
            yield
            dve.wait_ge(*scalar.at("rwkv_y", l))
            dve.wait_ge(*tensor.at("gn_mean", l))
            V.scalar_tensor_tensor(rt, halves(bank("gn_mean", l)), -1.0 / 64, rt, ALU.mult, ALU.add).then_inc(*vector.mark("gn_mean", l))
            dve.wait_ge(*vector.now("gn_mean"))
            yield
            dve.wait_ge(*tensor.at("gn_var", l))
            link(dve, V.tensor_scalar(kt, halves(bank("gn_var", l)), 1.0 / 64, GN_EPS, ALU.mult, ALU.add))
            V.reciprocal(kt, kt).then_inc(*vector.mark("gn_var", l))
            dve.wait_ge(*scalar.at("gn_root", l))
            link(dve, V.tensor_tensor(rt, rt, kt, ALU.mult))
            for c in range(2):
                V.tensor_scalar(rt[:, c, :], rt[:, c, :], vc("rwkv_gn_w_2", 2 * l + c), vc("rwkv_gn_b_2", 2 * l + c), ALU.mult, ALU.add)\
                 .then_inc(*vector.mark("chain"))
            dve.wait_ge(*vector.now("chain"))
            link(dve, V.tensor_tensor(rt, rt, av, ALU.add))
            link(dve, V.tensor_tensor(ys[1], rt, gv, ALU.mult))
            yield

        def rwkv_scalar(act, l):
            W = rwkv_buffers()
            yield
            act.wait_ge(vector.sem("shifted_r"), book.old.get(("vector", "shifted_67", l), 1))
            SC.activation(pr_[:, 7, :], pr_[:, 7, :], ACT.Sigmoid).then_inc(*scalar.mark("chain"))
            SC.activation(pr_[0:64, 6, :], pr_[0:64, 6, :], ACT.Tanh).then_inc(*scalar.mark("lora_in", l))
            for dst, w_, src, sl, bias in LORA:
                act.wait_ge(*tensor.at("lora", l, dst))
                b = bank("lora", l, dst)
                if bias:
                    SC.activation(W[dst][:, 0, :], b[:, 0:S], ACT.Sigmoid, bias=vc(bias, 2 * l)).then_inc(*scalar.mark("chain"))
                    SC.activation(W[dst][:, 1, :], b[:, S:T2], ACT.Sigmoid, bias=vc(bias, 2 * l + 1)).then_inc(*scalar.mark("lora", l, dst))
                else:
                    SC.activation(W[dst], halves(b), ACT.Copy).then_inc(*scalar.mark("lora", l, dst))
            if l:
                out_scalar(act, W["kt"][0:32, 0, :], bank("vmix1", l)[0:32, 0:S], "vmix1", l)
                act.wait_ge(*tensor.at("vmix2", l))
                SC.activation(W["bt"][:, 0, :], bank("vmix2", l)[:, 0:S], ACT.Sigmoid, bias=vc("rwkv_v0_2", 0)).then_inc(*scalar.mark("chain"))
                SC.activation(W["bt"][:, 1, :], bank("vmix2", l)[:, S:T2], ACT.Sigmoid, bias=vc("rwkv_v0_2", 1)).then_inc(*scalar.mark("vmix2", l))
            act.wait_ge(*vector.at("kk", l))
            SC.activation(W["rt"], W["kk"], ACT.Square).then_inc(*scalar.mark("kk_sq", l))
            yield
            act.wait_ge(*vector.at("kk_sum", l))
            SC.activation(W["rt"], W["rt"], ACT.Sqrt).then_inc(*scalar.mark("kk_root", l))
            yield
            act.wait_ge(*vector.at("exponents", l))
            endx = stat[:, 52:54]
            SC.activation(endx, endx, ACT.Exp).then_inc(*scalar.mark("chain"))
            link_s(act, SC.activation(W["kt"], W["rt"], ACT.Exp, scale=-1.0))
            SC.activation(W["rt"], W["rt"], ACT.Exp).then_inc(*scalar.mark("chain"))
            SC.activation(W["ld"], W["ld"], ACT.Exp).then_inc(*scalar.mark("exponentials", l))
            yield
            act.wait_ge(*vector.at("exponents", l))
            out_scalar(act, W["B"], halves(bank("rwkv_vt", l)), "rwkv_vt", l)
            yield
            for n in range(4):
                for par in range(2):
                    out_scalar(act, CROSS[2 * n + par], bank("cross", l, n, par)[:, 0:S], "cross", l, n, par)
            yield
            for lev in range(LEVELS):
                out_scalar(act, Xm[:, 0:512], bank("NT_T", l, lev, 0)[:, :], "NT_T", l, lev, 0)
                yield
                yield
            for j in range(2):
                out_scalar(act, Wm[:, j, :], bank("W", l, j)[:, 0:S], "W", l, j)
                out_scalar(act, SA[:, j, :], bank("SA", l, j)[:, 0:S], "SA", l, j)
                yield
            out_scalar(act, W["rt"], halves(bank("rwkv_y", l)), "rwkv_y", l)
            yield
            act.wait_ge(*vector.at("gn_mean", l))
            SC.activation(W["kt"], W["rt"], ACT.Square).then_inc(*scalar.mark("gn_sq", l))
            act.wait_ge(*vector.at("gn_var", l))
            SC.activation(W["kt"], W["kt"], ACT.Sqrt).then_inc(*scalar.mark("gn_root", l))
            yield

        Wm, SA = Xm[:, 0:512].rearrange("p (j c) -> p j c", j=2), Xm[:, 512:1024].rearrange("p (j c) -> p j c", j=2)
        o = pool0 + 7 * 1024 + 1536
        BUF9 = [chan() for _ in range(9)]
        NL = [place(512), rstd[:, :]]
        assert o <= AR, (o, AR)
        CROSS = x_hi[4:8] + [place(256) for _ in range(4)]
        assert o <= AR, (o, AR)

        def cross_of(n, hd):
            return CROSS[2 * n + hd % 2][:, (hd // 2) * P:(hd // 2 + 1) * P]

        def together(*mixers, filler=None):
            live = list(mixers)
            while live:
                for m in list(live):
                    if next(m, "end") == "end":
                        live.remove(m)
                    if filler:
                        next(filler, None)

        MIX_DST = [[raw_s[:, i, :] for i in range(4)], [raw_s[:, i, :] for i in (4, 5)],
                   [raw_m[:, i, :] for i in range(4)], [raw_m[:, i, :] for i in (4, 5)],
                   [raw_r[:, i, 1:S + 1] for i in range(4)], [raw_r[:, i, 1:S + 1] for i in range(4, 8)],
                   [raw_h[:, i, :] for i in range(4)], [raw_h[:, i, :] for i in range(4, 8)]]

        def in_tiles(pe, l, chunks):
            for c in chunks:
                w = next_weights(pe)
                for i in range(len(MIX_DST[c])):
                    project_tensor(pe, w, i * P, P, S, ("mixin", l, c, i))
                    if i == len(MIX_DST[c]) - 1:
                        chunk_read()
                    yield

        def in_outs(act, l, chunks):
            for c in chunks:
                for i, dst in enumerate(MIX_DST[c]):
                    out_scalar(act, dst, bank("mixin", l, c, i)[:, 0:S], "mixin", l, c, i)
                    yield

        def gate_tiles(pe, l, half):
            for i in range(16):
                if i % 4 == 0:
                    w = next_weights(pe)
                project_tensor(pe, w, (i % 4) * P, P, S, ("gate", l, half, i))
                if i % 4 == 3:
                    chunk_read()
                yield

        def gate_outs(act, l, half):
            for i in range(16):
                if half:
                    act.wait_ge(*vector.at("merged", l, i % 4))
                out_scalar(act, gates[:, i, :], bank("gate", l, half, i)[:, 0:S], "gate", l, half, i, func=ACT.Sigmoid)
                yield

        def mixer_tensor(pe, l):
            norm_tensor(pe, S, ("m1", l))
            pe.wait_ge(*vector.at("normed", ("m1", l), KD - 1))
            for _ in in_tiles(pe, l, range(4)):
                pass
            join(tensor, pe, ("mixers", l))
            fill = in_tiles(pe, l, range(4, 8))
            together(stick_tensor(pe, l), moba_tensor(pe, l, fill), filler=fill)
            for _ in fill:
                pass
            join(tensor, pe, ("group1", l))
            fill = gate_tiles(pe, l, 0)
            rotating[0] = 6
            together(rwkv_tensor(pe, l), hgrn_tensor(pe, l), filler=fill)
            rotating[0] = 8
            for _ in fill:
                pass
            join(tensor, pe, ("branches", l))
            for half in range(2):
                if half:
                    for _ in gate_tiles(pe, l, 1):
                        pass
                w = next_weights(pe)
                for m in range(4):
                    for br in range(0, 4, 2):
                        b = take(pe, "branch", l, 4 * half + m, br)
                        for q in range(2):
                            for k in range(2):
                                last = mm(b[:, q * S:(q + 1) * S], w[:, 2 * (br + q) + k, m * P:(m + 1) * P], ys[br + q][:, k, :], k, 2)
                        last.then_inc(*tensor.mark("branch", l, 4 * half + m, br))
                chunk_read()
            pe.wait_ge(*vector.at("merged", l, KD - 1))
            for i in range(2):
                w = next_weights(pe)
                for m in range(4):
                    b = take(pe, "w_out", l, 4 * i + m)
                    for k in range(KD):
                        last = mm(b[:, 0:S], w[:, k, m * P:(m + 1) * P], merged[:, k, :], k, KD)
                    last.then_inc(*tensor.mark("w_out", l, 4 * i + m))
                chunk_read()

        merged = raw_h

        def mixer_vector(dve, l):
            norm_vector(dve, S, ("m1", l), lambda s, k: vc("norm1_g_2", 8 * l + k))
            V.memset(raw_r[:, :, 0:1], 0.0).then_inc(*vector.mark("chain"))
            for c in range(4):
                for i in range(0, len(MIX_DST[c]), 2):
                    out_vector(dve, MIX_DST[c][i], bank("mixin", l, c, i)[:, 0:S], "mixin", l, c, i)
            join(vector, dve, ("mixers", l))
            together(stick_vector(dve, l), moba_vector(dve, l))
            join(vector, dve, ("group1", l))
            together(rwkv_vector(dve, l), hgrn_vector(dve, l))
            join(vector, dve, ("branches", l))
            for m in range(KD):
                gt = gates.rearrange("p (b m) t -> p b m t", b=4)[:, :, m % 4, :]
                dve.wait_ge(*scalar.at("gate", l, m // 4, 12 + m % 4))
                for br in range(0, 4, 2):
                    dve.wait_ge(*tensor.at("branch", l, m, br))
                    g2 = gt[:, br:br + 2, :]
                    V.tensor_tensor(g2, g2, halves(bank("branch", l, m, br)), ALU.mult).then_inc(*vector.mark("branch", l, m, br))
                dve.wait_ge(*vector.now("branch"))
                link(dve, V.tensor_tensor(gt[:, 0:2, :], gt[:, 0:2, :], gt[:, 2:4, :], ALU.add))
                V.tensor_tensor(merged[:, m, :], gt[:, 0, :], gt[:, 1, :], ALU.add).then_inc(*vector.mark("merged", l, m))
            for d in range(KD):
                dve.wait_ge(*tensor.at("w_out", l, d))
                V.tensor_tensor(x[:, d, 0:S], x[:, d, 0:S], bank("w_out", l, d)[:, 0:S], ALU.add).then_inc(*vector.mark("w_out", l, d))

        def mixer_scalar(act, l):
            norm_scalar(act, S, ("m1", l))
            for c in range(4):
                for i in range(1, len(MIX_DST[c]), 2):
                    out_scalar(act, MIX_DST[c][i], bank("mixin", l, c, i)[:, 0:S], "mixin", l, c, i)
            join(scalar, act, ("mixers", l))
            fill = in_outs(act, l, range(4, 8))
            together(stick_scalar(act, l), moba_scalar(act, l, fill), filler=fill)
            for _ in fill:
                pass
            join(scalar, act, ("group1", l))
            fill = gate_outs(act, l, 0)
            together(rwkv_scalar(act, l), hgrn_scalar(act, l), filler=fill)
            for _ in fill:
                pass
            join(scalar, act, ("branches", l))
            for _ in gate_outs(act, l, 1):
                pass
            act.wait_ge(*vector.at("w_out", l, KD - 1))

        hid = arena[:, 0:NF * S].rearrange("p (f t) -> p f t", f=NF)

        def ffn_tensor(pe, l):
            norm_tensor(pe, S, ("m2", l))
            pe.wait_ge(*vector.at("normed", ("m2", l), KD - 1))
            for i in range(6):
                nf = min(4, NF - 4 * i)
                for which in ("ffn_gate", "ffn_up"):
                    w = next_weights(pe)
                    for m in range(0, nf, 2):
                        b = take(pe, which, l, 4 * i + m)
                        for q in range(2):
                            for k in range(KD):
                                last = mm(b[:, q * S:(q + 1) * S], w[:, k, (m + q) * P:(m + q + 1) * P], h[:, k, 0:S], k, KD)
                        last.then_inc(*tensor.mark(which, l, 4 * i + m))
                    chunk_read()
            pe.wait_ge(*vector.at("ffn_up", l, NF - 2))
            for d in range(KD):
                w = next_weights(pe)
                b = take(pe, "ffn_down", l, d)
                for k in range(NF):
                    last = mm(b[:, 0:S], w[:, k, :], hid[:, k, :], k, NF)
                last.then_inc(*tensor.mark("ffn_down", l, d))
                chunk_read()

        def ffn_vector(dve, l):
            norm_vector(dve, S, ("m2", l), lambda s, k: vc("norm2_g_2", 8 * l + k))
            for f in range(0, NF, 2):
                dve.wait_ge(*scalar.at("ffn_gate", l, f))
                dve.wait_ge(*tensor.at("ffn_up", l, f))
                a = hid[:, f:f + 2, :]
                V.tensor_tensor(a, a, halves(bank("ffn_up", l, f)), ALU.mult).then_inc(*vector.mark("ffn_up", l, f))
            for d in range(KD):
                dve.wait_ge(*tensor.at("ffn_down", l, d))
                V.tensor_tensor(x[:, d, 0:S], x[:, d, 0:S], bank("ffn_down", l, d)[:, 0:S], ALU.add).then_inc(*vector.mark("ffn_down", l, d))
            join(vector, dve, ("ffn", l))

        def ffn_scalar(act, l):
            norm_scalar(act, S, ("m2", l))
            for f in range(0, NF, 2):
                act.wait_ge(*tensor.at("ffn_gate", l, f))
                SC.activation(hid[:, f:f + 2, :], halves(bank("ffn_gate", l, f)), ACT.Silu).then_inc(*scalar.mark("ffn_gate", l, f))
            join(scalar, act, ("ffn", l))

        otok = arena[:, 0:2048].rearrange("p (j d) -> p j d", j=2)

        small_list = []
        for name, n in VECS:
            r, a = vcol[name], A[name]
            if len(a.shape) == 3:
                a = a.rearrange("a b c -> (a b c)")
            elif len(a.shape) == 2:
                a = a.rearrange("a b -> (a b)")
            a = a.rearrange("(r c) -> r c", c=P)
            done = 0
            while done < n:
                m = min(n - done, P - (r + done) % P)
                small_list.append((stage[(r + done) % P:(r + done) % P + m, (r + done) // P, :], a[done:done + m, :]))
                done += m
        small_list += [
            (stage[0:8, 2, :], A["c"].rearrange("a (r c) -> (a r) c", c=P)),
            (stage[8:16, 2, :], A["c_ctx"].rearrange("(r c) -> r c", c=P)),
            (sink_row[:, 0:12], A["swa_sink"].rearrange("a b -> (a b)").rearrange("(o n) -> o n", o=1)),
            (xtok[:, 0], A["x"][0].rearrange("(j p) d -> p j d", p=P)),
            (xtok[:, 1], A["ctx"][0].rearrange("(j p) d -> p j d", p=P)),
        ]
        late_list = []
        for l in range(L):
            late_list += [
                (uq[:, l], A["mla_w_uq"][l].rearrange("(k p) n -> p k n", p=P)),
                (ukv[:, l], A["mla_w_ukv"][l]),
                (rtr[:, l], A["router_w"][l].rearrange("(k p) n -> p k n", p=P)),
                (wa2[0:64, l], A["rwkv_w2_2"][l]),
                (wa2[64:128, l], A["rwkv_a2_2"][l]),
                (g2w[:, l], A["rwkv_g2_2"][l]),
            ]
        late_list += [(v1w, A["rwkv_v1_2"][0].rearrange("(k p) n -> p k n", p=P)), (v2w[0:32, :], A["rwkv_v2_2"][0])]
        late_loaded = sem("late_loaded")

        def loads_scalar(act):
            act.dma_start(cst[:, :], A["consts"][:, 0:N_BOTH]).then_inc(const_loaded, 16)
            for dst, src in small_list:
                act.dma_start(dst, src).then_inc(small_loaded, 16)
            act.dma_start(cst1, A["consts"][:, N_BOTH:N_BOTH + N_FIRST]).then_inc(late_loaded, 16)
            for dst, src in late_list:
                act.dma_start(dst, src).then_inc(late_loaded, 16)

        with nc.Block() as block:
            @block.tensor
            def _(pe):
                turn[0], at[0] = 0, 0
                pe.wait_ge(const_loaded, 16)
                pe.wait_ge(small_loaded, 16 * len(small_list))
                start_tensor(pe)
                pe.wait_ge(*scalar.at("cond"))
                for i in range(12):
                    ada_tensor(pe, 0, i)
                pe.wait_ge(late_loaded, 16 * (1 + len(late_list)))
                join(tensor, pe, "start")
                for l in range(L):
                    hybrid_tensor(pe, l)
                    moe_tensor(pe, l)
                norm_tensor(pe, S, "final1")
                join(tensor, pe, "block1")
                for l in range(L):
                    mixer_tensor(pe, l)
                    ffn_tensor(pe, l)
                    join(tensor, pe, ("ffn", l))
                norm_tensor(pe, S, "final2")
                for j in range(2):
                    for half in range(2):
                        pe.wait_ge(*vector.at("normed", "final2", 4 * half + 3))
                        b = take(pe, "tokens", j, half)
                        for k in range(4):
                            last = PE.transpose(b[:, k * P:(k + 1) * P], h[:, 4 * half + k, j * P:(j + 1) * P], ident)
                        last.then_inc(*tensor.mark("tokens", j, half))

            @block.vector
            def _(dve):
                dve.wait_ge(const_loaded, 16)
                start_vector(dve)
                for i in range(12):
                    ada_vector(dve, 0, i)
                dve.wait_ge(late_loaded, 16 * (1 + len(late_list)))
                join(vector, dve, "start")
                for l in range(L):
                    hybrid_vector(dve, l)
                    moe_vector(dve, l)
                norm_vector(dve, S, "final1", lambda s, k: vc("final_norm_g", k))
                dve.wait_ge(*vector.now("normed"))
                link(dve, V.tensor_copy(x[:, :, 0:S], h[:, :, 0:S]))
                join(vector, dve, "block1")
                for l in range(L):
                    mixer_vector(dve, l)
                    ffn_vector(dve, l)
                norm_vector(dve, S, "final2", lambda s, k: vc("final_g_2", k))
                for j in range(2):
                    out_vector(dve, otok[:, j, 0:512], bank("tokens", j, 0)[:, :], "tokens", j, 0)

            @block.scalar
            def _(act):
                loads_scalar(act)
                start_scalar(act)
                join(scalar, act, "start")
                for l in range(L):
                    hybrid_scalar(act, l)
                    moe_scalar(act, l)
                norm_scalar(act, S, "final1")
                join(scalar, act, "block1")
                for l in range(L):
                    mixer_scalar(act, l)
                    ffn_scalar(act, l)
                norm_scalar(act, S, "final2")
                for j in range(2):
                    out_scalar(act, otok[:, j, 512:1024], bank("tokens", j, 1)[:, :], "tokens", j, 1)

            @block.sync
            def _(sp):
                def load(n):
                    sp.dma_start(slot(n), stream[n][0]).then_inc(loaded[n % RING], 16)

                def wait_used(n):
                    kind, v = book.old.get(("used", n)) or ("mods", 1)
                    sp.wait_ge(tensor.sem(kind), v)

                for n in range(RING):
                    load(n)
                n = RING
                ecs = {expert_chunk[l]: l for l in range(L)}
                while n < len(stream):
                    m = n - RING
                    if m in ecs:
                        l = ecs[m]
                        sources = [A[w][l] for w in ("exp_w_gate", "exp_w_up", "exp_w_down")]

                        def step(g, q, c):
                            e = NE * l + q
                            if c == 2:
                                sp.wait_ge(half_made, 2 * e + 2 + 8 * g)
                            else:
                                sp.wait_ge((gate_made, up_made)[c], e + 1 + 4 * g)

                        with sp.Fori(0, NE // 4 - 1) as g:
                            for q in range(4):
                                for c in range(3):
                                    step(g, q, c)
                                    qq, cc = q + (c + RING) // 3, (c + RING) % 3
                                    src = sources[cc].rearrange("e (k p) n -> p e k n", p=P)[:, bass.ds(4 * g + qq, 1)]
                                    later = m + 3 * q + c + RING
                                    sp.dma_start(slot(later), src.rearrange("p e k n -> p (e k) n"))\
                                      .then_inc(loaded[later % RING], 16)
                        n += 36
                        for q in range(4):
                            for c in range(3):
                                step(NE // 4 - 1, q, c)
                                load(n)
                                n += 1
                        continue
                    wait_used(m)
                    load(n)
                    n += 1
                sp.wait_ge(*vector.at("tokens", 1, 0))
                sp.wait_ge(*scalar.at("tokens", 1, 1))
                sp.dma_start(out[0].rearrange("(j p) d -> p j d", p=P), otok).then_inc(stored, 16)
                sp.wait_ge(stored, 16)


_INS = ["x", "c", "ctx", "c_ctx", "ada_w", "ada_b", "norm1_g", "w_in", "mla_q_norm_g", "mla_w_uq", "mla_kv_norm_g",
        "mla_w_ukv", "swa_sink", "conv_w", "w_o", "norm2_g", "router_w", "exp_w_gate", "exp_w_up", "exp_w_down",
        "final_norm_g", "norm1_g_2", "w_in_2", "rwkv_mu_2", "rwkv_w0_2", "rwkv_w2_2", "rwkv_a0_2", "rwkv_a2_2",
        "rwkv_g2_2", "rwkv_k_k_2", "rwkv_k_a_2", "rwkv_r_k_2", "rwkv_gn_w_2", "rwkv_gn_b_2", "rwkv_v0_2",
        "rwkv_v1_2", "rwkv_v2_2", "hgrn_lb_logits_2", "hgrn_gn_g_2", "w_branch_2", "w_out_2", "norm2_g_2",
        "w_ffn_gate_2", "w_ffn_up_2", "w_ffn_down_2", "final_g_2"]


def kernel(**inputs):
    import concourse.bacc as _bacc
    from concourse.bass_utils import run_bass_kernel_spmd as _run

    arrays = {f"in_{name}": np.ascontiguousarray(inputs[name]) for name in _INS}
    arrays["consts"] = CONST
    book = Book()
    for _ in range(2):
        nc = _bacc.Bacc("TRN2", target_bir_lowering=False, num_devices=1)
        A = {n.removeprefix("in_"): nc.dram_tensor(n, a.shape, mybir.dt.from_np(a.dtype), kind="ExternalInput").ap()
             for n, a in arrays.items()}
        out = nc.dram_tensor("out", (1, S, D), F32, kind="ExternalOutput").ap()
        program(nc, A, out, book)
        book.turn()
    r = _run(nc, [arrays], core_ids=[0])
    return r.results[0]["out"]
```

```python
import numpy as np
import concourse.bass as bass
from concourse import mybir
from contextlib import ExitStack

F32 = mybir.dt.float32
U32 = mybir.dt.uint32
ALU = mybir.AluOpType
ACT = mybir.ActivationFunctionType
AX = mybir.AxisListType.X

P = 128
D = 1024
KD = D // P
S = 256
T2 = 2 * S
EPS = 1e-6
NEG = -1e30
L = 2
H1 = 6
NE, CAP, FF = 16, 32, 512
DFF = 2816
NF = DFF // P
MLA_SCALE = 96 ** -0.5
HEAD_SCALE = 64 ** -0.5
GN_EPS = 64e-5
SLOT = 4096
RING = 3
LEVELS = 7


def constants():
    cols, at, width = ([], []), {}, [0, 0]

    def put(name, a, first=False):
        a = np.asarray(a, np.float32)
        full = np.zeros((P, a.shape[1]), np.float32)
        full[:a.shape[0]] = a
        cols[first].append(full)
        at[name] = (first, width[first], a.shape[1])
        width[first] += a.shape[1]

    i = np.arange(P)
    t = np.arange(S)
    put("ident", np.eye(P))
    put("ones", np.ones((P, P)))
    put("heads", (i[:, None] // 64 == i[None, :] // 64))
    put("suffix", (i[:, None] >= i[None, :]))
    lev = []
    for l in range(LEVELS):
        n = 2 ** l
        a, b = i[:, None] // n, i[None, :] // n
        lev.append((a // 2 == b // 2) & (a % 2 == 0) & (b % 2 == 1))
    put("levels", np.concatenate(lev, 1))
    put("before", i[:, None] < i[None, :])
    put("upto", i[:, None] <= i[None, :])
    put("seg", np.tile((i > 0)[None, :], (P, 4)))
    put("no_sink", np.full((P, 1), NEG))
    q = np.arange(2)[None, :, None] * P + i[:, None, None]
    put("window", np.where(np.abs(q - t[None, None, :]) <= 128, 0, NEG).reshape(P, -1), True)
    put("causal", np.where(t[None, None, :] <= q, 0, NEG).reshape(P, -1))
    put("stick", np.where(q < t[None, None, :], -1.0, 0).reshape(P, -1))
    put("stick_add", np.where(q < t[None, None, :], 0, NEG).reshape(P, -1))

    def axial(rot):
        n = rot // 4
        inv = np.float32(10000.0) ** (-np.arange(n, dtype=np.float32) / np.float32(n))
        row, col = (t // 64).astype(np.float32), (t % 64).astype(np.float32)
        ang = np.concatenate([row[:, None] * inv, col[:, None] * inv], 1).astype(np.float32)
        return np.cos(ang).T, np.sin(ang).T

    def rot(n, base, half):
        r = np.zeros((n, n), np.float32)
        for b in base:
            for k in range(half):
                r[b + half + k, b + k] = -1.0
                r[b + k, b + half + k] = 1.0
        return r

    c, s = axial(64)
    put("cos_swa", np.tile(c, (4, 1)), True)
    put("sin_swa", np.tile(s, (4, 1)), True)
    rs = rot(P, (0, 64), 32)
    put("rot_swa", rs, True)
    for g in range(2):
        dup = np.zeros((P, P), np.float32)
        dup[64 * g + i % 64, i] = 1.0
        put(f"dup{g}", dup, True)
        put(f"duprot{g}", rs @ dup, True)
    c, s = axial(32)
    put("cos_mla", np.concatenate([np.ones((64, S)), c, c]), True)
    put("sin_mla", np.concatenate([np.zeros((64, S)), s, s]), True)
    put("rot_mla", rot(96, (64,), 16), True)
    inv = np.float32(500000.0) ** (-np.arange(0, 16, 2, dtype=np.float32) / np.float32(16))
    ang = (t.astype(np.float32)[:, None] * inv[None, :]).astype(np.float32)
    c, s = np.cos(ang).T, np.sin(ang).T
    one = np.concatenate([c, c, np.ones((48, S))])
    zero = np.concatenate([s, s, np.zeros((48, S))])
    put("cos_moba", np.concatenate([one, one]))
    put("sin_moba", np.concatenate([zero, zero]))
    put("rot_moba", rot(P, (0, 64), 8))
    e = np.zeros((32, 8, P), np.float32)
    for sg in range(8):
        for p in range(P):
            e[(sg // 4) * 16 + (sg % 4) * 4 + p // CAP, sg, p] = 1.0
    put("spread", e.reshape(32, -1), True)
    put("pick", (i[:, None] % 32 == np.arange(2)[None, :]))
    put("slot", (i % CAP + 1)[:, None], True)
    put("slots", np.tile(np.arange(1, CAP + 1)[None, :], (P, 1)), True)
    return np.concatenate(cols[0] + cols[1], 1), at, width


CONST, CONST_AT, (N_BOTH, N_FIRST) = constants()

VECS = [
    ("ada_b", 96), ("norm1_g", 16), ("norm2_g", 16),
    ("mla_q_norm_g", 4), ("mla_kv_norm_g", 2), ("conv_w", 12), ("norm1_g_2", 16), ("norm2_g_2", 16),
    ("rwkv_mu_2", 16), ("final_g_2", 8), ("rwkv_w0_2", 4), ("rwkv_a0_2", 4), ("rwkv_k_k_2", 4),
    ("rwkv_k_a_2", 4), ("rwkv_r_k_2", 4), ("rwkv_gn_w_2", 4), ("rwkv_gn_b_2", 4), ("rwkv_v0_2", 2),
    ("hgrn_lb_logits_2", 4), ("hgrn_gn_g_2", 4), ("final_norm_g", 8),
]


class Book:

    def __init__(self):
        self.old, self.new = {}, {}

    def turn(self):
        self.old, self.new = self.new, {}


FAMILY = {w: family for family, words in {
    "routing": ("aff", "affT", "pos", "posT", "sel", "xg", "htok"), "scatter": ("slot", "weight", "scattered"),
    "heads": ("q96", "k96", "v", "keys", "values", "latent"), "lora": ("vmix1", "vmix2"),
    "solve": ("NT", "dT", "dTT", "level"), "state": ("W", "SA"),
    "decays": ("bonus", "rk", "moved", "decayed", "exponents", "exponentials"), "turned": ("streams", "sinks", "cond"), "normed": ("unit",),
}.items() for w in words}


def family(kind):
    word = kind.split("_")[0]
    return FAMILY.get(word, word)


class Signals:

    def __init__(self, engine, nc, ctx, book):
        self.engine, self.nc, self.ctx, self.book, self.sems, self.n = engine, nc, ctx, book, {}, {}
        self.last = None

    def sem(self, kind):
        kind = family(kind)
        if kind not in self.sems:
            self.sems[kind] = self.ctx.enter_context(self.nc.semaphore(f"{self.engine}_{kind}"))
            self.n[kind] = 0
        return self.sems[kind]

    def mark(self, *key):
        s, kind = self.sem(key[0]), family(key[0])
        self.n[kind] += 1
        self.book.new[(self.engine,) + key] = self.n[kind]
        self.last = (kind, self.n[kind])
        return s, 1

    def at(self, *key):
        return self.sem(key[0]), self.book.old.get((self.engine,) + key, 1)

    def now(self, kind):
        return self.sem(kind), self.n[family(kind)]

    def close(self, tag):
        self.book.new[("join", self.engine, tag)] = self.last

    def closed(self, tag):
        kind, n = self.book.old.get(("join", self.engine, tag)) or ("chain", 0)
        return (self.sem(kind), n) if n else None


def program(nc, A, out, book):
    ctx = ExitStack()
    with ctx:
        def sb(name, n):
            return ctx.enter_context(nc.sbuf_tensor(name, [P, n], F32))

        def sem(name):
            return ctx.enter_context(nc.semaphore(name))

        tensor, scalar, vector = (Signals(n, nc, ctx, book) for n in ("tensor", "scalar", "vector"))
        loaded = [sem(f"slot_loaded_{i}") for i in range(RING)]
        const_loaded, small_loaded, stored = (sem(n) for n in ("const_loaded", "small_loaded", "stored"))
        V, SC, PE = nc.vector, nc.scalar, nc.tensor

        ring = sb("ring", RING * SLOT)
        x = sb("x", KD * T2)[:, :].rearrange("p (k t) -> p k t", k=KD)
        h = sb("h", KD * T2)[:, :].rearrange("p (k t) -> p k t", k=KD)
        cst = sb("cst", N_BOTH)
        vec = sb("vec", 256)
        mods = sb("mods", 2 * 96)[:, :].rearrange("p (l m s) -> p l m s", l=L, s=2)
        stat = sb("stat", 160)
        rstd = sb("rstd", T2)
        wa2 = sb("wa2", L * 256)[:, :].rearrange("p (l n) -> p l n", l=L)
        g2w = sb("g2w", L * 256)[:, :].rearrange("p (l n) -> p l n", l=L)
        v1w = sb("v1w", 64)[:, :].rearrange("p (k n) -> p k n", k=2)
        v2w = sb("v2w", 256)
        v_first = sb("v_first", 512)[:, :].rearrange("p (c t) -> p c t", c=2)
        AR1 = 16384
        n_first = N_FIRST + L * (2 * 576 + 768 + KD * NE + 12)
        AR = max(AR1 + n_first, 25096)
        arena = sb("arena", AR)
        o = AR1
        cst1 = arena[:, o:o + N_FIRST]
        o += N_FIRST
        uq = arena[:, o:o + L * 1152].rearrange("p (l k n) -> p l k n", l=L, k=2)
        o += L * 1152
        ukv = arena[:, o:o + L * 768].rearrange("p (l n) -> p l n", l=L)
        o += L * 768
        rtr = arena[:, o:o + L * 128].rearrange("p (l k e) -> p l k e", l=L, k=KD)
        o += L * 128
        sinkb = arena[:, o:o + L * 12].rearrange("p (l n) -> p l n", l=L)
        o += L * 12
        cond32 = arena[:, o:o + 32 * KD].rearrange("p (k n) -> p k n", k=KD)
        cond_rows = [arena[:, AR1 - 1024:AR1 - 512], arena[:, AR1 - 512:AR1]]
        assert o + 32 * KD <= AR
        banks = [ctx.enter_context(nc.psum_tensor(f"bank{i}", [P, 512], F32)) for i in range(8)]

        def C(name):
            first, a, n = CONST_AT[name]
            return (cst1 if first else cst)[:, a:a + n]

        ident, ones = C("ident"), C("ones")
        vcol, row = {}, 0
        for name, n in VECS:
            vcol[name] = row
            row += n
        rows = row

        def vc(name, i, n=1):
            return vec[:, vcol[name] + i:vcol[name] + i + n]

        def tiles(off, n, w):
            return arena[:, off:off + n * w].rearrange("p (n w) -> p n w", n=n)

        def flat(a):
            return a.rearrange("p c t -> p (c t)")

        def mm(o, lhsT, rhs, k, n):
            return PE.matmul(o, lhsT, rhs, start=(k == 0), stop=(k == n - 1))

        turn, rotating = [0], [8]
        holder = [None] * 8

        def got(*key):
            return (scalar if ("scalar",) + key in book.old else vector).at(*key)

        def take(pe, *key):
            if key[0] == "hgrn_scores":
                b = 6 + key[-1]
            else:
                b = turn[0] % rotating[0]
                turn[0] += 1
            if holder[b]:
                pe.wait_ge(*got(*holder[b]))
            holder[b] = key
            book.new[("bank",) + key] = b
            return banks[b]

        def bank(*key):
            return banks[book.old.get(("bank",) + key, 0)]

        def join(me, eng, tag):
            me.close(tag)
            for s in (tensor, scalar, vector):
                value = s.closed(tag)
                if value:
                    eng.wait_ge(*value)

        stream, used = [], {}

        def w_chunk(src, k, n):
            stream.append((src.rearrange("(k p) n -> p k n", p=P), k, n))

        IN1 = [(1312, 1824), (928, 1312), (0, 416), (416, 928)]
        IN2 = [(0, 512), (512, 768), (1792, 2304), (2304, 2560), (768, 1280), (1280, 1792), (2560, 3072), (3072, 3584)]
        ADA_FIRST = 4
        ADA_LATE = 12

        def ada_after(l, c):
            return range(ADA_FIRST + 2 * c, ADA_FIRST + 2 * c + 2) if l == 0 else ()

        def ada_chunk(l, i):
            w_chunk(A["ada_w"][l, :, i * 512:(i + 1) * 512], KD, 512)

        expert_chunk = {}
        for i in range(ADA_FIRST):
            ada_chunk(0, i)
        for l in range(L):
            for c, (a, b) in enumerate(IN1):
                w_chunk(A["w_in"][l, :, a:b], KD, b - a)
                for i in ada_after(l, c):
                    ada_chunk(0, i)
            if l == 0:
                for i in range(ADA_LATE):
                    ada_chunk(1, i)
            for i in range(2):
                w_chunk(A["w_o"][l, :, i * 512:(i + 1) * 512], KD, 512)
            expert_chunk[l] = len(stream)
            for e in range(NE):
                w_chunk(A["exp_w_gate"][l, e], KD, FF)
                w_chunk(A["exp_w_up"][l, e], KD, FF)
                w_chunk(A["exp_w_down"][l, e], FF // P, D)
        for l in range(L):
            for a, b in IN2:
                w_chunk(A["w_in_2"][l, :, a:b], KD, b - a)
            for i in range(2):
                for br in range(4):
                    a = 3584 + br * D + i * 512
                    w_chunk(A["w_in_2"][l, :, a:a + 512], KD, 512)
            for i in range(2):
                w_chunk(A["w_branch_2"][l].rearrange("b k n -> (b k) n")[:, i * 512:(i + 1) * 512], 8, 512)
            for i in range(2):
                w_chunk(A["w_out_2"][l, :, i * 512:(i + 1) * 512], KD, 512)
            for i in range(6):
                n = min(512, DFF - i * 512)
                w_chunk(A["w_ffn_gate_2"][l, :, i * 512:i * 512 + n], KD, n)
                w_chunk(A["w_ffn_up_2"][l, :, i * 512:i * 512 + n], KD, n)
            for i in range(KD):
                w_chunk(A["w_ffn_down_2"][l, :, i * P:(i + 1) * P], NF, P)

        def slot(n):
            src, k, w = stream[n]
            return ring[:, n % RING * SLOT:n % RING * SLOT + k * w].rearrange("p (k n) -> p k n", k=k)

        at = [0]

        def next_weights(pe):
            n = at[0]
            at[0] += 1
            pe.wait_ge(loaded[n % RING], 16 * (n // RING + 1))
            return slot(n)

        def chunk_read():
            book.new[("used", at[0] - 1)] = tensor.last


        eps, idle = stat[:, 100:101], stat[:, 101:102]
        stage = arena[:, 0:384].rearrange("p (s c) -> p s c", c=P)
        xtok = arena[:, 512:512 + 4096].rearrange("p (s j d) -> p s j d", s=2, j=2)
        sink_row = stat[0:1, 128:152]
        TURNS = ((0, P), (1, rows - P), (2, 16))

        def start_tensor(pe):
            for s, n in TURNS:
                b = take(pe, "turned", s)
                PE.transpose(b[:, 0:n], stage[0:n, s, :], ident[0:n, 0:n]).then_inc(*tensor.mark("turned", s))
            b = take(pe, "sinks")
            mm(b[:, 0:12], ones[0:1, :], sink_row[:, 0:12], 0, 1).then_inc(*tensor.mark("sinks"))
            for s in range(2):
                for k in range(KD):
                    b = take(pe, "streams", s, k)
                    for j in range(2):
                        last = PE.transpose(b[:, j * P:(j + 1) * P], xtok[:, s, j, k * P:(k + 1) * P], ident)
                        if s == j == 0 and k < len(counted_ahead):
                            last.then_inc(counted_ahead[k], AHEAD)
                    last.then_inc(*tensor.mark("streams", s, k))

        def start_vector(dve):
            V.memset(eps, EPS).then_inc(*vector.mark("chain"))
            V.memset(idle, 0.0).then_inc(hid_done, AHEAD)
            V.memset(stat[:, 103:104], 0.0).then_inc(half_out[1], AHEAD)
            V.memset(cond32, 0.0).then_inc(*vector.mark("turned_cond"))
            for s, n in TURNS:
                dve.wait_ge(*tensor.at("turned", s))
                dst = vec[:, s * P:s * P + n] if s < 2 else stat[:, 64:80]
                V.tensor_copy(dst, bank("turned", s)[:, 0:n]).then_inc(*vector.mark("turned", s))
            V.memset(sinkb, NEG).then_inc(*vector.mark("chain"))
            dve.wait_ge(*vector.now("chain"))
            dve.wait_ge(*tensor.at("sinks"))
            V.tensor_copy(sinkb[:, :, 6:12], bank("sinks")[:, 0:12].rearrange("p (l n) -> p l n", l=L))\
             .then_inc(*vector.mark("sinks"))
            for k in range(KD):
                dve.wait_ge(*tensor.at("streams", 0, k))
                V.tensor_copy(x[:, k, 0:S], bank("streams", 0, k)[:, 0:S]).then_inc(*vector.mark("streams", 0, k))

        def start_scalar(act):
            SC.activation(stat[:, 102:103], ones[:, 0:1], ACT.Copy).then_inc(half_out[0], AHEAD)
            act.wait_ge(*vector.at("turned", 2))
            act.wait_ge(*vector.at("turned_cond"))
            SC.activation(cond32[:, :, 0:2], stat[:, 64:80].rearrange("p (s k) -> p k s", s=2), ACT.Silu).then_inc(*scalar.mark("cond"))
            for k in range(KD):
                act.wait_ge(*tensor.at("streams", 1, k))
                SC.activation(x[:, k, S:T2], bank("streams", 1, k)[:, 0:S], ACT.Copy).then_inc(*scalar.mark("streams", 1, k))

        def rows_tensor(pe, l, i):
            w = next_weights(pe)
            b = take(pe, "mods_rows", l, i)
            for k in range(KD):
                g = k % 4
                last = mm(b[32 * g:32 * g + 32, :], cond32[:, k, :], w[:, k, :], k // 4, KD // 4)
            last.then_inc(*tensor.mark("mods_rows", l, i))
            chunk_read()

        def rows_scalar(act, l, i):
            if i:
                act.wait_ge(*tensor.at("mods", l, i - 1))
            out_scalar(act, cond_rows[l], bank("mods_rows", l, i)[:, :], "mods_rows", l, i)

        def ada_tensor(pe, l, i):
            pe.wait_ge(*scalar.at("mods_rows", l, i))
            b = take(pe, "mods", l, i)
            for m in range(4):
                last = mm(b[:, 2 * m:2 * m + 2], cond_rows[l][:, m * P:(m + 1) * P], C("pick"), 0, 1)
            last.then_inc(*tensor.mark("mods", l, i))

        def ada_vector(dve, l, i):
            dve.wait_ge(*tensor.at("mods", l, i))
            V.tensor_tensor(mods[:, l, 4 * i:4 * i + 4, :], bank("mods", l, i)[:, 0:8].rearrange("p (m s) -> p m s", s=2),
                            vec[:, l * 48 + 4 * i:l * 48 + 4 * i + 4].unsqueeze(2).broadcast_to((P, 4, 2)), ALU.add)\
             .then_inc(*vector.mark("mods", l, i))

        def link(dve, ins):
            ins.then_inc(*vector.mark("chain"))
            dve.wait_ge(*vector.now("chain"))

        def link_s(act, ins):
            ins.then_inc(*scalar.mark("chain"))
            act.wait_ge(*scalar.now("chain"))

        def squared(T, tag, k):
            o = 0 if tag[0] == "m2" else 8192 - KD * T
            return arena[:, o + k * T:o + (k + 1) * T]

        def squares_scalar(act, T, tag, k, made):
            act.wait_ge(*made)
            SC.activation(squared(T, tag, k), x[:, k, 0:T], ACT.Square).then_inc(*scalar.mark("squares", tag, k))

        mean_bank = [None]

        def mean_tensor(pe, T, tag, k):
            if k == 0:
                mean_bank[0] = take(pe, "mean", tag)
            pe.wait_ge(*scalar.at("squares", tag, k))
            last = mm(mean_bank[0][:, 0:T], ones, squared(T, tag, k), k, KD)
            if k == KD - 1:
                last.then_inc(*tensor.mark("mean", tag))

        def root_scalar(act, T, tag):
            out_scalar(act, rstd[:, 0:T], bank("mean", tag)[:, 0:T], "mean", tag, func=ACT.Sqrt, scale=1.0 / D, bias=eps)

        def modulate_scalar(act, T, tag, gain, shift):
            for k in range(KD):
                act.wait_ge(*vector.at("unit", tag, k))
                for s in range(T // S):
                    a = h[:, k, s * S:(s + 1) * S]
                    SC.activation(a, a, ACT.Identity, scale=gain(s, k), bias=shift(s, k)).then_inc(*scalar.mark("normed", tag, k))

        def unit_vector(dve, T, tag, gain=None, dst=None):
            dve.wait_ge(*scalar.at("mean", tag))
            link(dve, V.reciprocal(rstd[:, 0:T], rstd[:, 0:T]))
            for k in range(KD):
                if gain is None:
                    V.tensor_tensor(h[:, k, 0:T], x[:, k, 0:T], rstd[:, 0:T], ALU.mult).then_inc(*vector.mark("unit", tag, k))
                else:
                    V.scalar_tensor_tensor((h if dst is None else dst)[:, k, 0:T], x[:, k, 0:T], gain(k), rstd[:, 0:T], ALU.mult, ALU.mult)\
                     .then_inc(*vector.mark("normed", tag, k))

        gcol = stat[:, 0:16].rearrange("p (k s) -> p k s", s=2)

        def modulation(l, sh):
            return (lambda s, k: gcol[:, k, s:s + 1]), (lambda s, k: mods[:, l, sh + k, s:s + 1])

        def modulation_vector(dve, l, gname, sc):
            link(dve, V.scalar_tensor_tensor(gcol, mods[:, l, sc:sc + 8, :], 1.0,
                                             vc(gname, 8 * l, 8).unsqueeze(2).broadcast_to((P, 8, 2)), ALU.add, ALU.mult))

        def project_tensor(pe, w, c0, n, T, key, parts=None, fresh=None):
            b = take(pe, *key)
            ps = b[parts if parts else slice(0, n), 0:T]
            for k in range(KD):
                if fresh:
                    pe.wait_ge(*got("normed", fresh, k))
                last = mm(ps, w[:, k, c0:c0 + n], h[:, k, 0:T], k, KD)
            last.then_inc(*tensor.mark(*key))

        def out_vector(dve, dst, src, *key):
            dve.wait_ge(*tensor.at(*key))
            V.tensor_copy(dst, src).then_inc(*vector.mark(*key))

        def out_scalar(act, dst, src, *key, func=ACT.Copy, **kw):
            act.wait_ge(*tensor.at(*key))
            SC.activation(dst, src, func, **kw).then_inc(*scalar.mark(*key))

        def rotate_tensor(pe, q, rot, K, key):
            b = take(pe, *key)
            mm(b[K, 0:S], rot, q, 0, 1).then_inc(*tensor.mark(*key))

        def rotate_vector(dve, q, cos, sin, K, key):
            dve.wait_ge(*tensor.at(*key))
            ps = bank(*key)[K, 0:S]
            V.tensor_tensor(ps, ps, sin, ALU.mult).then_inc(*vector.mark("chain"))
            link(dve, V.tensor_tensor(q, q, cos, ALU.mult))
            V.tensor_tensor(q, q, ps, ALU.add).then_inc(*vector.mark(*key))

        def attend_tensor(pe, heads, prob, probT, tag, between=None):
            def scores(i):
                q, keys, nk = heads[i][0:3]
                for j in range(2):
                    b = take(pe, "scores", tag, i, j)
                    mm(b[:, 0:nk], q(j), keys, 0, 1).then_inc(*tensor.mark("scores", tag, i, j))

            def values(i):
                nk, vals, parts = heads[i][2:5]
                n = nk // P
                for j in range(2):
                    pe.wait_ge(*vector.at("probs", tag, i, j))
                    b = take(pe, "turned_probs", tag, i, j)
                    for k in range(n):
                        last = PE.transpose(b[:, k * P:(k + 1) * P], prob[i % 2][:, j, k * P:(k + 1) * P], ident)
                    last.then_inc(*tensor.mark("turned_probs", tag, i, j))
                b = take(pe, "attended", tag, i)
                for j in range(2):
                    pe.wait_ge(*got("turned_probs", tag, i, j))
                for k in range(n):
                    last = mm(b[parts, 0:S], vals(k), probT[i % 2][:, k, :], k, n)
                last.then_inc(*tensor.mark("attended", tag, i))

            scores(0)
            for i in range(len(heads) + 1):
                if i + 1 < len(heads):
                    scores(i + 1)
                if between:
                    between(i)
                if i:
                    values(i - 1)

        def attend_vector(dve, heads, prob, probT, tag, between=None):
            def stats(i):
                nk, mask, sink, scale = heads[i][2], heads[i][6], heads[i][7], heads[i][8]
                mx, nm, es = (stat[:, 32 + 8 * (i % 2) + 2 * n:34 + 8 * (i % 2) + 2 * n] for n in range(3))
                for j in range(2):
                    dve.wait_ge(*tensor.at("scores", tag, i, j))
                    b = bank("scores", tag, i, j)
                    if mask is not None:
                        link(dve, V.tensor_tensor(b[:, 0:S], b[:, 0:S], mask[:, j, :], ALU.add))
                    V.reduce_max(mx[:, j:j + 1], b[:, 0:nk], AX).then_inc(*vector.mark("chain"))
                dve.wait_ge(*vector.now("chain"))
                sk = sink.broadcast_to((P, 2))
                link(dve, V.scalar_tensor_tensor(mx, mx, scale, sk, ALU.mult, ALU.max))
                V.tensor_scalar(nm, mx, -1.0, None, ALU.mult).then_inc(*vector.mark("chain"))
                V.tensor_tensor(es, sk, mx, ALU.subtract).then_inc(*vector.mark("maxima", tag, i))

            def normalise(i):
                nk = heads[i][2]
                es, sm = (stat[:, 32 + 8 * (i % 2) + 2 * n:34 + 8 * (i % 2) + 2 * n] for n in (2, 3))
                dve.wait_ge(*scalar.at("sink", tag, i))
                link(dve, V.tensor_tensor(sm, sm, es, ALU.add))
                link(dve, V.reciprocal(sm, sm))
                for j in range(2):
                    pr = prob[i % 2][:, j, 0:nk]
                    V.tensor_scalar(pr, pr, sm[:, j:j + 1], None, ALU.mult).then_inc(*vector.mark("probs", tag, i, j))
                out_turned(i, 1)

            def out_turned(i, j):
                n = heads[i][2] // P
                out_vector(dve, probT[i % 2][:, 0:n, j * P:(j + 1) * P],
                           bank("turned_probs", tag, i, j)[:, 0:n * P].rearrange("p (k q) -> p k q", k=n),
                           "turned_probs", tag, i, j)

            for i in range(len(heads) + 1):
                if i < len(heads):
                    stats(i)
                if between:
                    between(i)
                if i:
                    normalise(i - 1)

        def attend_scalar(act, heads, prob, probT, tag, between=None):
            def exps(i):
                nk, scale = heads[i][2], heads[i][8]
                nm, es, sm = (stat[:, 32 + 8 * (i % 2) + 2 * n:34 + 8 * (i % 2) + 2 * n] for n in (1, 2, 3))
                act.wait_ge(*vector.at("maxima", tag, i))
                if i >= 2:
                    act.wait_ge(*tensor.at("turned_probs", tag, i - 2, 1))
                for j in range(2):
                    SC.activation(prob[i % 2][:, j, 0:nk], bank("scores", tag, i, j)[:, 0:nk], ACT.Exp,
                                  bias=nm[:, j:j + 1], scale=scale, accum_out=sm[:, j:j + 1])\
                      .then_inc(*scalar.mark("scores", tag, i, j))
                SC.activation(es, es, ACT.Exp).then_inc(*scalar.mark("sink", tag, i))

            def outs(i):
                nk, parts, dst = heads[i][2], heads[i][4], heads[i][5]
                n = nk // P
                out_scalar(act, probT[i % 2][:, 0:n, 0:P],
                           bank("turned_probs", tag, i, 0)[:, 0:n * P].rearrange("p (k q) -> p k q", k=n),
                           "turned_probs", tag, i, 0)
                out_scalar(act, dst, bank("attended", tag, i)[parts, 0:S], "attended", tag, i)

            for i in range(len(heads) + 1):
                if i < len(heads):
                    exps(i)
                if between:
                    between(i)
                if i:
                    outs(i - 1)

        bcu, k96, cv = tiles(0, 6, 512), tiles(0, 6, 512), tiles(3072, 2, 512)
        swaq, kd, q96, vall = tiles(4096, 3, 512), tiles(5632, 2, 512), tiles(6656, 6, 512), tiles(9728, 4, 512)
        prob1 = [tiles(11776, 2, 512), tiles(12800, 2, 512)]
        probT1 = [tiles(13824, 4, 256), tiles(14848, 4, 256)]
        cq, ckv, swak, swav = tiles(11776, 2, 512), tiles(12800, 1, 512), tiles(13312, 1, 512), tiles(13824, 1, 512)
        sq, krb = tiles(14336, 3, 512), tiles(15872, 1, 512)
        LO, HI = slice(0, 64), slice(64, 96)
        mix = h
        z = q96[:, 0:3, :].rearrange("p a b -> p (a b)")[:, 0:2 * 2 * (S + 2)].rearrange("p (c s t) -> p c s t", c=2, s=2)

        def in_list(l):
            TQ = T2 if l < L - 1 else S
            return [
                [(i * P, P, TQ, bcu[:, 2 + i, 0:TQ], None) for i in range(4)],
                [(0, P, T2, swav[:, 0, :], None)] + [(P + i * P, P, TQ, bcu[:, i, 0:TQ], None) for i in range(2)],
                [(i * P, P, TQ, cq[:, i, 0:TQ], None) for i in range(2)] + [(256, P, T2, ckv[:, 0, :], None),
                                                                            (384, 32, T2, krb[HI, 0, :], HI)],
                [(i * P, P, TQ, swaq[:, i, 0:TQ], None) for i in range(3)] + [(384, P, T2, swak[:, 0, :], None)],
            ]

        def head_list(l, s):
            k0, nk = (0, T2) if s == 0 else (S, S)
            window = C("window").rearrange("p (a t) -> p a t", a=2)
            heads = []
            for hd in range(12):
                o = 64 * (hd % 2)
                parts = slice(o, o + 64)
                if hd < 6:
                    q = lambda j, hd=hd: q96[0:96, hd, s * S + j * P:s * S + j * P + P]
                    keys = k96[0:96, hd, k0:k0 + nk]
                    vals = lambda k, hd=hd: vall[:, k + 2 * s, 64 * hd:64 * hd + 64]
                else:
                    q = lambda j, hd=hd, parts=parts: swaq[parts, hd // 2 - 3, s * S + j * P:s * S + j * P + P]
                    keys = kd[parts, (hd - 6) // 3, k0:k0 + nk]
                    vals = lambda k, hd=hd: vall[:, k + 2 * s, 384 + 64 * ((hd - 6) // 3):448 + 64 * ((hd - 6) // 3)]
                heads.append((q, keys, nk, vals, parts, mix[parts, hd // 2, s * S:(s + 1) * S],
                              window if hd >= 6 and s == 0 else None, sinkb[:, l, hd:hd + 1],
                              MLA_SCALE if hd < 6 else HEAD_SCALE))
            return heads

        ROT_MLA = (C("rot_mla")[0:96, 0:96], C("cos_mla")[0:96, :], C("sin_mla")[0:96, :])

        def hybrid_tensor(pe, l):
            TQ = T2 if l < L - 1 else S
            for c, chunk in enumerate(in_list(l)):
                w = next_weights(pe)
                for i, (c0, n, T, dst, parts) in enumerate(chunk):
                    project_tensor(pe, w, c0, n, T, ("projected", l, c, i), parts, ("n1", l) if c == i == 0 else None)
                chunk_read()
                for i in ada_after(l, c):
                    rows_tensor(pe, 0, i)
                    ada_tensor(pe, 0, i)
            if l == 0:
                pe.wait_ge(late_loaded, 16 * (1 + len(late_list)))
            join(tensor, pe, ("in", l))
            b = take(pe, "values", l)
            for j in range(4):
                last = PE.transpose(b[:, j * P:(j + 1) * P], swav[:, 0, j * P:(j + 1) * P], ident)
            last.then_inc(*tensor.mark("values", l))
            for g in range(2):
                b = take(pe, "keys", l, g)
                mm(b[:, :], C(f"dup{g}"), swak[:, 0, :], 0, 1).then_inc(*tensor.mark("keys", l, g))
                b = take(pe, "keys_rot", l, g)
                mm(b[:, 0:S], C(f"duprot{g}"), swak[:, 0, 0:S], 0, 1).then_inc(*tensor.mark("keys_rot", l, g))
            for i in range(3):
                rotate_tensor(pe, swaq[:, i, 0:S], C("rot_swa"), slice(0, P), ("rot", l, "swa", i))
            rotate_tensor(pe, krb[HI, 0, 0:S], C("rot_mla")[HI, 64:96], HI, ("rot", l, "kr"))
            for name, n, T, o in (("q", 2, TQ, 0), ("kv", 1, T2, 2)):
                pe.wait_ge(*scalar.at("squares", l, name))
                b = take(pe, "mean", l, name)
                for k in range(n):
                    last = mm(b[:, 0:T], ones, sq[:, o + k, 0:T], k, n)
                last.then_inc(*tensor.mark("mean", l, name))
            pe.wait_ge(*vector.at("latent", l, "q"))
            for i in range(H1):
                b = take(pe, "q96", l, i)
                for k in range(2):
                    last = mm(b[0:96, 0:TQ], uq[:, l, k, 96 * i:96 * i + 96], cq[:, k, 0:TQ], k, 2)
                last.then_inc(*tensor.mark("q96", l, i))
            pe.wait_ge(*vector.at("latent", l, "kv"))
            for i in range(H1):
                b = take(pe, "k96", l, i)
                mm(b[LO, :], ukv[:, l, 128 * i:128 * i + 64], ckv[:, 0, :], 0, 1).then_inc(*tensor.mark("k96", l, i))
            wv = ukv[:, l, :].rearrange("p (h a) -> p h a", a=P)[:, :, 64:128]
            for j in range(4):
                b = take(pe, "v_mla", l, j)
                mm(b[:, 0:384], ckv[:, 0, j * P:(j + 1) * P], wv, 0, 1).then_inc(*tensor.mark("v_mla", l, j))
            for i in range(H1):
                pe.wait_ge(*got("q96", l, i))
                rotate_tensor(pe, q96[0:96, i, 0:S], ROT_MLA[0], slice(0, 96), ("rot", l, "q", i))
            join(tensor, pe, ("heads", l))
            def ada(i):
                if l == 0 and i:
                    ada_tensor(pe, 1, i - 1)
                if l == 0 and i < ADA_LATE:
                    rows_tensor(pe, 1, i)

            attend_tensor(pe, head_list(l, 0), prob1, probT1, ("lat", l), ada)
            join(tensor, pe, ("lat_done", l))
            if l < L - 1:
                attend_tensor(pe, head_list(l, 1), prob1, probT1, ("ctx", l))
                join(tensor, pe, ("ctx_done", l))
            for i in range(2):
                w = next_weights(pe)
                for m in range(4):
                    b = take(pe, "out", l, 4 * i + m)
                    for k in range(KD):
                        last = mm(b[:, 0:TQ], w[:, k, m * P:(m + 1) * P], mix[:, k, 0:TQ], k, KD)
                    last.then_inc(*tensor.mark("out", l, 4 * i + m))
                    if 4 * i + m >= 2:
                        mean_tensor(pe, TQ, ("n2", l), 4 * i + m - 2)
                chunk_read()
            for k in (KD - 2, KD - 1):
                mean_tensor(pe, TQ, ("n2", l), k)
            join(tensor, pe, ("mixed", l))

        def hybrid_vector(dve, l):
            TQ = T2 if l < L - 1 else S
            NS = TQ // S
            modulation_vector(dve, l, "norm1_g", 8)
            unit_vector(dve, T2, ("n1", l))
            lists = in_list(l)

            def outs(c):
                for i, (c0, n, T, dst, parts) in enumerate(lists[c]):
                    if i % 2:
                        src = bank("projected", l, c, i)[parts if parts else slice(0, n), 0:T]
                        out_vector(dve, dst, src, "projected", l, c, i)
                for i in ada_after(l, c):
                    ada_vector(dve, 0, i)

            outs(0)
            outs(1)
            dve.wait_ge(*vector.now("projected"))
            dve.wait_ge(*scalar.at("projected", l, 1, 2))
            link(dve, V.memset(z, 0.0))
            for c in range(2):
                halves = [bcu[:, i + c, 0:TQ].rearrange("p (s t) -> p s t", s=NS) for i in (2, 4)]
                link(dve, V.tensor_tensor(z[:, c, 0:NS, 1:S + 1], halves[0], halves[1], ALU.mult))
                y = cv[:, c, 0:TQ].rearrange("p (s t) -> p s t", s=NS)
                link(dve, V.tensor_scalar(y, z[:, c, 0:NS, 0:S], vc("conv_w", 6 * l + c), None, ALU.mult))
                for tap in (1, 2):
                    link(dve, V.scalar_tensor_tensor(y, z[:, c, 0:NS, tap:tap + S], vc("conv_w", 6 * l + 2 * tap + c), y,
                                                     ALU.mult, ALU.add))
                link(dve, V.tensor_tensor(cv[:, c, 0:TQ], cv[:, c, 0:TQ], bcu[:, c, 0:TQ], ALU.mult))
            outs(2)
            outs(3)
            if l == 0:
                dve.wait_ge(late_loaded, 16 * (1 + len(late_list)))
            join(vector, dve, ("in", l))
            out_vector(dve, vall[:, :, 384:512], bank("values", l)[:, :].rearrange("p (j c) -> p j c", j=4), "values", l)
            for g in range(2):
                a, r = bank("keys", l, g), bank("keys_rot", l, g)
                dve.wait_ge(*tensor.at("keys", l, g))
                link(dve, V.tensor_tensor(kd[:, g, 0:S], a[:, 0:S], C("cos_swa"), ALU.mult))
                V.tensor_copy(kd[:, g, S:T2], a[:, S:T2]).then_inc(*vector.mark("keys", l, g))
                dve.wait_ge(*tensor.at("keys_rot", l, g))
                link(dve, V.tensor_tensor(r[:, 0:S], r[:, 0:S], C("sin_swa"), ALU.mult))
                V.tensor_tensor(kd[:, g, 0:S], kd[:, g, 0:S], r[:, 0:S], ALU.add).then_inc(*vector.mark("keys_rot", l, g))
            for i in range(3):
                rotate_vector(dve, swaq[:, i, 0:S], C("cos_swa"), C("sin_swa"), slice(0, P), ("rot", l, "swa", i))
            rotate_vector(dve, krb[HI, 0, 0:S], C("cos_mla")[HI, :], C("sin_mla")[HI, :], HI, ("rot", l, "kr"))
            for name, src, n, T, gname in (("q", cq, 2, TQ, "mla_q_norm_g"), ("kv", ckv, 1, T2, "mla_kv_norm_g")):
                dve.wait_ge(*tensor.at("mean", l, name))
                link(dve, V.tensor_scalar(rstd[:, 0:T], bank("mean", l, name)[:, 0:T], 1.0 / (n * P), EPS, ALU.mult, ALU.add))
                V.reciprocal(rstd[:, 0:T], rstd[:, 0:T]).then_inc(*vector.mark("mean", l, name))
                dve.wait_ge(*scalar.at("root", l, name))
                for i in range(n):
                    V.scalar_tensor_tensor(src[:, i, 0:T], src[:, i, 0:T], vc(gname, n * l + i), rstd[:, 0:T],
                                           ALU.mult, ALU.mult).then_inc(*vector.mark("latent", l, name))
                dve.wait_ge(*vector.now("latent"))
            for i in range(0, H1, 2):
                out_vector(dve, q96[0:96, i, 0:TQ], bank("q96", l, i)[0:96, 0:TQ], "q96", l, i)
            for i in range(0, H1, 2):
                out_vector(dve, k96[LO, i, :], bank("k96", l, i)[LO, :], "k96", l, i)
            for j in range(0, 4, 2):
                out_vector(dve, vall[:, j, 0:384], bank("v_mla", l, j)[:, 0:384], "v_mla", l, j)
            for i in range(H1):
                dve.wait_ge(*got("q96", l, i))
                rotate_vector(dve, q96[0:96, i, 0:S], ROT_MLA[1], ROT_MLA[2], slice(0, 96), ("rot", l, "q", i))
            join(vector, dve, ("heads", l))
            attend_vector(dve, head_list(l, 0), prob1, probT1, ("lat", l),
                          lambda i: ada_vector(dve, 1, i - 1) if l == 0 and i else None)
            join(vector, dve, ("lat_done", l))
            if l < L - 1:
                attend_vector(dve, head_list(l, 1), prob1, probT1, ("ctx", l))
                join(vector, dve, ("ctx_done", l))
            for d in range(KD):
                dve.wait_ge(*tensor.at("out", l, d))
                for s in range(NS):
                    xs = x[:, d, s * S:(s + 1) * S]
                    V.scalar_tensor_tensor(xs, bank("out", l, d)[:, s * S:(s + 1) * S], mods[:, l, 16 + d, s:s + 1], xs,
                                           ALU.mult, ALU.add).then_inc(*vector.mark("out", l, d))
            join(vector, dve, ("mixed", l))

        def hybrid_scalar(act, l):
            TQ = T2 if l < L - 1 else S
            root_scalar(act, T2, ("n1", l))
            modulate_scalar(act, T2, ("n1", l), *modulation(l, 0))
            for c, chunk in enumerate(in_list(l)):
                for i, (c0, n, T, dst, parts) in enumerate(chunk):
                    if i % 2 == 0:
                        src = bank("projected", l, c, i)[parts if parts else slice(0, n), 0:T]
                        out_scalar(act, dst, src, "projected", l, c, i)
                for i in ada_after(l, c):
                    rows_scalar(act, 0, i)
            join(scalar, act, ("in", l))
            for name, src, n, T, o in (("q", cq, 2, TQ, 0), ("kv", ckv, 1, T2, 2)):
                SC.activation(sq[:, o:o + n, 0:T], src[:, :, 0:T], ACT.Square).then_inc(*scalar.mark("squares", l, name))
            for name, T in (("q", TQ), ("kv", T2)):
                act.wait_ge(*vector.at("mean", l, name))
                SC.activation(rstd[:, 0:T], rstd[:, 0:T], ACT.Sqrt).then_inc(*scalar.mark("root", l, name))
            for i in range(1, H1, 2):
                out_scalar(act, q96[0:96, i, 0:TQ], bank("q96", l, i)[0:96, 0:TQ], "q96", l, i)
            for i in range(1, H1, 2):
                out_scalar(act, k96[LO, i, :], bank("k96", l, i)[LO, :], "k96", l, i)
            for j in range(1, 4, 2):
                out_scalar(act, vall[:, j, 0:384], bank("v_mla", l, j)[:, 0:384], "v_mla", l, j)
            act.wait_ge(*vector.at("rot", l, "kr"))
            for i in range(H1):
                SC.activation(k96[HI, i, :], krb[HI, 0, :], ACT.Copy).then_inc(*scalar.mark("chain"))
            join(scalar, act, ("heads", l))
            attend_scalar(act, head_list(l, 0), prob1, probT1, ("lat", l),
                          lambda i: rows_scalar(act, 1, i) if l == 0 and i < ADA_LATE else None)
            SC.activation(mix[:, 6:8, 0:TQ], cv[:, :, 0:TQ], ACT.Copy).then_inc(*scalar.mark("chain"))
            join(scalar, act, ("lat_done", l))
            if l < L - 1:
                attend_scalar(act, head_list(l, 1), prob1, probT1, ("ctx", l))
                join(scalar, act, ("ctx_done", l))
            for d in range(KD):
                squares_scalar(act, TQ, ("n2", l), d, vector.at("out", l, d))
            join(scalar, act, ("mixed", l))

        xg = arena[:, 0:8192].rearrange("p (k e c) -> p k e c", k=KD, e=NE)
        htok = arena[:, 8192:12288].rearrange("p (j d) -> p j d", j=4)
        sel = arena[:, 12288:14336].rearrange("p (s j e c) -> p s j e c", s=2, j=2, e=NE)
        aff = arena[:, 14336:14400].rearrange("p (j s e) -> p j s e", j=2, s=2)
        posT = arena[:, 14400:14464].rearrange("p (j s e) -> p j s e", j=2, s=2)
        affT, work, pos = (arena[0:32, 14464 + 256 * i:14720 + 256 * i] for i in range(3))
        m8 = arena[0:32, 15232:15240]
        scat = h[:, 0:4, :].rearrange("p a b -> p (a b)").rearrange("p (s g t) -> p s g t", s=2, g=4)
        yst = arena[:, 8192:16384].rearrange("p (s g d) -> p s g d", s=2, g=4)
        hid1, hidT = h[:, 4, :].rearrange("p (i f) -> p i f", i=2), h[:, 5, :].rearrange("p (i b n) -> p i b n", i=2, b=2)
        xe = h[:, 6:8, :].rearrange("p i (k c) -> p i k c", k=KD)
        GB, UB, YB, TB = (0, 4), (1, 5), (2, 6), (3, 7)
        xe_ready, gate_made, up_made, down_made = sem("xe_ready"), sem("gate_made"), sem("up_made"), sem("down_made")
        silu_done, hid_done, turned_made, turned_out = sem("silu_done"), sem("hid_done"), sem("turned_made"), sem("turned_out")
        half_out = sem("half_out_scalar"), sem("half_out_vector")
        counted_ahead, AHEAD = (up_made, down_made, turned_made), 2

        def after_moe(l):
            return ("n1", l + 1) if l < L - 1 else "final1"

        def moe_tensor(pe, l):
            NS = 2 if l < L - 1 else 1
            T, CS = NS * S, NS * CAP
            b = take(pe, "router", l)
            for s in range(NS):
                for j in range(2):
                    o = 32 * j + 16 * s
                    for k in range(KD):
                        pe.wait_ge(*got("normed", ("n2", l), k))
                        last = mm(b[:, o:o + 16], h[:, k, s * S + j * P:s * S + j * P + P], rtr[:, l, k, :], k, KD)
            last.then_inc(*tensor.mark("router", l))
            for j in range(2 * NS):
                for half in range(2):
                    b = take(pe, "htok", l, j, half)
                    for k in range(4):
                        last = PE.transpose(b[:, k * P:(k + 1) * P], h[:, 4 * half + k, j * P:(j + 1) * P], ident)
                    last.then_inc(*tensor.mark("htok", l, j, half))
            pe.wait_ge(*vector.at("aff", l))
            b = take(pe, "affT", l)
            for j in range(2):
                last = PE.transpose(b[0:32, j * P:(j + 1) * P], aff[:, j].rearrange("p s e -> p (s e)"), ident)
            last.then_inc(*tensor.mark("affT", l))
            pe.wait_ge(*vector.at("pos", l))
            b = take(pe, "posT", l)
            for j in range(2):
                last = PE.transpose(b[:, j * 32:(j + 1) * 32], pos[:, j * P:(j + 1) * P], ident[0:32, 0:32])
            last.then_inc(*tensor.mark("posT", l))
            pe.wait_ge(*scalar.at("htok", l, 2 * NS - 1, 1))
            for s in range(NS):
                pe.wait_ge(*vector.at("sel", l, s, 1))
                for k in range(KD):
                    b = take(pe, "xg", l, s, k)
                    for j in range(2):
                        last = mm(b[:, :], htok[:, 2 * s + j, k * P:(k + 1) * P], sel[:, s, j].rearrange("p e c -> p (e c)"), j, 2)
                    last.then_inc(*tensor.mark("xg", l, s, k))
            for s in range(NS):
                for g in range(4):
                    sp = C("spread")[0:32, (4 * s + g) * P:(4 * s + g + 1) * P]
                    b = take(pe, "slot_of", l, s, g)
                    mm(b[:, 0:S], sp, pos, 0, 1).then_inc(*tensor.mark("slot_of", l, s, g))
                    b = take(pe, "weight_of", l, s, g)
                    mm(b[:, 0:S], sp, affT, 0, 1).then_inc(*tensor.mark("weight_of", l, s, g))
            join(tensor, pe, ("gathered", l))
            n0 = expert_chunk[l]
            assert at[0] == n0
            with pe.Fori(0, NE // 4) as g:
                for q in range(4):
                    e = NE * l + q
                    pe.wait_ge(xe_ready, e + 1 + 4 * g)
                    pe.wait_ge(hid_done, e + 1 + 4 * g)
                    for c, (B, made) in enumerate(((GB, gate_made), (UB, up_made))):
                        n = n0 + 3 * q + c
                        pe.wait_ge(loaded[n % RING], 16 * (n // RING + 1) + (16 * 12 // RING) * g)
                        for k in range(KD):
                            for hf_ in range(2):
                                last = mm(banks[B[q % 2]][64 * hf_:64 * hf_ + 64, 0:256], xe[:, q % 2, k, :],
                                          slot(n)[:, k, hf_ * 256:(hf_ + 1) * 256], k, KD)
                        last.then_inc(made, 1)
                    pe.wait_ge(hid_done, e + 1 + AHEAD + 4 * g)
                    for b in range(2):
                        last = PE.transpose(banks[TB[q % 2]][:, b * P:(b + 1) * P], hid1[:, q % 2, b * P:(b + 1) * P], ident)
                    last.then_inc(turned_made, 1)
                    n = n0 + 3 * q + 2
                    pe.wait_ge(loaded[n % RING], 16 * (n // RING + 1) + (16 * 12 // RING) * g)
                    pe.wait_ge(turned_out, e + 1 + 4 * g)
                    for half in range(2):
                        pe.wait_ge(half_out[half], e + 1 + 4 * g)
                    for f in range(4):
                        for half in range(2):
                            last = mm(banks[YB[q % 2]][64 * half:64 * half + 64, :], hidT[:, q % 2, f % 2, 64 * (f // 2):64 * (f // 2) + 64],
                                      slot(n)[:, f, half * 512:(half + 1) * 512], f, 4)
                    last.then_inc(down_made, 1)
            at[0] += 3 * NE
            for i in range(2):
                pe.wait_ge(half_out[i], NE * (l + 1) + AHEAD)
            for b in range(8):
                holder[b] = None
            for s in range(NS):
                for d in range(KD):
                    b = take(pe, "scattered", l, s, d)
                    for g in range(4):
                        last = mm(b[:, 0:S], yst[:, s, g, d * P:(d + 1) * P], scat[:, s, g, :], g, 4)
                    last.then_inc(*tensor.mark("scattered", l, s, d))
                    if s == NS - 1 and d >= 2:
                        mean_tensor(pe, NS * S, after_moe(l), d - 2)
            for k in (KD - 2, KD - 1):
                mean_tensor(pe, NS * S, after_moe(l), k)
            join(tensor, pe, ("moe", l))

        def moe_vector(dve, l):
            NS = 2 if l < L - 1 else 1
            CS = NS * CAP
            modulation_vector(dve, l, "norm2_g", 32)
            unit_vector(dve, NS * S, ("n2", l))
            if NS == 1:
                link(dve, V.memset(aff, 0.0))
            dve.wait_ge(*tensor.at("router", l))
            lg = bank("router", l)[:, 0:64].rearrange("p (j s e) -> p j s e", j=2, s=2)
            mx = stat[:, 32:36].rearrange("p (j s) -> p j s", j=2)
            for s in range(NS):
                a = aff[:, :, s, :]
                link(dve, V.tensor_reduce(mx[:, :, s:s + 1], lg[:, :, s, :], AX, ALU.max))
                V.tensor_tensor(a, lg[:, :, s, :], mx[:, :, s:s + 1].broadcast_to((P, 2, NE)), ALU.subtract)\
                 .then_inc(*vector.mark("router", l))
                book.new[("vector", "shifted", l, s)] = vector.n["router"]
            for s in range(NS):
                a = aff[:, :, s, :]
                dve.wait_ge(*scalar.at("aff_exp", l, s))
                link(dve, V.tensor_reduce(mx[:, :, s:s + 1], a, AX, ALU.add))
                link(dve, V.reciprocal(mx[:, :, s:s + 1], mx[:, :, s:s + 1]))
                V.tensor_tensor(a, a, mx[:, :, s:s + 1].broadcast_to((P, 2, NE)), ALU.mult).then_inc(*vector.mark("aff", l))
            dve.wait_ge(*tensor.at("affT", l))
            V.tensor_copy(affT, bank("affT", l)[0:32, 0:S]).then_inc(*vector.mark("chain"))
            V.tensor_copy(work, bank("affT", l)[0:32, 0:S]).then_inc(*vector.mark("affT", l))
            dve.wait_ge(*vector.now("affT"))
            for r in range(CAP // 8):
                link(dve, V.max(m8, work))
                link(dve, V.match_replace(work, m8, work, -1.0))
            link(dve, V.tensor_scalar(work, work, 0.0, None, ALU.is_lt))
            link(dve, V.tensor_tensor_scan(pos, ones[0:32, 0:1].broadcast_to((32, S)), work, 0.0, ALU.mult, ALU.add))
            V.tensor_tensor(pos, pos, work, ALU.mult).then_inc(*vector.mark("pos", l))
            out_vector(dve, posT.rearrange("p j s e -> p (j s e)"), bank("posT", l)[:, 0:64], "posT", l)
            dve.wait_ge(*vector.now("posT"))
            for s in range(NS):
                for j in range(2):
                    V.tensor_tensor(sel[:, s, j], posT[:, j, s, :].unsqueeze(2).broadcast_to((P, NE, CAP)),
                                    C("slots").unsqueeze(1).broadcast_to((P, NE, CAP)), ALU.is_equal)\
                     .then_inc(*vector.mark("sel", l, s, j))
            for s in range(NS):
                for k in range(0, KD, 2):
                    out_vector(dve, xg[:, k, :, s * CAP:(s + 1) * CAP],
                               bank("xg", l, s, k)[:, :].rearrange("p (e c) -> p e c", e=NE), "xg", l, s, k)
            dve.wait_ge(*tensor.at("xg", l, NS - 1, KD - 1))
            for s in range(NS):
                for gr in range(4):
                    o = scat[:, s, gr, :]
                    dve.wait_ge(*tensor.at("slot_of", l, s, gr))
                    V.tensor_scalar(o, bank("slot_of", l, s, gr)[:, 0:S], C("slot"), None, ALU.is_equal)\
                     .then_inc(*vector.mark("slot_of", l, s, gr))
                    dve.wait_ge(*vector.now("slot_of"))
                    dve.wait_ge(*tensor.at("weight_of", l, s, gr))
                    V.tensor_tensor(o, o, bank("weight_of", l, s, gr)[:, 0:S], ALU.mult).then_inc(*vector.mark("weight_of", l, s, gr))
            join(vector, dve, ("gathered", l))
            with dve.Fori(0, NE // 4) as g:
                for q in range(4):
                    e = NE * l + q
                    dve.wait_ge(silu_done, e + 1 + 4 * g)
                    dve.wait_ge(up_made, e + 1 + AHEAD + 4 * g)
                    V.tensor_tensor(hid1[:, q % 2], hid1[:, q % 2], banks[UB[q % 2]][:, 0:256], ALU.mult).then_inc(hid_done, 1)
                    dve.wait_ge(turned_made, e + 1 + AHEAD + 4 * g)
                    dve.wait_ge(down_made, e + 1 + 4 * g)
                    V.tensor_copy(hidT[:, q % 2].rearrange("p b n -> p (b n)"), banks[TB[q % 2]][:, 0:256]).then_inc(turned_out, 1)
                    dve.wait_ge(down_made, e + 1 + AHEAD + 4 * g)
                    for s in range(NS):
                        ins = V.tensor_copy(yst[32 * q:32 * q + 32, s, bass.ds(g, 1), 512:1024].rearrange("p g d -> p (g d)"),
                                            banks[YB[q % 2]][64 + s * CAP:64 + (s + 1) * CAP, :])
                    ins.then_inc(half_out[1], 1)
            for s in range(NS):
                for d in range(KD):
                    dve.wait_ge(*tensor.at("scattered", l, s, d))
                    xs = x[:, d, s * S:(s + 1) * S]
                    V.scalar_tensor_tensor(xs, bank("scattered", l, s, d)[:, 0:S], mods[:, l, 40 + d, s:s + 1], xs,
                                           ALU.mult, ALU.add).then_inc(*vector.mark("scattered", l, s, d))
            join(vector, dve, ("moe", l))

        def moe_scalar(act, l):
            NS = 2 if l < L - 1 else 1
            CS = NS * CAP
            root_scalar(act, NS * S, ("n2", l))
            modulate_scalar(act, NS * S, ("n2", l), *modulation(l, 24))
            for s in range(NS):
                a = aff[:, :, s, :]
                act.wait_ge(vector.sem("router"), book.old.get(("vector", "shifted", l, s), 1))
                SC.activation(a, a, ACT.Exp).then_inc(*scalar.mark("aff_exp", l, s))
            for j in range(2 * NS):
                for half in range(2):
                    out_scalar(act, htok[:, j, half * 512:(half + 1) * 512], bank("htok", l, j, half)[:, :], "htok", l, j, half)
            for s in range(NS):
                for k in range(1, KD, 2):
                    out_scalar(act, xg[:, k, :, s * CAP:(s + 1) * CAP],
                               bank("xg", l, s, k)[:, :].rearrange("p (e c) -> p e c", e=NE), "xg", l, s, k)
            join(scalar, act, ("gathered", l))
            with act.Fori(0, NE // 4) as g:
                for q in range(4):
                    e = NE * l + q
                    act.wait_ge(gate_made, e + 1 + 4 * g)
                    act.wait_ge(turned_made, e + 1 + 4 * g)
                    SC.activation(hid1[:, q % 2], banks[GB[q % 2]][:, 0:256], ACT.Silu).then_inc(silu_done, 1)
                    act.wait_ge(down_made, e + 1 + AHEAD + 4 * g)
                    for s in range(NS):
                        ins = SC.activation(yst[32 * q:32 * q + 32, s, bass.ds(g, 1), 0:512].rearrange("p g d -> p (g d)"),
                                            banks[YB[q % 2]][s * CAP:(s + 1) * CAP, :], ACT.Copy)
                    ins.then_inc(half_out[0], 1)
            for d in range(KD):
                squares_scalar(act, NS * S, after_moe(l), d, vector.at("scattered", l, NS - 1, d))
            join(scalar, act, ("moe", l))

        def moe_pool(pool, l):
            n = (2 if l < L - 1 else 1) * CAP
            for s in (tensor, scalar, vector):
                value = s.closed(("gathered", l))
                if value:
                    pool.wait_ge(*value)
            if n < 2 * CAP:
                nc.gpsimd.memset(xe[:, :, :, n:2 * CAP], 0.0)
            with pool.Fori(0, NE // 4) as g:
                for q in range(4):
                    e = NE * l + q
                    pool.wait_ge(up_made, e + 1 + 4 * g)
                    nc.gpsimd.tensor_copy(xe[:, q % 2, :, 0:n], xg[:, :, bass.ds(4 * g + q, 1), 0:n].rearrange("p k e c -> p k (e c)"))\
                      .then_inc(xe_ready, 1)

        o = 0

        def place(n):
            nonlocal o
            a = arena[:, o:o + n]
            o += n
            return a

        def chan():
            return place(512).rearrange("p (c t) -> p c t", c=2)

        gates = place(4096).rearrange("p (n t) -> p n t", n=16)
        ys = [chan() for _ in range(4)]
        raw_r = place(2056).rearrange("p (n t) -> p n t", n=8)
        raw_h = place(2048).rearrange("p (n t) -> p n t", n=8)
        pool0 = o
        raw_s = place(1536).rearrange("p (n t) -> p n t", n=6)
        raw_m = place(1536).rearrange("p (n t) -> p n t", n=6)
        vt_s, vt_m = chan(), chan()
        Zs, Es = place(2048), place(2048)
        prob_m = [place(512).rearrange("p (j n) -> p j n", j=2) for _ in range(2)]
        probT_m = [place(512).rearrange("p (k q) -> p k q", k=2) for _ in range(2)]
        assert o <= AR, (o, AR)
        o = pool0
        NT, AkT, RbT, RkT, Tm, TT, Xm = (place(1024) for _ in range(7))
        sc_d, sc_x = place(1024), place(512)
        assert o <= AR, (o, AR)
        x_hi = [x[:, k, S:T2] for k in range(KD)]

        def wide(t, k):
            return t[:, k:k + 2, S:T2]

        def sl_of(hd):
            return slice(64 * (hd % 2), 64 * (hd % 2) + 64)

        def turn_tensor(pe, src, *key):
            b = take(pe, *key)
            for j in range(2):
                for c in range(2):
                    last = PE.transpose(b[:, j * S + c * P:j * S + (c + 1) * P], src[:, c, j * P:(j + 1) * P], ident)
            last.then_inc(*tensor.mark(*key))

        def halves(b):
            return b[:, :].rearrange("p (j c) -> p j c", j=2)

        def head_sum_tensor(pe, src, *key):
            b = take(pe, *key)
            mm(b[:, :], C("heads"), src, 0, 1).then_inc(*tensor.mark(*key))

        sq_, sk_, sv_ = raw_s[:, 0:2, :], raw_s[:, 2:4, :], raw_s[:, 4:6, :]
        Z4, E4 = (t.rearrange("p (h s t) -> p h s t", h=4, s=2) for t in (Zs, Es))
        Z2, E2 = (t.rearrange("p (h x) -> p h x", h=4) for t in (Zs, Es))

        def stick_tensor(pe, l):
            for hd in range(4):
                b = take(pe, "stick_z", l, hd)
                for st in range(2):
                    last = mm(b[:, st * S:(st + 1) * S], sk_[sl_of(hd), hd // 2, st * P:(st + 1) * P], sq_[sl_of(hd), hd // 2, :], 0, 1)
                last.then_inc(*tensor.mark("stick_z", l, hd))
            turn_tensor(pe, sv_, "stick_v", l)
            yield
            pe.wait_ge(*vector.at("stick_keep", l))
            for hd in range(4):
                b = take(pe, "stick_sum", l, hd)
                mm(b[:, 0:S], C("suffix"), E4[:, hd, 0, :], 0, 2)
                mm(b[:, 0:S], ones, E4[:, hd, 1, :], 1, 2)
                mm(b[:, S:T2], C("suffix"), E4[:, hd, 1, :], 0, 1).then_inc(*tensor.mark("stick_sum", l, hd))
            yield
            pe.wait_ge(*scalar.at("stick_att", l))
            pe.wait_ge(*got("stick_v", l))
            b = take(pe, "stick_y", l)
            for hd in range(4):
                for st in range(2):
                    last = mm(b[sl_of(hd), (hd // 2) * S:(hd // 2 + 1) * S], vt_s[:, st, 64 * hd:64 * hd + 64], Z4[:, hd, st, :], st, 2)
            last.then_inc(*tensor.mark("stick_y", l))
            yield

        def stick_vector(dve, l):
            out_vector(dve, vt_s, halves(bank("stick_v", l)), "stick_v", l)
            dve.wait_ge(*scalar.at("stick_z", l, 3))
            V.scalar_tensor_tensor(Es, Zs, -1.0, Zs, ALU.mult, ALU.max).then_inc(*vector.mark("stick_abs", l))
            yield
            dve.wait_ge(*scalar.at("stick_log", l))
            link(dve, V.scalar_tensor_tensor(Es, Zs, 0.0, Es, ALU.max, ALU.add))
            V.tensor_tensor(E2, E2, C("stick").unsqueeze(1).broadcast_to((P, 4, 512)), ALU.mult).then_inc(*vector.mark("stick_keep", l))
            link(dve, V.tensor_tensor(Z2, Z2, C("stick_add").unsqueeze(1).broadcast_to((P, 4, 512)), ALU.add))
            for hd in range(4):
                dve.wait_ge(*tensor.at("stick_sum", l, hd))
                V.tensor_tensor(Z2[:, hd], Z2[:, hd], bank("stick_sum", l, hd)[:, :], ALU.add).then_inc(*vector.mark("stick_sum", l, hd))
            yield
            out_vector(dve, flat(ys[0]), bank("stick_y", l)[:, :], "stick_y", l)
            yield

        def stick_scalar(act, l):
            for hd in range(4):
                out_scalar(act, Zs[:, hd * 512:(hd + 1) * 512], bank("stick_z", l, hd)[:, :], "stick_z", l, hd, scale=HEAD_SCALE)
            act.wait_ge(*vector.at("stick_abs", l))
            link_s(act, SC.activation(Es, Es, ACT.Exp, scale=-1.0))
            SC.activation(Es, Es, ACT.Ln, bias=1.0).then_inc(*scalar.mark("stick_log", l))
            yield
            act.wait_ge(*vector.at("stick_sum", l, 3))
            SC.activation(Zs, Zs, ACT.Exp).then_inc(*scalar.mark("stick_att", l))
            yield
            yield

        def moba_heads():
            causal = C("causal").rearrange("p (a t) -> p a t", a=2)
            heads = []
            for hd in range(4):
                parts, c = sl_of(hd), hd // 2
                heads.append((lambda j, parts=parts, c=c: raw_m[parts, c, j * P:(j + 1) * P], raw_m[parts, 2 + c, :], S,
                              lambda k, hd=hd: vt_m[:, k, 64 * hd:64 * hd + 64], parts, ys[2][parts, c, :],
                              causal, C("no_sink"), HEAD_SCALE))
            return heads

        def moba_tensor(pe, l, fill):
            turn_tensor(pe, raw_m[:, 4:6, :], "moba_v", l)
            for i in range(4):
                rotate_tensor(pe, raw_m[:, i, :], C("rot_moba"), slice(0, P), ("moba_rot", l, i))
            yield
            pe.wait_ge(*vector.at("moba_rot", l, 3))
            pe.wait_ge(*got("moba_v", l))
            attend_tensor(pe, moba_heads(), prob_m, probT_m, ("moba", l), lambda i: next(fill, None))
            yield
            yield

        def moba_vector(dve, l):
            for i in range(4):
                rotate_vector(dve, raw_m[:, i, :], C("cos_moba"), C("sin_moba"), slice(0, P), ("moba_rot", l, i))
            yield
            attend_vector(dve, moba_heads(), prob_m, probT_m, ("moba", l))
            yield
            yield

        def moba_scalar(act, l, fill):
            out_scalar(act, vt_m, halves(bank("moba_v", l)), "moba_v", l)
            yield
            attend_scalar(act, moba_heads(), prob_m, probT_m, ("moba", l), lambda i: next(fill, None))
            yield
            yield

        hq, hf, hi_, hg = (raw_h[:, 2 * n:2 * n + 2, :] for n in range(4))
        key_h, B_h, D_h, qd, kdc, vt_h = (wide(h, 0), wide(h, 2), wide(h, 4), wide(h, 6), wide(x, 0), wide(x, 2))
        one_m, lb = stat[:, 20:22], stat[:, 22:24]

        def blocks(t, n):
            return t.rearrange("p c (a n) -> p c a n", n=n)

        def hgrn_scores_tensor(pe, l, lev, a, bq):
            both = [take(pe, "hgrn_scores", l, lev, par) for par in range(2)]
            for u in range(4):
                c, j = u // 2, u % 2
                for par in range(2):
                    sl = slice(64 * par, 64 * par + 64)
                    last = mm(both[par][:, u * P:(u + 1) * P], a[sl, c, j * P:(j + 1) * P], bq[sl, c, j * P:(j + 1) * P], 0, 1)
                    if u == 3:
                        last.then_inc(*tensor.mark("hgrn_scores", l, lev, par))

        def hgrn_scores_vector(dve, l, lev, mask):
            for par in range(2):
                dve.wait_ge(*tensor.at("hgrn_scores", l, lev, par))
                dst = sc_d[:, par * 512:(par + 1) * 512].rearrange("p (u t) -> p u t", u=4)
                src = bank("hgrn_scores", l, lev, par)[:, :].rearrange("p (u t) -> p u t", u=4)
                m = mask.unsqueeze(1).broadcast_to((P, 4, P))
                if lev < 0:
                    V.tensor_tensor(dst, src, m, ALU.mult).then_inc(*vector.mark("hgrn_scores", l, lev, par))
                else:
                    V.copy_predicated(dst, m.bitcast(U32), src).then_inc(*vector.mark("hgrn_scores", l, lev, par))
            dve.wait_ge(*vector.now("hgrn_scores"))

        def hgrn_tensor(pe, l):
            turn_tensor(pe, hi_, "hgrn_v", l)
            pe.wait_ge(*vector.at("hgrn_key", l))
            hgrn_scores_tensor(pe, l, -1, key_h, hq)
            yield
            for lev in range(LEVELS + 1):
                pe.wait_ge(*vector.at("hgrn_decayed", l, lev))
                if lev < LEVELS:
                    hgrn_scores_tensor(pe, l, lev, kdc, qd)
                else:
                    for par in range(2):
                        sl = slice(64 * par, 64 * par + 64)
                        b = take(pe, "hgrn_cross", l, par)
                        for c in range(2):
                            last = mm(b[:, c * P:(c + 1) * P], kdc[sl, c, 0:P], qd[sl, c, P:S], 0, 1)
                        last.then_inc(*tensor.mark("hgrn_cross", l, par))
                yield
            pe.wait_ge(*scalar.at("hgrn_cross", l, 1))
            pe.wait_ge(*vector.at("hgrn_scores", l, LEVELS - 1, 1))
            pe.wait_ge(*got("hgrn_v", l))
            b = take(pe, "hgrn_y", l)
            for hd in range(4):
                par, c = hd % 2, hd // 2
                o_, d0 = c * S, par * 512 + 2 * c * P
                hs = slice(64 * hd, 64 * hd + 64)
                mm(b[sl_of(hd), o_:o_ + P], vt_h[:, 0, hs], sc_d[:, d0:d0 + P], 0, 1)
                mm(b[sl_of(hd), o_ + P:o_ + S], vt_h[:, 0, hs], sc_x[:, par * S + c * P:par * S + (c + 1) * P], 0, 2)
                last = mm(b[sl_of(hd), o_ + P:o_ + S], vt_h[:, 1, hs], sc_d[:, d0 + P:d0 + 2 * P], 1, 2)
            last.then_inc(*tensor.mark("hgrn_y", l))
            yield
            pe.wait_ge(*scalar.at("hgrn_sq", l))
            head_sum_tensor(pe, kdc, "hgrn_sum", l)
            yield

        def hgrn_vector(dve, l):
            if l == 0:
                V.memset(lb, 0.0).then_inc(*vector.mark("chain"))
                link(dve, V.memset(one_m, 1.0))
            else:
                e0, e1, top = stat[:, 24:26], stat[:, 26:28], stat[:, 28:30]
                l0, l1 = vc("hgrn_lb_logits_2", 0, 2), vc("hgrn_lb_logits_2", 2, 2)
                link(dve, V.tensor_tensor(top, l0, l1, ALU.max))
                V.tensor_tensor(e0, l0, top, ALU.subtract).then_inc(*vector.mark("chain"))
                V.tensor_tensor(e1, l1, top, ALU.subtract).then_inc(*vector.mark("hgrn_lb", l))
                dve.wait_ge(*scalar.at("hgrn_lb", l))
                link(dve, V.tensor_tensor(top, e0, e1, ALU.add))
                link(dve, V.reciprocal(top, top))
                link(dve, V.tensor_tensor(lb, e1, top, ALU.mult))
                link(dve, V.tensor_scalar(one_m, lb, -1.0, 1.0, ALU.mult, ALU.add))
            out_vector(dve, vt_h, halves(bank("hgrn_v", l)), "hgrn_v", l)
            dve.wait_ge(*scalar.at("hgrn_sig", l))
            for c in range(2):
                V.tensor_scalar(key_h[:, c, :], key_h[:, c, :], one_m[:, c:c + 1], None, ALU.mult).then_inc(*vector.mark("hgrn_key", l))
            for c in range(2):
                V.tensor_scalar(B_h[:, c, :], B_h[:, c, :], one_m[:, c:c + 1], lb[:, c:c + 1], ALU.mult, ALU.add)\
                 .then_inc(*vector.mark("hgrn_forget", l))
            hgrn_scores_vector(dve, l, -1, ident)
            dve.wait_ge(*scalar.at("hgrn_log", l))
            for c in range(2):
                V.tensor_tensor_scan(B_h[:, c, :], ones[:, 0:1].broadcast_to((P, S)), D_h[:, c, :], 0.0, ALU.mult, ALU.add).then_inc(*vector.mark("chain"))
            dve.wait_ge(*vector.now("chain"))
            yield
            for lev in range(LEVELS + 1):
                n = 2 ** (lev + 1)
                half = n // 2
                if lev:
                    dve.wait_ge(*vector.at("hgrn_decayed", l, lev - 1))
                for c in range(2):
                    Bp, Dp = B_h[:, c, :].rearrange("p (a n) -> p a n", n=n), D_h[:, c, :].rearrange("p (a n) -> p a n", n=n)
                    V.tensor_tensor(Dp, Bp, Bp[:, :, half - 1:half].broadcast_to((P, S // n, n)), ALU.subtract)\
                     .then_inc(*vector.mark("chain"))
                dve.wait_ge(*vector.now("chain"))
                V.scalar_tensor_tensor(D_h, D_h, -1.0, D_h, ALU.mult, ALU.min).then_inc(*vector.mark("hgrn_decay", l, lev))
                if lev:
                    hgrn_scores_vector(dve, l, lev - 1, C("levels")[:, (lev - 1) * P:lev * P])
                dve.wait_ge(*scalar.at("hgrn_decay", l, lev))
                V.tensor_tensor(qd, hq, D_h, ALU.mult).then_inc(*vector.mark("chain"))
                V.tensor_tensor(kdc, key_h, D_h, ALU.mult).then_inc(*vector.mark("hgrn_decayed", l, lev))
                yield
            yield
            dve.wait_ge(*tensor.at("hgrn_sum", l))
            link(dve, V.tensor_scalar(D_h, halves(bank("hgrn_sum", l)), 1.0 / 64, EPS, ALU.mult, ALU.add))
            V.reciprocal(D_h, D_h).then_inc(*vector.mark("hgrn_sum", l))
            dve.wait_ge(*scalar.at("hgrn_silu", l))
            link(dve, V.tensor_tensor(qd, qd, D_h, ALU.mult))
            for c in range(2):
                V.scalar_tensor_tensor(ys[3][:, c, :], qd[:, c, :], vc("hgrn_gn_g_2", 2 * l + c), key_h[:, c, :], ALU.mult, ALU.mult)\
                 .then_inc(*vector.mark("hgrn_done", l))
            yield

        def hgrn_scalar(act, l):
            SC.activation(key_h, hf, ACT.Sigmoid, scale=-1.0).then_inc(*scalar.mark("chain"))
            SC.activation(B_h, hf, ACT.Sigmoid).then_inc(*scalar.mark("hgrn_sig", l))
            if l:
                act.wait_ge(*vector.at("hgrn_lb", l))
                SC.activation(stat[:, 24:28], stat[:, 24:28], ACT.Exp).then_inc(*scalar.mark("hgrn_lb", l))
            act.wait_ge(*vector.at("hgrn_forget", l))
            SC.activation(D_h, B_h, ACT.Ln).then_inc(*scalar.mark("hgrn_log", l))
            yield
            for lev in range(LEVELS + 1):
                act.wait_ge(*vector.at("hgrn_decay", l, lev))
                SC.activation(D_h, D_h, ACT.Exp).then_inc(*scalar.mark("hgrn_decay", l, lev))
                if lev == LEVELS:
                    for par in range(2):
                        out_scalar(act, sc_x[:, par * S:(par + 1) * S], bank("hgrn_cross", l, par)[:, 0:S], "hgrn_cross", l, par)
                yield
            out_scalar(act, qd, halves(bank("hgrn_y", l)), "hgrn_y", l)
            act.wait_ge(*scalar.now("hgrn_y"))
            SC.activation(kdc, qd, ACT.Square).then_inc(*scalar.mark("hgrn_sq", l))
            yield
            act.wait_ge(*vector.at("hgrn_sum", l))
            SC.activation(D_h, D_h, ACT.Sqrt).then_inc(*scalar.mark("chain"))
            SC.activation(key_h, hg, ACT.Silu).then_inc(*scalar.mark("hgrn_silu", l))
            yield

        pr_ = raw_r[:, :, 1:S + 1]
        r_, k_, v_ = pr_[:, 0:2, :], pr_[:, 2:4, :], pr_[:, 4:6, :]

        def rwkv_buffers():
            names = ("ld", "av", "gv", "kk", "B", "rt", "at", "bt", "kt")
            return dict(zip(names, BUF9))

        LORA = (("ld", "wa2", 6, slice(0, 64), "rwkv_w0_2"), ("av", "wa2", 6, slice(64, 128), "rwkv_a0_2"), ("gv", "g2w", 7, slice(0, 128), None))

        def pairs(Bf):
            return (("NT", NT, "bt", "at", "before"), ("AkT", AkT, "kt", "at", "before"), ("RbT", RbT, "bt", "rt", "upto"), ("RkT", RkT, "kt", "rt", "upto"))

        def rwkv_tensor(pe, l, fill):
            W = rwkv_buffers()
            yield
            pe.wait_ge(*scalar.at("lora_in", l))
            pe.wait_ge(*vector.at("shifted_r", l, 7))
            for dst, w_, src, sl, bias in LORA:
                wt = wa2 if w_ == "wa2" else g2w
                b = take(pe, "lora", l, dst)
                for c in range(2):
                    last = mm(b[:, c * S:(c + 1) * S], wt[sl, l, c * P:(c + 1) * P], pr_[sl, src, :], 0, 1)
                last.then_inc(*tensor.mark("lora", l, dst))
            if l:
                b = take(pe, "vmix1", l)
                for c in range(2):
                    last = mm(b[0:32, 0:S], v1w[:, c, :], v_[:, c, :], c, 2)
                last.then_inc(*tensor.mark("vmix1", l))
                pe.wait_ge(*scalar.at("vmix1", l))
                b = take(pe, "vmix2", l)
                for c in range(2):
                    last = mm(b[:, c * S:(c + 1) * S], v2w[0:32, c * P:(c + 1) * P], W["kt"][0:32, 0, :], 0, 1)
                last.then_inc(*tensor.mark("vmix2", l))
            yield
            pe.wait_ge(*scalar.at("kk_sq", l))
            head_sum_tensor(pe, W["rt"], "kk_sum", l)
            next(fill, None)
            pe.wait_ge(*vector.at("rk", l))
            head_sum_tensor(pe, W["av"], "bonus", l)
            yield
            yield
            pe.wait_ge(*vector.at("rwkv_v", l))
            turn_tensor(pe, v_, "rwkv_vt", l)
            pe.wait_ge(*vector.at("decayed", l))
            for name, dst, a, bq, m in pairs(W):
                both = [take(pe, "pairs", l, name, par) for par in range(2)]
                for u in range(4):
                    c, j = u // 2, u % 2
                    for par in range(2):
                        sl = slice(64 * par, 64 * par + 64)
                        last = mm(both[par][:, u * P:(u + 1) * P], W[a][sl, c, j * P:(j + 1) * P], W[bq][sl, c, j * P:(j + 1) * P], 0, 1)
                        if u == 3:
                            last.then_inc(*tensor.mark("pairs", l, name, par))
            yield
            pe.wait_ge(*vector.at("moved", l))
            bx, kx = W["kk"][:, :, 0:P], W["kk"][:, :, P:S]
            for n, (a, bq) in enumerate(((bx, "at"), (kx, "at"), (bx, "rt"), (kx, "rt"))):
                both = [take(pe, "cross", l, n, par) for par in range(2)]
                for c in range(2):
                    for par in range(2):
                        sl = slice(64 * par, 64 * par + 64)
                        last = mm(both[par][:, c * P:(c + 1) * P], a[sl, c, :], W[bq][sl, c, P:S], 0, 1)
                        if c == 1:
                            last.then_inc(*tensor.mark("cross", l, n, par))
            yield
            for lev in range(LEVELS):
                pe.wait_ge(level_masked, LEVELS * l + lev + 1)
                pe.wait_ge(*(vector.at("dTT", l, lev - 1, 1) if lev else vector.at("pairs", l, "RkT", 1)))
                for par in range(2):
                    b = take(pe, "NT_T", l, lev, par)
                    for u in range(4):
                        o_ = par * 512 + u * P
                        last = mm(b[:, u * P:(u + 1) * P], NL[par][:, u * P:(u + 1) * P], Tm[:, o_:o_ + P], 0, 1)
                    last.then_inc(*tensor.mark("NT_T", l, lev, par))
                yield
                for par in range(2):
                    pe.wait_ge(*got("NT_T", l, lev, par))
                    b = take(pe, "dT", l, lev, par)
                    for u in range(4):
                        o_ = par * 512 + u * P
                        last = mm(b[:, u * P:(u + 1) * P], TT[:, o_:o_ + P], Xm[:, o_:o_ + P], 0, 1)
                    last.then_inc(*tensor.mark("dT", l, lev, par))
                    b = take(pe, "dTT", l, lev, par)
                    for u in range(4):
                        o_ = par * 512 + u * P
                        last = mm(b[:, u * P:(u + 1) * P], Xm[:, o_:o_ + P], TT[:, o_:o_ + P], 0, 1)
                    last.then_inc(*tensor.mark("dTT", l, lev, par))
                yield
            pe.wait_ge(*vector.at("dTT", l, LEVELS - 1, 1))
            pe.wait_ge(*scalar.at("rwkv_vt", l))
            pe.wait_ge(*scalar.at("cross", l, 3, 1))
            vt = W["B"]
            for j in range(2):
                b = take(pe, "W", l, j)
                for hd in range(4):
                    hs = slice(64 * hd, 64 * hd + 64)
                    n = 1 + 2 * j
                    last = mm(b[:, hs], unit(AkT, hd, j), vt[:, j, hs], 0, n)
                    if j == 1:
                        mm(b[:, hs], cross_of(1, hd), vt[:, 0, hs], 1, n)
                        last = mm(b[:, hs], cross_of(0, hd), SA[:, 0, hs], 2, n)
                last.then_inc(*tensor.mark("W", l, j))
                pe.wait_ge(*scalar.at("W", l, j))
                b = take(pe, "SA", l, j)
                for hd in range(4):
                    hs = slice(64 * hd, 64 * hd + 64)
                    last = mm(b[:, hs], unit(TT, hd, j), Wm[:, j, hs], 0, 1)
                last.then_inc(*tensor.mark("SA", l, j))
                pe.wait_ge(*scalar.at("SA", l, j))
                yield
            b = take(pe, "rwkv_y", l)
            for hd in range(4):
                hs = slice(64 * hd, 64 * hd + 64)
                o_ = (hd // 2) * S
                ps = b[sl_of(hd), o_:o_ + P]
                mm(ps, SA[:, 0, hs], unit(RbT, hd, 0), 0, 2)
                mm(ps, vt[:, 0, hs], unit(RkT, hd, 0), 1, 2)
                ps = b[sl_of(hd), o_ + P:o_ + S]
                mm(ps, SA[:, 0, hs], cross_of(2, hd), 0, 4)
                mm(ps, vt[:, 0, hs], cross_of(3, hd), 1, 4)
                mm(ps, SA[:, 1, hs], unit(RbT, hd, 1), 2, 4)
                last = mm(ps, vt[:, 1, hs], unit(RkT, hd, 1), 3, 4)
            last.then_inc(*tensor.mark("rwkv_y", l))
            pe.wait_ge(*scalar.at("rwkv_y", l))
            head_sum_tensor(pe, W["rt"], "gn_mean", l)
            yield
            pe.wait_ge(*scalar.at("gn_sq", l))
            head_sum_tensor(pe, W["kt"], "gn_var", l)
            yield

        def unit(M, hd, j):
            o_ = (hd % 2) * 512 + (2 * (hd // 2) + j) * P
            return M[:, o_:o_ + P]

        level_masked, identity_set = sem("level_masked"), sem("identity_set")

        def rwkv_pool(pool, l):
            for s in (tensor, scalar, vector):
                value = s.closed(("group1", l))
                if value:
                    pool.wait_ge(*value)
            idb = ident.unsqueeze(1).broadcast_to((P, 8, P))
            for t in (Tm, TT):
                nc.gpsimd.tensor_copy(t.rearrange("p (u t) -> p u t", u=8), idb).then_inc(identity_set, 1)
            pool.wait_ge(identity_set, 2 * l + 2)
            pool.wait_ge(*vector.at("pairs", l, "NT", 1))
            for lev in range(LEVELS):
                if lev:
                    pool.wait_ge(*tensor.at("NT_T", l, lev - 1, 1))
                for par in range(2):
                    last = nc.gpsimd.tensor_tensor(NL[par].rearrange("p (u t) -> p u t", u=4),
                                                   NT[:, par * 512:(par + 1) * 512].rearrange("p (u t) -> p u t", u=4),
                                                   C("levels")[:, lev * P:(lev + 1) * P].unsqueeze(1).broadcast_to((P, 4, P)), ALU.mult)
                last.then_inc(level_masked, 1)

        def rwkv_vector(dve, l):
            W = rwkv_buffers()
            ld, av, gv, kk, Bc, rt, at_, bt, kt = (W[n] for n in ("ld", "av", "gv", "kk", "B", "rt", "at", "bt", "kt"))
            d = arena[:, pool0:pool0 + 2048].rearrange("p (n t) -> p n t", n=8)
            link(dve, V.tensor_tensor(d, raw_r[:, :, 0:S], pr_, ALU.subtract))
            for i in (6, 7, 0, 1, 2, 3, 4, 5):
                V.scalar_tensor_tensor(pr_[:, i, :], d[:, i, :], vc("rwkv_mu_2", 8 * l + i), pr_[:, i, :], ALU.mult, ALU.add)\
                 .then_inc(*vector.mark("shifted_r", l, i))
            book.new[("vector", "shifted_r", l, 7)] = vector.n["shifted"]
            book.new[("vector", "shifted_67", l)] = vector.n["shifted"] - 6
            dve.wait_ge(*vector.now("shifted_r"))
            yield
            for c in range(2):
                V.tensor_scalar(kk[:, c, :], k_[:, c, :], vc("rwkv_k_k_2", 2 * l + c), None, ALU.mult).then_inc(*vector.mark("kk", l))
            dve.wait_ge(*vector.now("kk"))
            dve.wait_ge(*scalar.at("lora", l, "gv"))
            link(dve, V.tensor_scalar(ld, ld, -float(np.exp(-0.5)), None, ALU.mult))
            link(dve, V.tensor_tensor_scan(flat(Bc), C("seg"), flat(ld), 0.0, ALU.mult, ALU.add))
            if l:
                dve.wait_ge(*scalar.at("vmix2", l))
                link(dve, V.tensor_tensor(kt, v_first, v_, ALU.subtract))
                link(dve, V.tensor_tensor(kt, kt, bt, ALU.mult))
                V.tensor_tensor(v_, v_, kt, ALU.add).then_inc(*vector.mark("rwkv_v", l))
            else:
                V.tensor_copy(v_first, v_).then_inc(*vector.mark("rwkv_v", l))
            dve.wait_ge(*vector.now("rwkv_v"))
            yield
            dve.wait_ge(*tensor.at("kk_sum", l))
            link(dve, V.tensor_scalar(rt, halves(bank("kk_sum", l)), 1e-24, None, ALU.max))
            V.reciprocal(rt, rt).then_inc(*vector.mark("kk_sum", l))
            dve.wait_ge(*scalar.at("kk_root", l))
            link(dve, V.tensor_tensor(kk, kk, rt, ALU.mult))
            link(dve, V.tensor_tensor(bt, kk, av, ALU.mult))
            for c in range(2):
                link(dve, V.tensor_scalar(av[:, c, :], av[:, c, :], -1.0, vc("rwkv_k_a_2", 2 * l + c), ALU.add, ALU.mult))
            link(dve, V.scalar_tensor_tensor(k_, av, 1.0, k_, ALU.add, ALU.mult))
            for c in range(2):
                V.scalar_tensor_tensor(av[:, c, :], r_[:, c, :], vc("rwkv_r_k_2", 2 * l + c), k_[:, c, :], ALU.mult, ALU.mult)\
                 .then_inc(*vector.mark("rk", l))
            B4, D4 = (flat(t).rearrange("p (u t) -> p u t", u=4) for t in (Bc, rt))
            mid, endx = stat[:, 48:52], stat[:, 52:54]
            link(dve, V.tensor_copy(mid.unsqueeze(2), B4[:, :, 63:64]))
            m2 = mid.rearrange("p (c j) -> p c j", c=2)
            link(dve, V.tensor_tensor(endx.unsqueeze(2), m2[:, :, 1:2], m2[:, :, 0:1], ALU.subtract))
            link(dve, V.tensor_tensor(endx, endx, Bc[:, :, P - 1], ALU.add))
            link(dve, V.tensor_tensor(D4, B4, mid.unsqueeze(2).broadcast_to((P, 4, P)), ALU.subtract))
            V.tensor_tensor(ld, rt, ld, ALU.subtract).then_inc(*vector.mark("exponents", l))
            yield
            dve.wait_ge(*tensor.at("bonus", l))
            V.tensor_tensor(av, halves(bank("bonus", l)), v_, ALU.mult).then_inc(*vector.mark("bonus", l))
            dve.wait_ge(*scalar.at("exponentials", l))
            V.scalar_tensor_tensor(at_, kk, -1.0, ld, ALU.mult, ALU.mult).then_inc(*vector.mark("chain"))
            V.tensor_tensor(bt, bt, kt, ALU.mult).then_inc(*vector.mark("chain"))
            V.tensor_tensor(rt, rt, r_, ALU.mult).then_inc(*vector.mark("chain"))
            V.tensor_tensor(kt, kt, k_, ALU.mult).then_inc(*vector.mark("decayed", l))
            dve.wait_ge(*vector.now("decayed"))
            bx, kx = kk[:, :, 0:P], kk[:, :, P:S]
            for c in range(2):
                V.tensor_scalar(bx[:, c, :], bt[:, c, 0:P], endx[:, c:c + 1], None, ALU.mult).then_inc(*vector.mark("chain"))
                V.tensor_scalar(kx[:, c, :], kt[:, c, 0:P], endx[:, c:c + 1], None, ALU.mult).then_inc(*vector.mark("moved", l))
            dve.wait_ge(*vector.now("moved"))
            yield
            for name, dst, a, bq, m in pairs(W):
                for par in range(2):
                    dve.wait_ge(*tensor.at("pairs", l, name, par))
                    V.tensor_tensor(dst[:, par * 512:(par + 1) * 512].rearrange("p (u t) -> p u t", u=4),
                                    bank("pairs", l, name, par)[:, :].rearrange("p (u t) -> p u t", u=4),
                                    C(m).unsqueeze(1).broadcast_to((P, 4, P)), ALU.mult).then_inc(*vector.mark("pairs", l, name, par))
            dve.wait_ge(*vector.now("pairs"))
            yield
            yield
            for lev in range(LEVELS):
                yield
                for par in range(2):
                    hs = slice(par * 512, par * 512 + 512)
                    dve.wait_ge(*tensor.at("dTT", l, lev, par))
                    V.tensor_tensor(Tm[:, hs], Tm[:, hs], bank("dT", l, lev, par)[:, :], ALU.add).then_inc(*vector.mark("dT", l, lev, par))
                    V.tensor_tensor(TT[:, hs], TT[:, hs], bank("dTT", l, lev, par)[:, :], ALU.add).then_inc(*vector.mark("dTT", l, lev, par))
                dve.wait_ge(*vector.now("dTT"))
                yield
            yield
            yield
            dve.wait_ge(*scalar.at("rwkv_y", l))
            dve.wait_ge(*tensor.at("gn_mean", l))
            V.scalar_tensor_tensor(rt, halves(bank("gn_mean", l)), -1.0 / 64, rt, ALU.mult, ALU.add).then_inc(*vector.mark("gn_mean", l))
            dve.wait_ge(*vector.now("gn_mean"))
            yield
            dve.wait_ge(*tensor.at("gn_var", l))
            link(dve, V.tensor_scalar(kt, halves(bank("gn_var", l)), 1.0 / 64, GN_EPS, ALU.mult, ALU.add))
            V.reciprocal(kt, kt).then_inc(*vector.mark("gn_var", l))
            dve.wait_ge(*scalar.at("gn_root", l))
            link(dve, V.tensor_tensor(rt, rt, kt, ALU.mult))
            for c in range(2):
                V.tensor_scalar(rt[:, c, :], rt[:, c, :], vc("rwkv_gn_w_2", 2 * l + c), vc("rwkv_gn_b_2", 2 * l + c), ALU.mult, ALU.add)\
                 .then_inc(*vector.mark("chain"))
            dve.wait_ge(*vector.now("chain"))
            link(dve, V.tensor_tensor(rt, rt, av, ALU.add))
            link(dve, V.tensor_tensor(ys[1], rt, gv, ALU.mult))
            yield

        def rwkv_scalar(act, l, fill):
            W = rwkv_buffers()
            yield
            act.wait_ge(vector.sem("shifted_r"), book.old.get(("vector", "shifted_67", l), 1))
            SC.activation(pr_[:, 7, :], pr_[:, 7, :], ACT.Sigmoid).then_inc(*scalar.mark("chain"))
            SC.activation(pr_[0:64, 6, :], pr_[0:64, 6, :], ACT.Tanh).then_inc(*scalar.mark("lora_in", l))
            for dst, w_, src, sl, bias in LORA:
                act.wait_ge(*tensor.at("lora", l, dst))
                b = bank("lora", l, dst)
                if bias:
                    SC.activation(W[dst][:, 0, :], b[:, 0:S], ACT.Sigmoid, bias=vc(bias, 2 * l)).then_inc(*scalar.mark("chain"))
                    SC.activation(W[dst][:, 1, :], b[:, S:T2], ACT.Sigmoid, bias=vc(bias, 2 * l + 1)).then_inc(*scalar.mark("lora", l, dst))
                else:
                    SC.activation(W[dst], halves(b), ACT.Copy).then_inc(*scalar.mark("lora", l, dst))
            if l:
                out_scalar(act, W["kt"][0:32, 0, :], bank("vmix1", l)[0:32, 0:S], "vmix1", l)
                act.wait_ge(*tensor.at("vmix2", l))
                SC.activation(W["bt"][:, 0, :], bank("vmix2", l)[:, 0:S], ACT.Sigmoid, bias=vc("rwkv_v0_2", 0)).then_inc(*scalar.mark("chain"))
                SC.activation(W["bt"][:, 1, :], bank("vmix2", l)[:, S:T2], ACT.Sigmoid, bias=vc("rwkv_v0_2", 1)).then_inc(*scalar.mark("vmix2", l))
            act.wait_ge(*vector.at("kk", l))
            SC.activation(W["rt"], W["kk"], ACT.Square).then_inc(*scalar.mark("kk_sq", l))
            yield
            act.wait_ge(*vector.at("kk_sum", l))
            SC.activation(W["rt"], W["rt"], ACT.Sqrt).then_inc(*scalar.mark("kk_root", l))
            next(fill, None)
            act.wait_ge(*vector.at("exponents", l))
            endx = stat[:, 52:54]
            SC.activation(endx, endx, ACT.Exp).then_inc(*scalar.mark("chain"))
            link_s(act, SC.activation(W["kt"], W["rt"], ACT.Exp, scale=-1.0))
            SC.activation(W["rt"], W["rt"], ACT.Exp).then_inc(*scalar.mark("chain"))
            SC.activation(W["ld"], W["ld"], ACT.Exp).then_inc(*scalar.mark("exponentials", l))
            yield
            yield
            act.wait_ge(*vector.at("exponents", l))
            out_scalar(act, W["B"], halves(bank("rwkv_vt", l)), "rwkv_vt", l)
            yield
            for n in range(4):
                for par in range(2):
                    out_scalar(act, CROSS[2 * n + par], bank("cross", l, n, par)[:, 0:S], "cross", l, n, par)
            yield
            for lev in range(LEVELS):
                for par in range(2):
                    out_scalar(act, Xm[:, par * 512:(par + 1) * 512], bank("NT_T", l, lev, par)[:, :], "NT_T", l, lev, par)
                yield
                yield
            for j in range(2):
                out_scalar(act, Wm[:, j, :], bank("W", l, j)[:, 0:S], "W", l, j)
                out_scalar(act, SA[:, j, :], bank("SA", l, j)[:, 0:S], "SA", l, j)
                yield
            out_scalar(act, W["rt"], halves(bank("rwkv_y", l)), "rwkv_y", l)
            yield
            act.wait_ge(*vector.at("gn_mean", l))
            SC.activation(W["kt"], W["rt"], ACT.Square).then_inc(*scalar.mark("gn_sq", l))
            act.wait_ge(*vector.at("gn_var", l))
            SC.activation(W["kt"], W["kt"], ACT.Sqrt).then_inc(*scalar.mark("gn_root", l))
            yield

        Wm, SA = Xm[:, 0:512].rearrange("p (j c) -> p j c", j=2), Xm[:, 512:1024].rearrange("p (j c) -> p j c", j=2)
        o = pool0 + 7 * 1024 + 1536
        BUF9 = [chan() for _ in range(9)]
        NL = [place(512), rstd[:, :]]
        assert o <= AR, (o, AR)
        CROSS = x_hi[4:8] + [place(256) for _ in range(4)]
        assert o <= AR, (o, AR)

        def cross_of(n, hd):
            return CROSS[2 * n + hd % 2][:, (hd // 2) * P:(hd // 2 + 1) * P]

        def together(*mixers, filler=None, later=None):
            live = list(mixers)
            while live:
                for m in list(live):
                    if next(m, "end") == "end":
                        live.remove(m)
                    if filler and next(filler, "end") == "end" and later and len(live) == 1:
                        next(later, None)

        MIX_DST = [[raw_s[:, i, :] for i in range(4)], [raw_s[:, i, :] for i in (4, 5)],
                   [raw_m[:, i, :] for i in range(4)], [raw_m[:, i, :] for i in (4, 5)],
                   [raw_r[:, i, 1:S + 1] for i in range(4)], [raw_r[:, i, 1:S + 1] for i in range(4, 8)],
                   [raw_h[:, i, :] for i in range(4)], [raw_h[:, i, :] for i in range(4, 8)]]

        def in_tiles(pe, l, chunks):
            for c in chunks:
                w = next_weights(pe)
                for i in range(len(MIX_DST[c])):
                    project_tensor(pe, w, i * P, P, S, ("mixin", l, c, i), None, ("m1", l) if c == i == 0 else None)
                    if i == len(MIX_DST[c]) - 1:
                        chunk_read()
                    yield

        def in_outs(act, l, chunks):
            for c in chunks:
                for i, dst in enumerate(MIX_DST[c]):
                    out_scalar(act, dst, bank("mixin", l, c, i)[:, 0:S], "mixin", l, c, i)
                    yield

        def gate_tiles(pe, l, half):
            for i in range(16):
                if i % 4 == 0:
                    w = next_weights(pe)
                project_tensor(pe, w, (i % 4) * P, P, S, ("gate", l, half, i))
                if i % 4 == 3:
                    chunk_read()
                yield

        def gate_outs(act, l, half):
            for i in range(16):
                if half and i == 0:
                    act.wait_ge(*vector.at("hgrn_done", l))
                dst = gates[:, i, :] if not half else raw_h[:, i, :] if i < 8 else h[:, i - 8, S:T2]
                out_scalar(act, dst, bank("gate", l, half, i)[:, 0:S], "gate", l, half, i, func=ACT.Sigmoid)
                yield i

        def mixer_tensor(pe, l):
            for _ in in_tiles(pe, l, range(4)):
                pass
            join(tensor, pe, ("mixers", l))
            fill = in_tiles(pe, l, range(4, 8))
            together(stick_tensor(pe, l), moba_tensor(pe, l, fill), filler=fill)
            for _ in fill:
                pass
            join(tensor, pe, ("group1", l))
            fill, later = gate_tiles(pe, l, 0), gate_tiles(pe, l, 1)
            rotating[0] = 6
            together(rwkv_tensor(pe, l, fill), hgrn_tensor(pe, l), filler=fill, later=later)
            rotating[0] = 8
            for _ in later:
                pass
            join(tensor, pe, ("branches", l))
            for half in range(2):
                w = next_weights(pe)
                for m in range(4):
                    for br in range(0, 4, 2):
                        b = take(pe, "branch", l, 4 * half + m, br)
                        for q in range(2):
                            for k in range(2):
                                last = mm(b[:, q * S:(q + 1) * S], w[:, 2 * (br + q) + k, m * P:(m + 1) * P], ys[br + q][:, k, :], k, 2)
                        last.then_inc(*tensor.mark("branch", l, 4 * half + m, br))
                chunk_read()
            pe.wait_ge(*vector.at("merged", l, KD - 1))
            for i in range(2):
                w = next_weights(pe)
                for m in range(4):
                    b = take(pe, "w_out", l, 4 * i + m)
                    for k in range(KD):
                        last = mm(b[:, 0:S], w[:, k, m * P:(m + 1) * P], merged[:, k, :], k, KD)
                    last.then_inc(*tensor.mark("w_out", l, 4 * i + m))
                    if 4 * i + m >= 2:
                        mean_tensor(pe, S, ("m2", l), 4 * i + m - 2)
                chunk_read()
            for k in (KD - 2, KD - 1):
                mean_tensor(pe, S, ("m2", l), k)

        merged = raw_r[:, :, 1:S + 1]

        def gate_pair(m, br):
            t, i = (gates, 4 * br) if m < 4 else (raw_h, 0) if br == 0 else (h[:, :, S:T2], 0)
            return t[:, i:i + 8, :].rearrange("p (b m) t -> p b m t", b=2)[:, :, m % 4, :]

        def mixer_vector(dve, l):
            unit_vector(dve, S, ("m1", l), lambda k: vc("norm1_g_2", 8 * l + k))
            V.memset(raw_r[:, :, 0:1], 0.0).then_inc(*vector.mark("chain"))
            for c in range(4):
                for i in range(0, len(MIX_DST[c]), 2):
                    out_vector(dve, MIX_DST[c][i], bank("mixin", l, c, i)[:, 0:S], "mixin", l, c, i)
            join(vector, dve, ("mixers", l))
            together(stick_vector(dve, l), moba_vector(dve, l))
            join(vector, dve, ("group1", l))
            together(rwkv_vector(dve, l), hgrn_vector(dve, l))
            join(vector, dve, ("branches", l))
            for m in range(KD):
                dve.wait_ge(*scalar.at("gate", l, m // 4, 12 + m % 4))
                for br in range(0, 4, 2):
                    dve.wait_ge(*tensor.at("branch", l, m, br))
                    g2 = gate_pair(m, br)
                    V.tensor_tensor(g2, g2, halves(bank("branch", l, m, br)), ALU.mult).then_inc(*vector.mark("branch", l, m, br))
                dve.wait_ge(*vector.now("branch"))
                g2, g4 = gate_pair(m, 0), gate_pair(m, 2)
                link(dve, V.tensor_tensor(g2, g2, g4, ALU.add))
                V.tensor_tensor(merged[:, m, :], g2[:, 0, :], g2[:, 1, :], ALU.add).then_inc(*vector.mark("merged", l, m))
            for d in range(KD):
                dve.wait_ge(*tensor.at("w_out", l, d))
                V.tensor_tensor(x[:, d, 0:S], x[:, d, 0:S], bank("w_out", l, d)[:, 0:S], ALU.add).then_inc(*vector.mark("w_out", l, d))

        def mixer_scalar(act, l):
            root_scalar(act, S, ("m1", l))
            for c in range(4):
                for i in range(1, len(MIX_DST[c]), 2):
                    out_scalar(act, MIX_DST[c][i], bank("mixin", l, c, i)[:, 0:S], "mixin", l, c, i)
            join(scalar, act, ("mixers", l))
            fill = in_outs(act, l, range(4, 8))
            together(stick_scalar(act, l), moba_scalar(act, l, fill), filler=fill)
            for _ in fill:
                pass
            join(scalar, act, ("group1", l))
            fill, later = gate_outs(act, l, 0), gate_outs(act, l, 1)
            together(rwkv_scalar(act, l, fill), hgrn_scalar(act, l), filler=fill, later=later)
            for _ in later:
                pass
            join(scalar, act, ("branches", l))
            for d in range(KD):
                squares_scalar(act, S, ("m2", l), d, vector.at("w_out", l, d))

        hid = arena[:, 0:NF * S].rearrange("p (f t) -> p f t", f=NF)

        def after_ffn(l):
            return ("m1", l + 1) if l < L - 1 else "final2"

        def ffn_tensor(pe, l):
            for i in range(6):
                nf = min(4, NF - 4 * i)
                for which in ("ffn_gate", "ffn_up"):
                    w = next_weights(pe)
                    for m in range(0, nf, 2):
                        b = take(pe, which, l, 4 * i + m)
                        for q in range(2):
                            for k in range(KD):
                                if which == "ffn_gate" and i == m == q == 0:
                                    pe.wait_ge(*got("normed", ("m2", l), k))
                                last = mm(b[:, q * S:(q + 1) * S], w[:, k, (m + q) * P:(m + q + 1) * P], h[:, k, 0:S], k, KD)
                        last.then_inc(*tensor.mark(which, l, 4 * i + m))
                    chunk_read()
            pe.wait_ge(*vector.at("ffn_up", l, NF - 2))
            for d in range(KD):
                w = next_weights(pe)
                b = take(pe, "ffn_down", l, d)
                for k in range(NF):
                    last = mm(b[:, 0:S], w[:, k, :], hid[:, k, :], k, NF)
                last.then_inc(*tensor.mark("ffn_down", l, d))
                chunk_read()
                if d:
                    mean_tensor(pe, S, after_ffn(l), d - 1)
            mean_tensor(pe, S, after_ffn(l), KD - 1)

        def ffn_vector(dve, l):
            unit_vector(dve, S, ("m2", l), lambda k: vc("norm2_g_2", 8 * l + k))
            for f in range(0, NF, 2):
                dve.wait_ge(*scalar.at("ffn_gate", l, f))
                dve.wait_ge(*tensor.at("ffn_up", l, f))
                a = hid[:, f:f + 2, :]
                V.tensor_tensor(a, a, halves(bank("ffn_up", l, f)), ALU.mult).then_inc(*vector.mark("ffn_up", l, f))
            for d in range(KD):
                dve.wait_ge(*tensor.at("ffn_down", l, d))
                V.tensor_tensor(x[:, d, 0:S], x[:, d, 0:S], bank("ffn_down", l, d)[:, 0:S], ALU.add).then_inc(*vector.mark("ffn_down", l, d))
            join(vector, dve, ("ffn", l))

        def ffn_scalar(act, l):
            root_scalar(act, S, ("m2", l))
            for f in range(0, NF, 2):
                act.wait_ge(*tensor.at("ffn_gate", l, f))
                SC.activation(hid[:, f:f + 2, :], halves(bank("ffn_gate", l, f)), ACT.Silu).then_inc(*scalar.mark("ffn_gate", l, f))
            for d in range(KD):
                squares_scalar(act, S, after_ffn(l), d, vector.at("ffn_down", l, d))
            join(scalar, act, ("ffn", l))

        otok = arena[:, 0:2048].rearrange("p (j d) -> p j d", j=2)

        small_list = []
        for name, n in VECS:
            r, a = vcol[name], A[name]
            if len(a.shape) == 3:
                a = a.rearrange("a b c -> (a b c)")
            elif len(a.shape) == 2:
                a = a.rearrange("a b -> (a b)")
            a = a.rearrange("(r c) -> r c", c=P)
            done = 0
            while done < n:
                m = min(n - done, P - (r + done) % P)
                small_list.append((stage[(r + done) % P:(r + done) % P + m, (r + done) // P, :], a[done:done + m, :]))
                done += m
        small_list += [
            (stage[0:8, 2, :], A["c"].rearrange("a (r c) -> (a r) c", c=P)),
            (stage[8:16, 2, :], A["c_ctx"].rearrange("(r c) -> r c", c=P)),
            (sink_row[:, 0:12], A["swa_sink"].rearrange("a b -> (a b)").rearrange("(o n) -> o n", o=1)),
            (xtok[:, 0], A["x"][0].rearrange("(j p) d -> p j d", p=P)),
            (xtok[:, 1], A["ctx"][0].rearrange("(j p) d -> p j d", p=P)),
        ]
        late_list = []
        for l in range(L):
            late_list += [
                (uq[:, l], A["mla_w_uq"][l].rearrange("(k p) n -> p k n", p=P)),
                (ukv[:, l], A["mla_w_ukv"][l]),
                (rtr[:, l], A["router_w"][l].rearrange("(k p) n -> p k n", p=P)),
                (wa2[0:64, l], A["rwkv_w2_2"][l]),
                (wa2[64:128, l], A["rwkv_a2_2"][l]),
                (g2w[:, l], A["rwkv_g2_2"][l]),
            ]
        late_list += [(v1w, A["rwkv_v1_2"][0].rearrange("(k p) n -> p k n", p=P)), (v2w[0:32, :], A["rwkv_v2_2"][0])]
        late_loaded = sem("late_loaded")

        def loads_scalar(act):
            act.dma_start(cst[:, :], A["consts"][:, 0:N_BOTH]).then_inc(const_loaded, 16)
            for dst, src in small_list:
                act.dma_start(dst, src).then_inc(small_loaded, 16)

        def late_loads_scalar(act):
            act.dma_start(cst1, A["consts"][:, N_BOTH:N_BOTH + N_FIRST]).then_inc(late_loaded, 16)
            for dst, src in late_list:
                act.dma_start(dst, src).then_inc(late_loaded, 16)

        with nc.Block() as block:
            @block.tensor
            def _(pe):
                turn[0], at[0] = 0, 0
                pe.wait_ge(const_loaded, 16)
                pe.wait_ge(small_loaded, 16 * len(small_list))
                start_tensor(pe)
                pe.wait_ge(*scalar.at("cond"))
                for i in range(ADA_FIRST):
                    rows_tensor(pe, 0, i)
                    ada_tensor(pe, 0, i)
                join(tensor, pe, "start")
                for k in range(KD):
                    mean_tensor(pe, T2, ("n1", 0), k)
                for l in range(L):
                    hybrid_tensor(pe, l)
                    moe_tensor(pe, l)
                for k in range(KD):
                    mean_tensor(pe, S, ("m1", 0), k)
                join(tensor, pe, "block1")
                for l in range(L):
                    mixer_tensor(pe, l)
                    ffn_tensor(pe, l)
                    join(tensor, pe, ("ffn", l))
                for j in range(2):
                    for half in range(2):
                        pe.wait_ge(*got("normed", "final2", 4 * half + 3))
                        b = take(pe, "tokens", j, half)
                        for k in range(4):
                            last = PE.transpose(b[:, k * P:(k + 1) * P], h[:, 4 * half + k, j * P:(j + 1) * P], ident)
                        last.then_inc(*tensor.mark("tokens", j, half))

            @block.vector
            def _(dve):
                dve.wait_ge(const_loaded, 16)
                start_vector(dve)
                for i in range(ADA_FIRST):
                    ada_vector(dve, 0, i)
                join(vector, dve, "start")
                for l in range(L):
                    hybrid_vector(dve, l)
                    moe_vector(dve, l)
                unit_vector(dve, S, "final1", lambda k: vc("final_norm_g", k), x)
                join(vector, dve, "block1")
                for l in range(L):
                    mixer_vector(dve, l)
                    ffn_vector(dve, l)
                unit_vector(dve, S, "final2", lambda k: vc("final_g_2", k))
                for j in range(2):
                    out_vector(dve, otok[:, j, 0:512], bank("tokens", j, 0)[:, :], "tokens", j, 0)

            @block.scalar
            def _(act):
                loads_scalar(act)
                act.wait_ge(const_loaded, 16)
                start_scalar(act)
                for i in range(ADA_FIRST):
                    rows_scalar(act, 0, i)
                late_loads_scalar(act)
                join(scalar, act, "start")
                for k in range(KD):
                    squares_scalar(act, T2, ("n1", 0), k, vector.at("streams", 0, k))
                for l in range(L):
                    hybrid_scalar(act, l)
                    moe_scalar(act, l)
                root_scalar(act, S, "final1")
                for k in range(KD):
                    squares_scalar(act, S, ("m1", 0), k, vector.at("normed", "final1", k))
                join(scalar, act, "block1")
                for l in range(L):
                    mixer_scalar(act, l)
                    ffn_scalar(act, l)
                root_scalar(act, S, "final2")
                for j in range(2):
                    out_scalar(act, otok[:, j, 512:1024], bank("tokens", j, 1)[:, :], "tokens", j, 1)

            @block.sync
            def _(sp):
                def load(n):
                    sp.dma_start(slot(n), stream[n][0]).then_inc(loaded[n % RING], 16)

                def wait_used(n):
                    kind, v = book.old.get(("used", n)) or ("mods_rows", 1)
                    sp.wait_ge(tensor.sem(kind), v)

                for n in range(RING):
                    if n == 1:
                        sp.wait_ge(small_loaded, 16 * len(small_list))
                    load(n)
                n = RING
                ecs = {expert_chunk[l]: l for l in range(L)}
                while n < len(stream):
                    m = n - RING
                    if m in ecs:
                        l = ecs[m]
                        sources = [A[w][l] for w in ("exp_w_gate", "exp_w_up", "exp_w_down")]

                        def step(g, q, c):
                            e = NE * l + q
                            sp.wait_ge((gate_made, up_made, down_made)[c], e + 1 + (AHEAD if c else 0) + 4 * g)

                        with sp.Fori(0, NE // 4 - 1) as g:
                            for q in range(4):
                                for c in range(3):
                                    step(g, q, c)
                                    qq, cc = q + (c + RING) // 3, (c + RING) % 3
                                    src = sources[cc].rearrange("e (k p) n -> p e k n", p=P)[:, bass.ds(4 * g + qq, 1)]
                                    later = m + 3 * q + c + RING
                                    sp.dma_start(slot(later), src.rearrange("p e k n -> p (e k) n"))\
                                      .then_inc(loaded[later % RING], 16)
                        n += 36
                        for q in range(4):
                            for c in range(3):
                                step(NE // 4 - 1, q, c)
                                load(n)
                                n += 1
                        continue
                    wait_used(m)
                    load(n)
                    n += 1
                sp.wait_ge(*vector.at("tokens", 1, 0))
                sp.wait_ge(*scalar.at("tokens", 1, 1))
                sp.dma_start(out[0].rearrange("(j p) d -> p j d", p=P), otok).then_inc(stored, 16)
                sp.wait_ge(stored, 16)

            @block.gpsimd
            def _(pool):
                for l in range(L):
                    moe_pool(pool, l)
                for l in range(L):
                    rwkv_pool(pool, l)


_INS = ["x", "c", "ctx", "c_ctx", "ada_w", "ada_b", "norm1_g", "w_in", "mla_q_norm_g", "mla_w_uq", "mla_kv_norm_g",
        "mla_w_ukv", "swa_sink", "conv_w", "w_o", "norm2_g", "router_w", "exp_w_gate", "exp_w_up", "exp_w_down",
        "final_norm_g", "norm1_g_2", "w_in_2", "rwkv_mu_2", "rwkv_w0_2", "rwkv_w2_2", "rwkv_a0_2", "rwkv_a2_2",
        "rwkv_g2_2", "rwkv_k_k_2", "rwkv_k_a_2", "rwkv_r_k_2", "rwkv_gn_w_2", "rwkv_gn_b_2", "rwkv_v0_2",
        "rwkv_v1_2", "rwkv_v2_2", "hgrn_lb_logits_2", "hgrn_gn_g_2", "w_branch_2", "w_out_2", "norm2_g_2",
        "w_ffn_gate_2", "w_ffn_up_2", "w_ffn_down_2", "final_g_2"]


def kernel(**inputs):
    import concourse.bacc as _bacc
    from concourse.bass_utils import run_bass_kernel_spmd as _run

    arrays = {f"in_{name}": np.ascontiguousarray(inputs[name]) for name in _INS}
    arrays["consts"] = CONST
    book = Book()
    for _ in range(2):
        nc = _bacc.Bacc("TRN2", target_bir_lowering=False, num_devices=1)
        A = {n.removeprefix("in_"): nc.dram_tensor(n, a.shape, mybir.dt.from_np(a.dtype), kind="ExternalInput").ap()
             for n, a in arrays.items()}
        out = nc.dram_tensor("out", (1, S, D), F32, kind="ExternalOutput").ap()
        program(nc, A, out, book)
        book.turn()
    r = _run(nc, [arrays], core_ids=[0])
    return r.results[0]["out"]
```
